# Optimizing a Trainium2 kernel written in Bass

```python
import math
import jax, jax.numpy as jnp
from jax import lax
import numpy as np

D_MODEL = 1024
BATCH = 1
SEQ = 256
DEPTH = 2

HEAD_DIM = 64
N_HEADS_A = 4
N_HEADS_B = 4
N_HEADS_C = 4
N_HEADS_D = 4
WA = N_HEADS_A * HEAD_DIM
WB = N_HEADS_B * HEAD_DIM
WC = N_HEADS_C * HEAD_DIM
WD = N_HEADS_D * HEAD_DIM
MIX_WIDTH = WA + WB + WC + WD
DIFF_HALF = HEAD_DIM // 2
Q_BLOCK = 128
MOBA_BLOCK = 256
MOBA_TOPK = 3
DSA_Q_RANK = 128
DSA_KV_RANK = 128
IDX_HEADS = 4
IDX_DIM = 64
DSA_TOPK_MAX = 256
T5_BUCKETS = 32
T5_MAX_DIST = 128
N_BIAS_HEADS = N_HEADS_A + N_HEADS_B + N_HEADS_D
D_FF = 2816
CONV_WIDTH = 3
EPS = 1e-6
NEG = -1e30
SPLIT_SIZES = (WA, WA, WA,
               WB, WB, WB,
               WC, WC, WC, N_HEADS_C, WC,
               DSA_Q_RANK, DSA_KV_RANK, IDX_DIM, IDX_HEADS)
IN_COLS = sum(SPLIT_SIZES)

kernel_name = "hybrid_parallel_heads_diff_moba_fox_dsa_convffn"

def _rms_norm(x, gain=None):
    xf = x.astype(jnp.float32)
    y = xf * lax.rsqrt(jnp.mean(xf * xf, axis=-1, keepdims=True) + EPS)
    if gain is not None:
        y = y * gain.astype(jnp.float32)
    return y.astype(x.dtype)

def _t5_bucket(dist):
    max_exact = T5_BUCKETS // 2
    d = jnp.maximum(dist, 0)
    ratio = jnp.maximum(d, 1).astype(jnp.float32) / max_exact
    large = max_exact + (jnp.log(ratio) / math.log(T5_MAX_DIST / max_exact)
                         * (T5_BUCKETS - max_exact)).astype(jnp.int32)
    large = jnp.minimum(large, T5_BUCKETS - 1)
    return jnp.where(d < max_exact, d, large)

def _sweep(block_fn, n_blocks):
    out = lax.map(block_fn, jnp.arange(n_blocks))
    nb, b, qb, h, d = out.shape
    return out.transpose(1, 0, 2, 3, 4).reshape(b, nb * qb, h, d)

def _diff_attention(q, k, v, lam, subln_gain, lambda_init, tab):
    S = v.shape[1]
    scale = DIFF_HALF ** -0.5
    kpos = jnp.arange(S)

    def block(i):
        q0 = i * Q_BLOCK
        qb = lax.dynamic_slice_in_dim(q, q0, Q_BLOCK, axis=1)
        dist = (q0 + jnp.arange(Q_BLOCK))[:, None] - kpos[None, :]
        bias = tab[:, _t5_bucket(dist)]
        logits = jnp.einsum('bqhcd,bkhcd->bchqk', qb, k).astype(jnp.float32) * scale + bias
        logits = jnp.where(dist >= 0, logits, NEG)
        p = jax.nn.softmax(logits, axis=-1)
        attn = p[:, 0] - lam * p[:, 1]
        return jnp.einsum('bhqk,bkhd->bqhd', attn.astype(v.dtype), v)

    o = _sweep(block, S // Q_BLOCK)
    return _rms_norm(o, subln_gain) * (1.0 - lambda_init)

def _moba_attention(q, k, v, tab):
    B, S, H, dh = q.shape
    scale = dh ** -0.5
    nb = -(-S // MOBA_BLOCK)
    kk = min(MOBA_TOPK, nb)
    pad = nb * MOBA_BLOCK - S
    kpad = jnp.pad(k, ((0, 0), (0, pad), (0, 0), (0, 0)))
    vpad = jnp.pad(v, ((0, 0), (0, pad), (0, 0), (0, 0)))
    kbh = kpad.reshape(B, nb, MOBA_BLOCK, H, dh).transpose(0, 3, 1, 2, 4)
    vbh = vpad.reshape(B, nb, MOBA_BLOCK, H, dh).transpose(0, 3, 1, 2, 4)
    kmean = jnp.mean(kbh.astype(jnp.float32), axis=3).astype(k.dtype)
    bi = jnp.arange(B)[:, None, None, None]
    hi = jnp.arange(H)[None, None, :, None]
    hi5 = jnp.arange(H)[None, None, :, None, None]
    blk_ids = jnp.arange(nb)
    in_blk = jnp.arange(MOBA_BLOCK)

    def block(i):
        q0 = i * Q_BLOCK
        qb = lax.dynamic_slice_in_dim(q, q0, Q_BLOCK, axis=1)
        qpos = q0 + jnp.arange(Q_BLOCK)
        cur = q0 // MOBA_BLOCK
        gate = jnp.einsum('bqhd,bhnd->bqhn', qb, kmean).astype(jnp.float32)
        gate = jnp.where(blk_ids < cur, gate, NEG)
        _, sel = lax.top_k(gate, kk)
        sel_valid = sel < cur
        ksel = kbh[bi, hi, sel]
        vsel = vbh[bi, hi, sel]
        s_sel = jnp.einsum('bqhd,bqhnkd->bqhnk', qb, ksel).astype(jnp.float32) * scale
        kpos_sel = sel[..., None] * MOBA_BLOCK + in_blk
        dist_sel = qpos[None, :, None, None, None] - kpos_sel
        s_sel = s_sel + tab[hi5, _t5_bucket(dist_sel)]
        s_sel = jnp.where(sel_valid[..., None], s_sel, NEG)
        k_own = lax.dynamic_slice_in_dim(kpad, cur * MOBA_BLOCK, MOBA_BLOCK, axis=1)
        v_own = lax.dynamic_slice_in_dim(vpad, cur * MOBA_BLOCK, MOBA_BLOCK, axis=1)
        dist_own = qpos[:, None] - (cur * MOBA_BLOCK + in_blk)[None, :]
        s_own = jnp.einsum('bqhd,bkhd->bqhk', qb, k_own).astype(jnp.float32) * scale
        s_own = s_own + tab[:, _t5_bucket(dist_own)].transpose(1, 0, 2)[None]
        s_own = jnp.where(dist_own[None, :, None, :] >= 0, s_own, NEG)
        logits = jnp.concatenate([s_sel.reshape(B, Q_BLOCK, H, kk * MOBA_BLOCK), s_own], axis=-1)
        p = jax.nn.softmax(logits, axis=-1).astype(v.dtype)
        p_sel = p[..., :kk * MOBA_BLOCK].reshape(B, Q_BLOCK, H, kk, MOBA_BLOCK)
        p_own = p[..., kk * MOBA_BLOCK:]
        return (jnp.einsum('bqhnk,bqhnkd->bqhd', p_sel, vsel)
                + jnp.einsum('bqhk,bkhd->bqhd', p_own, v_own))

    return _sweep(block, S // Q_BLOCK)

def _forgetting_attention(q, k, v, f_logit):
    S = q.shape[1]
    scale = HEAD_DIM ** -0.5
    cf = jnp.cumsum(jax.nn.log_sigmoid(f_logit.astype(jnp.float32)), axis=1).transpose(0, 2, 1)
    kpos = jnp.arange(S)

    def block(i):
        q0 = i * Q_BLOCK
        qb = lax.dynamic_slice_in_dim(q, q0, Q_BLOCK, axis=1)
        cq = lax.dynamic_slice_in_dim(cf, q0, Q_BLOCK, axis=2)
        dist = (q0 + jnp.arange(Q_BLOCK))[:, None] - kpos[None, :]
        logits = (jnp.einsum('bqhd,bkhd->bhqk', qb, k).astype(jnp.float32) * scale
                  + cq[..., None] - cf[:, :, None, :])
        logits = jnp.where(dist >= 0, logits, NEG)
        p = jax.nn.softmax(logits, axis=-1)
        return jnp.einsum('bhqk,bkhd->bqhd', p.astype(v.dtype), v)

    return _sweep(block, S // Q_BLOCK)

def _dsa_attention(q, k, v, q_idx, k_idx, w_idx, tab):
    B, S, H, dh = q.shape
    scale = dh ** -0.5
    topk = min(DSA_TOPK_MAX, S // 4)
    kpos = jnp.arange(S)

    def block(i):
        q0 = i * Q_BLOCK
        qpos = q0 + jnp.arange(Q_BLOCK)
        qb = lax.dynamic_slice_in_dim(q, q0, Q_BLOCK, axis=1)
        qi = lax.dynamic_slice_in_dim(q_idx, q0, Q_BLOCK, axis=1)
        wi = lax.dynamic_slice_in_dim(w_idx, q0, Q_BLOCK, axis=1)
        score = jnp.einsum('bqhd,bkd->bqhk', qi, k_idx).astype(jnp.float32) * IDX_DIM ** -0.5
        score = jnp.einsum('bqhk,bqh->bqk', jax.nn.relu(score), wi.astype(jnp.float32))
        score = jnp.where((qpos[:, None] >= kpos[None, :])[None], score, NEG)
        _, sel = lax.top_k(score, topk)
        valid = sel <= qpos[None, :, None]
        ksel = jax.vmap(lambda kb, ib: kb[ib])(k, sel)
        vsel = jax.vmap(lambda vb, ib: vb[ib])(v, sel)
        s = jnp.einsum('bqhd,bqkhd->bqhk', qb, ksel).astype(jnp.float32) * scale
        dist = qpos[None, :, None] - sel
        s = s + tab[:, _t5_bucket(dist)].transpose(1, 2, 0, 3)
        s = jnp.where(valid[:, :, None, :], s, NEG)
        p = jax.nn.softmax(s, axis=-1).astype(v.dtype)
        return jnp.einsum('bqhk,bqkhd->bqhd', p, vsel)

    return _sweep(block, S // Q_BLOCK)

def _causal_depthwise_conv(u, w, b):
    C = u.shape[-1]
    out = lax.conv_general_dilated(u, w[:, None, :].astype(u.dtype), window_strides=(1,),
                                   padding=[(CONV_WIDTH - 1, 0)],
                                   dimension_numbers=('NWC', 'WIO', 'NWC'),
                                   feature_group_count=C)
    return out + b

def _conv_glu_ffn(h, w_up, conv_w, conv_b, w_down):
    u = _causal_depthwise_conv(h @ w_up, conv_w, conv_b)
    gate, val = jnp.split(u, 2, axis=-1)
    return (jax.nn.silu(gate) * val) @ w_down

def setup_inputs(seed: int = 0) -> dict:
    key = jax.random.key(seed)
    ks = jax.random.split(key, 20)
    f32 = jnp.float32

    def nrm(k, shape, scale):
        return jax.random.normal(k, shape, f32) * scale

    return {
        "x": nrm(ks[0], (BATCH, SEQ, D_MODEL), 1.0),
        "c": nrm(ks[1], (BATCH, D_MODEL), 1.0),
        "w_ada": nrm(ks[2], (DEPTH, D_MODEL, 6 * D_MODEL), D_MODEL ** -0.5),
        "b_ada": nrm(ks[3], (DEPTH, 6 * D_MODEL), 0.02),
        "norm1_gain": 1.0 + nrm(ks[4], (DEPTH, D_MODEL), 0.02),
        "w_in": nrm(ks[5], (DEPTH, D_MODEL, IN_COLS), D_MODEL ** -0.5),
        "f_bias": 2.0 + nrm(ks[6], (DEPTH, N_HEADS_C), 0.5),
        "diff_lambda": nrm(ks[7], (DEPTH, 4, DIFF_HALF), 0.1),
        "diff_subln_gain": 1.0 + nrm(ks[8], (DEPTH, HEAD_DIM), 0.02),
        "w_dq_up": nrm(ks[9], (DEPTH, DSA_Q_RANK, WD), DSA_Q_RANK ** -0.5),
        "w_didx_q": nrm(ks[10], (DEPTH, DSA_Q_RANK, IDX_HEADS * IDX_DIM), DSA_Q_RANK ** -0.5),
        "w_dkv_up": nrm(ks[11], (DEPTH, DSA_KV_RANK, 2 * WD), DSA_KV_RANK ** -0.5),
        "w_out": nrm(ks[12], (DEPTH, MIX_WIDTH, D_MODEL), MIX_WIDTH ** -0.5),
        "t5_table": nrm(ks[13], (T5_BUCKETS, N_BIAS_HEADS), 0.5),
        "norm2_gain": 1.0 + nrm(ks[14], (DEPTH, D_MODEL), 0.02),
        "w_ffn_up": nrm(ks[15], (DEPTH, D_MODEL, 2 * D_FF), D_MODEL ** -0.5),
        "ffn_conv_w": nrm(ks[16], (DEPTH, CONV_WIDTH, 2 * D_FF), CONV_WIDTH ** -0.5),
        "ffn_conv_b": nrm(ks[17], (DEPTH, 2 * D_FF), 0.02),
        "w_ffn_down": nrm(ks[18], (DEPTH, D_FF, D_MODEL), D_FF ** -0.5),
        "final_gain": 1.0 + nrm(ks[19], (D_MODEL,), 0.02),
    }

def reference(x, c, w_ada, b_ada, norm1_gain, w_in, f_bias, diff_lambda, diff_subln_gain,
              w_dq_up, w_didx_q, w_dkv_up, w_out, t5_table, norm2_gain, w_ffn_up,
              ffn_conv_w, ffn_conv_b, w_ffn_down, final_gain):
    B, S, _ = x.shape
    split_points = np.cumsum(SPLIT_SIZES)[:-1].tolist()
    tab_a = t5_table[:, :N_HEADS_A].T
    tab_b = t5_table[:, N_HEADS_A:N_HEADS_A + N_HEADS_B].T
    tab_d = t5_table[:, N_HEADS_A + N_HEADS_B:].T
    cond = jax.nn.silu(c)

    def heads(t, n):
        return t.reshape(B, S, n, HEAD_DIM)

    for l in range(DEPTH):
        mod = cond @ w_ada[l] + b_ada[l]
        sh1, sc1, g1, sh2, sc2, g2 = [m[:, None, :] for m in jnp.split(mod, 6, axis=-1)]

        h = _rms_norm(x, norm1_gain[l]) * (1.0 + sc1) + sh1
        proj = h @ w_in[l]
        (qa, ka, va, qb, kb, vb, qc, kc, vc, fc, gc,
         qlat, kvlat, kidx, widx) = jnp.split(proj, split_points, axis=-1)

        lambda_init = 0.8 - 0.6 * math.exp(-0.3 * l)
        lq1, lk1, lq2, lk2 = diff_lambda[l]
        lam = jnp.exp(jnp.sum(lq1 * lk1)) - jnp.exp(jnp.sum(lq2 * lk2)) + lambda_init
        o_a = _diff_attention(qa.reshape(B, S, N_HEADS_A, 2, DIFF_HALF),
                              ka.reshape(B, S, N_HEADS_A, 2, DIFF_HALF),
                              heads(va, N_HEADS_A), lam, diff_subln_gain[l], lambda_init, tab_a)

        o_b = _moba_attention(heads(qb, N_HEADS_B), heads(kb, N_HEADS_B), heads(vb, N_HEADS_B), tab_b)

        o_c = _forgetting_attention(heads(qc, N_HEADS_C), heads(kc, N_HEADS_C), heads(vc, N_HEADS_C),
                                    fc + f_bias[l])
        o_c = o_c.reshape(B, S, WC) * jax.nn.sigmoid(gc)

        q_lat = _rms_norm(qlat)
        kv_lat = _rms_norm(kvlat)
        q_d = heads(q_lat @ w_dq_up[l], N_HEADS_D)
        q_i = (q_lat @ w_didx_q[l]).reshape(B, S, IDX_HEADS, IDX_DIM)
        k_d, v_d = jnp.split(kv_lat @ w_dkv_up[l], 2, axis=-1)
        o_d = _dsa_attention(q_d, heads(k_d, N_HEADS_D), heads(v_d, N_HEADS_D), q_i, kidx,
                             widx * IDX_HEADS ** -0.5, tab_d)

        o = jnp.concatenate([o_a.reshape(B, S, WA), o_b.reshape(B, S, WB), o_c,
                             o_d.reshape(B, S, WD)], axis=-1)
        x = x + g1 * (o @ w_out[l])

        h = _rms_norm(x, norm2_gain[l]) * (1.0 + sc2) + sh2
        x = x + g2 * _conv_glu_ffn(h, w_ffn_up[l], ffn_conv_w[l], ffn_conv_b[l], w_ffn_down[l])

    return _rms_norm(x, final_gain)


_drawn_inputs = setup_inputs


def setup_inputs(seed=0):
    import zlib

    import numpy as np

    out = dict(_drawn_inputs(seed))
    spreads = {}
    factors = {'norm1_gain': 4.199,
     'diff_lambda': 3.941,
     'diff_subln_gain': 7.942,
     'norm2_gain': 2.919,
     'ffn_conv_b': 3.515,
     'final_gain': 2.887}
    for name, (base, spread) in spreads.items():
        noise = np.random.default_rng([zlib.crc32(name.encode()), seed]).standard_normal(out[name].shape)
        drawn = base * np.exp(spread * noise) if base else spread * noise
        out[name] = __import__('jax').numpy.asarray(drawn.astype(out[name].dtype))
    for name, factor in factors.items():
        out[name] = (out[name] * factor).astype(out[name].dtype)
    return out
```

```python
import math
from contextlib import ExitStack

import concourse.bass as bass
import numpy as np
from concourse import mybir

F32 = mybir.dt.float32
F32R = mybir.dt.float32r
ACT = mybir.ActivationFunctionType
ALU = mybir.AluOpType
AX = mybir.AxisListType

P = 128
EPS = 1e-6
BIG = 1e30
TAKEN = -3e38

D_MODEL, SEQ, DEPTH, D_FF = 1024, 256, 2, 2816
HEAD, HALF, HEADS = 64, 32, 4
GROUP = HEADS * HEAD
KT = D_MODEL // P
TT = SEQ // P
UC = 256
FT = D_FF // P
STEPS = FT // 2
BUCKETS, T5_MAX = 32, 128
TOPK = min(256, SEQ // 4)

C_FC = 9 * GROUP
IN_COLS = C_FC + HEADS + GROUP + 2 * P + HEAD + HEADS
TAIL = IN_COLS - C_FC
T_GC, T_LAT = HEADS, HEADS + GROUP
T_KIDX = T_LAT + 2 * P
T_WIDX = T_KIDX + HEAD

IN_UNITS = [("tail", 256, 256), ("tail", 512, TAIL - 512), ("tail", 0, 256)]
IN_UNITS += [(what, g, UC) for g in range(3) for what in "qkv"]
NI = len(IN_UNITS)
NO = D_MODEL // UC
PER_LAYER = NI + NO + 3 * STEPS
RAW = 3

MAPS = [(0, h, c) for h in range(4) for c in range(2)] + [(g, h, 0) for g in (1, 2, 3) for h in range(4)]
NM = len(MAPS)
SCALE = [HALF ** -0.5, HEAD ** -0.5, HEAD ** -0.5, HEAD ** -0.5]

V_BADA, V_N1, V_N2, V_CB = 0, 48, 56, 64
V_W0, V_W1 = 128, 128 + 2 * FT
V_W2, V_FIN, V_C = 256, 256 + 2 * FT, 256 + 2 * FT + KT
VROWS = [64 + 2 * FT, 4 * FT, 2 * FT + 2 * KT]


def bucket_rows():
    y = np.arange(384)
    dist = SEQ - 1 - y
    exact = BUCKETS // 2
    d = np.maximum(dist, 0)
    ratio = np.maximum(d, 1).astype(np.float32) / np.float32(exact)
    large = exact + (np.log(ratio) / np.float32(math.log(T5_MAX / exact)) * np.float32(BUCKETS - exact)).astype(np.int32)
    bucket = np.where(d < exact, d, np.minimum(large, BUCKETS - 1))
    rows = np.zeros((BUCKETS + 1, 384), np.float32)
    rows[bucket, y] = dist >= 0
    rows[BUCKETS] = dist < 0
    return rows


def direct_units():
    ada = [[("ada", l, u) for u in range(6 * D_MODEL // UC)] for l in range(DEPTH)]
    return ada[0][:8] + [("dsa", 0, 0)] + ada[0][8:] + ada[1] + [("dsa", 1, 0)]


def layer_schedule(l):
    s = []
    fill = [("ada", 0, u) for u in range(8, 24)] if l == 0 else []
    tail = [("ada", 1, u) for u in range(2)] if l == 0 else []

    def unit(i):
        s.append(("unit", i))
        s.append(("evac", i))
        s.append(("split", i + RAW))

    def maps(a, b):
        for m in range(a, b):
            if m < NM:
                s.append(("scores", m))
            if 0 <= m - 1 < NM:
                s.append(("softmax", m - 1))
            if 0 <= m - 2 < NM:
                s.append(("probs", m - 2))
            if 0 <= m - 3 < NM:
                s.append(("values", m - 3))
                if (m - 3) % 4 == 3:
                    s.append(("heads", (m - 3) // 4))
                if m - 3 == 7:
                    s.append(("subln", 0))
                if m - 3 == 8:
                    s.append(("subln_end", 0))

    unit(0)
    unit(1)
    s.append(("latents", 0))
    unit(2)
    s.append(("latents_up", 0))
    unit(3)
    s.append(("forget", 0))
    s.append(("index", 0))
    unit(4)
    s.append(("forget_up", 0))
    s.append(("choose", 0))
    unit(5)
    s.append(("choose", 1))
    s.extend(fill[:4])
    at = 0
    for i in range(6, NI):
        unit(i)
        if i == 6:
            s.append(("choose", 2))
        if i == 7:
            s.append(("choose", 3))
        if i >= 7:
            maps(at, at + 2)
            at += 2
        s.extend(fill[4 + 2 * (i - 6):6 + 2 * (i - 6)])
    s.extend(tail)
    maps(at, 13)
    s.append(("turn", 0))
    maps(13, 17)
    s.append(("turn", 1))
    maps(17, 21)
    s.append(("turn", 2))
    maps(21, NM + 3)
    s.append(("turn", 3))
    for i in range(NI, NI + NO):
        s.append(("unit", i))
        s.append(("resid", i - NI))
        if i + RAW < NI + NO + 2:
            s.append(("split", i + RAW))
    return s


def trunk(nc, x, c, w_ada, b_ada, norm1_gain, w_in, f_bias, diff_lambda, diff_subln_gain, w_dq_up,
          w_didx_q, w_dkv_up, w_out, t5_table, norm2_gain, w_ffn_up, ffn_conv_w, ffn_conv_b,
          w_ffn_down, final_gain, buckets, out):
    DIRECT = direct_units()
    DSLOTS = 3
    direct_at = {u: a for a, u in enumerate(DIRECT)}
    schedules = [layer_schedule(l) for l in range(DEPTH)]
    lam_init = [0.8 - 0.6 * math.exp(-0.3 * l) for l in range(DEPTH)]

    with ExitStack() as ctx:
        def sb(name, shape, dt=F32):
            return ctx.enter_context(nc.sbuf_tensor(name, shape, dt))

        def sem(name):
            return ctx.enter_context(nc.semaphore(name))

        bank = [ctx.enter_context(nc.psum_tensor(f"bank{i}", [P, 512], F32)) for i in range(8)]
        raw = [sb(f"raw{i}", [P, KT * UC]) for i in range(RAW)]
        w_hi = [sb(f"w_hi{i}", [P, KT * UC], F32R) for i in range(RAW)]
        w_lo = [sb(f"w_lo{i}", [P, KT * UC], F32R) for i in range(RAW)]
        direct = [sb(f"direct{i}", [P, KT * UC]) for i in range(DSLOTS)]
        xT = sb("xT", [P, KT, SEQ])
        act_hi = sb("act_hi", [P, KT, SEQ], F32R)
        act_lo = sb("act_lo", [P, KT, SEQ], F32R)
        mlp_hi = sb("mlp_hi", [P, 2, SEQ], F32R)
        mlp_lo = sb("mlp_lo", [P, 2, SEQ], F32R)
        qkT = sb("qkT", [P, 4, 2, 2, SEQ])
        qiT = sb("qiT", [P, 2, SEQ])
        kiT = sb("kiT", [P, SEQ])
        v_sb = sb("v_sb", [P, 4, TT, GROUP])
        tail = sb("tail", [P, TT, TAIL])
        bias = sb("bias", [P, 3 * HEADS, SEQ])
        own_bias = sb("own_bias", [P, HEADS, 3, P])
        work = sb("work", [P, KT * SEQ])
        heads_out = sb("heads_out", [P, 4, TT, GROUP])
        vec = sb("vec", [P, DEPTH, 384])
        mod = sb("mod", [P, DEPTH, 48])
        amp = sb("amp", [P, 2, KT])
        cond = sb("cond", [P, KT])
        ident = sb("ident", [P, P])
        reverse = sb("reverse", [P, P])
        mean_w = sb("mean_w", [P, P])
        upto = sb("upto", [P, SEQ])
        one = sb("one", [P, 1])
        rstd = sb("rstd", [P, SEQ])
        lam_in = sb("lam_in", [P, DEPTH, 4, HALF])
        lam_pr = sb("lam_pr", [P, DEPTH * 2, HALF])
        lam_ex = sb("lam_ex", [P, DEPTH * 2])
        nlam = sb("nlam", [P, DEPTH])
        gain64 = sb("gain64", [P, DEPTH, HEAD])
        fb = sb("fb", [P, DEPTH, HEADS])
        tab = sb("tab", [BUCKETS + 1, 3 * HEADS])
        buck = sb("buck", [BUCKETS + 1, 384])
        diag = sb("diag", [3 * HEADS, 384])
        lat_ss = sb("lat_ss", [P, 4])
        fz = sb("fz", [P, 4, TT * HEADS])
        ncq = sb("ncq", [P, TT * HEADS])
        low = sb("low", [P, 3, 2])
        rsum = sb("rsum", [P, 2, TT, 4])
        rinv = sb("rinv", [P, TT, 4])
        top8 = sb("top8", [P, 8])
        gate_c = sb("gate_c", [P, TT, GROUP])
        pair = sb("pair", [P, TT, 4, HEAD])
        half = sb("half", [P, 8])
        nrm = sb("nrm", [P, TT * HEADS])
        score = sb("score", [P, 3, P])
        toeplitz = nc.dram_tensor("toeplitz", (3 * HEADS, 384), F32, kind="Internal").ap()

        soft = [work[:, 384 * i:384 * i + 384].rearrange("p (b k) -> p b k", b=3) for i in range(3)]
        probT = [work[:, 1152 + 384 * i:1536 + 384 * i].rearrange("p (b q) -> p b q", b=3) for i in range(2)]
        relu = [work[:, 384 * i:384 * i + 384].rearrange("p (b k) -> p b k", b=3) for i in range(2)]
        latT = work[:, 0:512].rearrange("p (w t) -> p w t", w=2)
        ki_twice = work[:, 1664:1920].rearrange("p (t a d) -> p t a d", t=TT, a=2)
        latn = work[:, 1152:1664].rearrange("p (t w d) -> p t w d", t=TT, w=2)
        lf_wide = work[:, 1024:2048].rearrange("p (c q) -> p c q", c=TT * HEADS)
        conv = work[:, 0:1024].rearrange("p (w f t) -> p w f t", w=2, f=2)
        silu = work[:, 1024:1536].rearrange("p (f t) -> p f t", f=2)
        prod = work[:, 1536:2048].rearrange("p (f t) -> p f t", f=2)
        wide = work[:, :].rearrange("p (k t) -> p k t", k=KT)
        flipped = qkT[:, :, :, :, :].rearrange("p g w h t -> p (g w h t)")[:, 0:3 * HEADS * SEQ].rearrange(
            "p (h k) -> p h k", k=SEQ)
        FLIP_BANKS = [1, 2, 3, 4, 5, 6]
        x_tok = heads_out[:, :, :, :].rearrange("p g t n -> p (g t n)").rearrange("p (t n) -> p t n", t=TT)
        rows_in = v_sb[:, 0:3, :, :].rearrange("p g t n -> p (g t n)")[:, 0:DEPTH * 384].rearrange(
            "p (l r n) -> p l r n", l=DEPTH, r=3)

        raw_in = [sem(f"raw_in{i}") for i in range(RAW)]
        direct_in = [sem(f"direct_in{i}") for i in range(DSLOTS)]
        small_in = sem("small_in")
        x_in = sem("x_in")
        rows_sem = sem("rows_in")
        consts = sem("consts")
        diag_ready = sem("diag_ready")
        toep_out = sem("toep_out")
        bias_in = sem("bias_in")
        flip_ready = sem("flip_ready")
        flip_read = sem("flip_read")
        setup_pe = sem("setup_pe")
        cond_ready = sem("cond_ready")
        lam_sem = sem("lam_sem")
        tab_ready = sem("tab_ready")
        lam_exp = sem("lam_exp")
        vec_in = sem("vec_in")
        tap_ready = sem("tap_ready")
        out_part = sem("out_part")
        hi_done = sem("hi_done")
        lo_done = sem("lo_done")
        unit_used = sem("unit_used")
        direct_used = sem("direct_used")
        mod_ready = sem("mod_ready")
        x_new = sem("x_new")
        squares = sem("squares")
        ms_ready = sem("ms_ready")
        ms_inv = sem("ms_inv")
        rstd_ready = sem("rstd_ready")
        scaled = sem("scaled")
        act_hi_ready = sem("act_hi_ready")
        act_lo_ready = sem("act_lo_ready")
        in_read = sem("in_read")
        lat_root = sem("lat_root")
        lat_ready = sem("lat_ready")
        latT_ready = sem("latT_ready")
        latT_read = sem("latT_read")
        up_read = sem("up_read")
        s_ready = sem("s_ready")
        idx_relu = sem("idx_relu")
        score_masked = sem("score_masked")
        chosen = sem("chosen")
        fz_ready = sem("fz_ready")
        fe_ready = sem("fe_ready")
        lf_ready = sem("lf_ready")
        lfw_ready = sem("lfw_ready")
        cum_ready = sem("cum_ready")
        ncq_ready = sem("ncq_ready")
        ck_ready = sem("ck_ready")
        own_ready = sem("own_ready")
        low_ready = sem("low_ready")
        exp_ready = sem("exp_ready")
        t_ready = sem("t_ready")
        pt_act = sem("pt_act")
        pt_dve = sem("pt_dve")
        pv_ready = sem("pv_ready")
        o_read = sem("o_read")
        group_ready = sem("group_ready")
        idx_acc = sem("idx_acc")
        lat_inv = sem("lat_inv")
        ki_ready = sem("ki_ready")
        up_ready = sem("up_ready")
        gate_exp = sem("gate_exp")
        finT_ready = sem("finT_ready")
        down_ready = sem("down_ready")
        sub_done = sem("sub_done")
        sub_ss = sem("sub_ss")
        sub_root = sem("sub_root")
        turn_hi = sem("turn_hi")
        turn_lo = sem("turn_lo")
        conv_read = sem("conv_read")
        silu_ready = sem("silu_ready")
        prod_done = sem("prod_done")
        mlp_hi_ready = sem("mlp_hi_ready")
        mlp_lo_ready = sem("mlp_lo_ready")
        fin_ready = sem("fin_ready")
        stored = sem("stored")
        dve_own = sem("dve_own")

        def unit_no(l, i):
            return PER_LAYER * l + i

        def wait_raw(eng, n):
            eng.wait_ge(raw_in[n % RAW], 16 * (n // RAW + 1))

        def unit_width(i):
            return IN_UNITS[i][2] if i < NI else UC

        def unit_shape(i):
            return KT * unit_width(i)

        SC = HEADS + NM
        turn_order = []
        for st, i in [e[:2] for e in schedules[0]]:
            if st == "probs":
                turn_order.append(("probs", i))
            elif st == "turn":
                turn_order += [("turn", i, 0)]
        NT = len(turn_order)
        turn_no = {k: n for n, k in enumerate(turn_order)}
        act_frees, dve_frees, freed_by = 0, 0, []
        for n, k in enumerate(turn_order):
            if k[0] == "turn":
                freed_by.append(("lo", k[1]))
            elif n % 2 == 0:
                act_frees += 1
                freed_by.append(("act", act_frees))
            else:
                dve_frees += 1
                freed_by.append(("dve", dve_frees))

        def wait_turned(eng, l, n, slack=0):
            kind, k = freed_by[n]
            if kind == "act":
                eng.wait_ge(pt_act, act_frees * l + k)
            elif kind == "dve":
                eng.wait_ge(pt_dve, dve_frees * l + k)
            else:
                eng.wait_ge(turn_lo, 4 * l + k + 1)

        block = ctx.enter_context(nc.Block())

        @block.sync
        def _(sp):
            for l in range(DEPTH):
                def rows(t, first, src, n):
                    sp.dma_start(rows_in[first:first + n, l, t, :], src.rearrange("(r n) -> r n", n=P)).then_inc(
                        rows_sem, 16)
                rows(0, V_BADA, b_ada[l], 48)
                rows(0, V_N1, norm1_gain[l], KT)
                rows(0, V_N2, norm2_gain[l], KT)
                rows(0, V_CB, ffn_conv_b[l], 2 * FT)
                rows(1, 0, ffn_conv_w[l, 0], 2 * FT)
                rows(1, 2 * FT, ffn_conv_w[l, 1], 2 * FT)
                rows(2, 0, ffn_conv_w[l, 2], 2 * FT)
                rows(2, 2 * FT, final_gain, KT)
                rows(2, 2 * FT + KT, c[0], KT)
            sp.dma_start(x_tok, x[0].rearrange("(t p) n -> p t n", p=P)).then_inc(x_in, 16)

            def load_direct(a):
                kind, l, u = DIRECT[a]
                if a >= DSLOTS:
                    sp.wait_ge(direct_used, a - DSLOTS + 1)
                slot = direct[a % DSLOTS]
                if kind == "ada":
                    sp.dma_start(slot[:, :].rearrange("p (k n) -> p k n", k=KT),
                                 w_ada[l].rearrange("(k p) n -> p k n", p=P)[:, :, u * UC:(u + 1) * UC]).then_inc(
                        direct_in[a % DSLOTS], 16)
                else:
                    sp.dma_start(slot[:, 0:256], w_dq_up[l]).then_inc(direct_in[a % DSLOTS], 16)
                    sp.dma_start(slot[:, 256:512], w_didx_q[l]).then_inc(direct_in[a % DSLOTS], 16)
                    sp.dma_start(slot[:, 512:1024], w_dkv_up[l]).then_inc(direct_in[a % DSLOTS], 16)

            def load_unit(l, i):
                n = unit_no(l, i)
                if n >= RAW:
                    sp.wait_ge(lo_done, n - RAW + 1)
                dst, j = raw[n % RAW], i - NI - NO
                if i < NI:
                    kind, g, width = IN_UNITS[i]
                    c0 = C_FC + g if kind == "tail" else 3 * GROUP * g + GROUP * "qkv".index(kind)
                    src = w_in[l].rearrange("(k p) n -> p k n", p=P)[:, :, c0:c0 + width]
                    dst = dst[:, 0:KT * width].rearrange("p (k n) -> p k n", k=KT)
                else:
                    src = w_out[l].rearrange("(k p) n -> p k n", p=P)[:, :, (i - NI) * UC:(i - NI + 1) * UC]
                    dst = dst[:, :].rearrange("p (k n) -> p k n", k=KT)
                sp.dma_start(dst, src).then_inc(raw_in[n % RAW], 16)

            def load_mlp(l, o, what, j):
                n = unit_no(l, NI + NO + o)
                sp.wait_ge(lo_done, n - RAW + 1)
                dst = raw[n % RAW]
                if what == "down":
                    src = w_ffn_down[l, j * UC:(j + 1) * UC, :].rearrange("(f p) n -> p f n", p=P)
                    dst = dst[:, :].rearrange("p (f n) -> p f n", f=2)
                else:
                    c0 = j * UC + (D_FF if what == "value" else 0)
                    src = w_ffn_up[l].rearrange("(k p) n -> p k n", p=P)[:, :, c0:c0 + UC]
                    dst = dst[:, :].rearrange("p (k n) -> p k n", k=KT)
                sp.dma_start(dst, src).then_inc(raw_in[n % RAW], 16)

            for a in range(4):
                if a < DSLOTS:
                    load_direct(a)
            sp.dma_start(tab[0:BUCKETS, :], t5_table).then_inc(small_in, 16)
            sp.dma_start(buck[:, :], buckets).then_inc(small_in, 16)
            sp.dma_start(lam_in[:, :, :, :], diff_lambda.rearrange("l a d -> (l a d)").partition_broadcast(P)).then_inc(
                small_in, 16)
            sp.dma_start(gain64[:, :, :], diff_subln_gain.rearrange("l d -> (l d)").partition_broadcast(P)).then_inc(
                small_in, 16)
            sp.dma_start(fb[:, :, :], f_bias.rearrange("l d -> (l d)").partition_broadcast(P)).then_inc(small_in, 16)
            for a in range(DSLOTS, 8):
                load_direct(a)
            for i in range(RAW):
                load_unit(0, i)
            a = 8
            for l in range(DEPTH):
                uses = 0
                for e in schedules[l]:
                    if e[0] == "latents":
                        load_direct(direct_at[("dsa", l, 0)])
                    elif e[0] == "ada":
                        load_direct(direct_at[e])
                    elif e[0] == "split" and e[1] < NI + NO:
                        load_unit(l, e[1])
                load_mlp(l, 0, "gate", 0)
                load_mlp(l, 1, "value", 0)
                for j in range(STEPS - 1):
                    load_mlp(l, 3 * j + 2, "gate", j + 1)
                    if l + 1 < DEPTH:
                        load_direct(direct_at[("ada", l + 1, 2 + 2 * j)])
                        load_direct(direct_at[("ada", l + 1, 3 + 2 * j)])
                    load_mlp(l, 3 * j + 3, "value", j + 1)
                    load_mlp(l, 3 * j + 4, "down", j)
                load_mlp(l, 3 * STEPS - 1, "down", STEPS - 1)
                if l + 1 < DEPTH:
                    load_direct(direct_at[("ada", l + 1, 22)])
                    load_direct(direct_at[("ada", l + 1, 23)])
                    for i in range(RAW):
                        load_unit(l + 1, i)
            for t in range(TT):
                sp.wait_ge(out_part, 2 * t + 2)
                sp.dma_start(out[0, t * P:(t + 1) * P, :], x_tok[:, t, :]).then_inc(stored, 16)
            sp.wait_ge(stored, 16 * TT)

        @block.gpsimd
        def _(pool):
            nc.gpsimd.memset(ident[:, :], 0.0)
            nc.gpsimd.memset(reverse[:, :], 0.0)
            nc.gpsimd.memset(upto[:, :], 1.0)
            nc.gpsimd.memset(mean_w[:, :], 1.0 / D_MODEL)
            nc.gpsimd.memset(one[:, :], 1.0)
            nc.gpsimd.memset(half[:, :], 0.5).then_inc(consts, 1)
            pool.wait_ge(consts, 1)
            nc.gpsimd.affine_select(out=ident[:, :], in_=ident[:, :], compare_op=ALU.not_equal, fill=1.0, base=0,
                                    pattern=[[-1, P]], channel_multiplier=1)
            nc.gpsimd.affine_select(out=upto[:, :], in_=upto[:, :], compare_op=ALU.is_ge, fill=0.0, base=0,
                                    pattern=[[1, SEQ]], channel_multiplier=-1).then_inc(consts, 1)
            nc.gpsimd.affine_select(out=reverse[:, :], in_=reverse[:, :], compare_op=ALU.not_equal, fill=1.0,
                                    base=1 - P, pattern=[[1, P]], channel_multiplier=1).then_inc(consts, 1)
            for l in range(DEPTH):
                for e in schedules[l]:
                    if e[0] == "latents":
                        pool.wait_ge(lat_inv, l + 1)
                        nc.gpsimd.tensor_tensor(lat_ss[:, :], lat_ss[:, :], half[:, 0:4], ALU.pow).then_inc(lat_root, 1)
                    elif e[0] == "subln":
                        pool.wait_ge(sub_ss, l + 1)
                        nc.gpsimd.tensor_tensor(nrm[:, :], nrm[:, :], half[:, :], ALU.pow).then_inc(sub_root, 1)
                    elif e[0] == "forget":
                        pool.wait_ge(lf_ready, l + 1)
                        nc.gpsimd.tensor_copy(lf_wide, fz[:, 3, :].unsqueeze(2).to_broadcast([P, TT * HEADS, P])).then_inc(
                            lfw_ready, 1)
                    elif e[0] == "choose" and e[1] == 0:
                        pool.wait_ge(idx_acc, 2 * HEADS * (l + 1))
                        nc.gpsimd.affine_select(out=score[:, 0::2, :], in_=score[:, 0::2, :], compare_op=ALU.is_ge,
                                                fill=-BIG, base=0, pattern=[[0, 2], [-1, P]],
                                                channel_multiplier=1).then_inc(score_masked, 1)
                    elif e[0] == "forget_up":
                        for h in range(HEADS):
                            pool.wait_ge(ck_ready, HEADS * l + h + 1)
                            nc.gpsimd.affine_select(out=own_bias[:, h, 0::2, :], in_=own_bias[:, h, 0::2, :],
                                                    compare_op=ALU.is_ge, fill=BIG, base=0,
                                                    pattern=[[0, 2], [-1, P]], channel_multiplier=1).then_inc(
                                own_ready, 1)
                    elif e[0] == "softmax" and MAPS[e[1]][0] == 2:
                        h = MAPS[e[1]][1]
                        pool.wait_ge(chosen, l + 1)
                        if l == 0 and h == 0:
                            pool.wait_ge(flip_read, 6)
                        pool.wait_ge(low_ready, 2 * (NM * l + e[1]) + 2)
                        nc.gpsimd.tensor_tensor(own_bias[:, h, 0, :], score[:, 0, :], bias[:, 2 * HEADS + h, P:2 * P],
                                                ALU.add)
                        nc.gpsimd.tensor_tensor(own_bias[:, h, 1:3, :], score[:, 1:3, :],
                                                bias[:, 2 * HEADS + h, :].rearrange("p (b k) -> p b k", b=2),
                                                ALU.add).then_inc(own_ready, 1)

        @block.tensor
        def _(pe):
            def product3(dst, lhs, rhs, first, last, check=False):
                (lh, ll), (rh, rl) = lhs, rhs
                pe.matmul(dst, lh, rh, start=first, stop=False, skip_group_check=check)
                pe.matmul(dst, lh, rl, start=False, stop=False, skip_group_check=check)
                return pe.matmul(dst, ll, rh, start=False, stop=last, skip_group_check=check)

            def ada(l, u):
                a = direct_at[("ada", l, u)]
                pe.wait_ge(direct_in[a % DSLOTS], direct_value(a))
                w = direct[a % DSLOTS][:, :].rearrange("p (k n) -> p k n", k=KT)
                for ct in range(2):
                    col = 48 * l + 2 * u + ct
                    for k in range(KT):
                        last = pe.matmul(bank[7][:, col:col + 1], w[:, k, ct * P:(ct + 1) * P], cond[:, k:k + 1],
                                         start=(k == 0), stop=(k == KT - 1))
                last.then_inc(direct_used, 1)

            def direct_value(a):
                return 16 * sum(3 if DIRECT[b][0] == "dsa" else 1 for b in range(a % DSLOTS, a + 1, DSLOTS))

            def mean_square(n):
                for p in range(KT // 2):
                    pe.wait_ge(squares, 4 * n + p + 1)
                    for k in (2 * p, 2 * p + 1):
                        mm = pe.matmul(bank[7][:, SEQ:2 * SEQ], mean_w[:, :], wide[:, k, :],
                                       start=(k == 0), stop=(k == KT - 1))
                mm.then_inc(ms_ready, 1)
                pe.wait_ge(ms_inv, n + 1)

            def unit_product(l, i, bk, wait_act=None):
                n = unit_no(l, i)
                pe.wait_ge(lo_done, n + 1)
                width = unit_width(i) if i < NI else UC
                wh = w_hi[n % RAW][:, 0:KT * width].rearrange("p (k n) -> p k n", k=KT)
                wl = w_lo[n % RAW][:, 0:KT * width].rearrange("p (k n) -> p k n", k=KT)
                token_rows = i < NI and IN_UNITS[i][0] in ("tail", "v")
                for t in range(2):
                    for k in range(KT):
                        if wait_act is not None and t == 0:
                            pe.wait_ge(act_lo_ready, wait_act + k + 1)
                        s = slice(t * P, (t + 1) * P)
                        if token_rows:
                            mm = product3(bk[:, t * width:(t + 1) * width],
                                          (act_hi[:, k, s], act_lo[:, k, s]), (wh[:, k, :], wl[:, k, :]),
                                          k == 0, k == KT - 1)
                        else:
                            mm = product3(bk[:, t * SEQ:(t + 1) * SEQ], (wh[:, k, s], wl[:, k, s]),
                                          (act_hi[:, k, :], act_lo[:, k, :]), k == 0, k == KT - 1)
                return mm

            pe.wait_ge(consts, 2)
            pe.wait_ge(rows_sem, 16 * 9 * DEPTH)
            for l in range(DEPTH):
                for t in range(3):
                    mm = pe.transpose(bank[l][:, P * t:P * t + VROWS[t]], rows_in[0:VROWS[t], l, t, :],
                                      ident[0:VROWS[t], 0:VROWS[t]])
            mm.then_inc(setup_pe, 1)
            pe.wait_ge(x_in, 16)
            for k in range(KT):
                for t in range(TT):
                    mm = pe.transpose(bank[2 + k // 2][:, (k % 2) * SEQ + t * P:(k % 2) * SEQ + (t + 1) * P],
                                      x_tok[:, t, k * P:(k + 1) * P], ident[:, :])
                if k % 2:
                    mm.then_inc(setup_pe, 1)
            pe.wait_ge(small_in, 16 * 5)
            pe.wait_ge(tab_ready, 1)
            pe.matmul(bank[6][0:3 * HEADS, 0:384], tab[:, :], buck[:, :], start=True, stop=True).then_inc(setup_pe, 1)
            mean_square(0)
            pe.wait_ge(cond_ready, 1)
            for u in range(8):
                ada(0, u)
            pe.wait_ge(bias_in, 16)
            pe.wait_ge(consts, 3)
            for i, b in enumerate(FLIP_BANKS):
                pe.matmul(bank[b][:, :], reverse[:, :], flipped[:, 2 * i:2 * i + 2, :], start=True,
                          stop=True).then_inc(flip_ready, 1)

            def scores(l, m):
                s = SC * l + HEADS + m
                g, h, comp = MAPS[m]
                if m < 2:
                    pe.wait_ge(idx_relu, HEADS * l + HEADS - 1 + m)
                else:
                    pe.wait_ge(low_ready, 2 * (NM * l + m - 2) + 2)
                p0, width = ((h % 2) * HEAD + comp * HALF, HALF) if g == 0 else ((h % 2) * HEAD, HEAD)
                q = qkT[p0:p0 + width, g, 0, h // 2, :]
                k = qkT[p0:p0 + width, g, 1, h // 2, :]
                pe.matmul(bank[2 + s % 2][:, 0:P], q[:, 0:P], k[:, 0:P], start=True, stop=True)
                pe.matmul(bank[2 + s % 2][:, P:3 * P], q[:, P:2 * P], k, start=True, stop=True).then_inc(s_ready, 1)

            for l in range(DEPTH):
                norm = 2 * l
                if l > 0:
                    mean_square(norm)
                for e in schedules[l]:
                    st, i = e[0], e[1]
                    if st == "unit":
                        if l == 0 and i == 1:
                            pe.wait_ge(flip_read, 1)
                        if 2 <= i < NI + 2:
                            pe.wait_ge(in_read, NI * l + i - 1)
                        elif i >= NI + 2:
                            pe.wait_ge(x_new, 4 * (2 * l + 1) + i - NI - 1)
                        if i == NI:
                            pe.wait_ge(turn_lo, 4 * l + 4)
                        mm = unit_product(l, i, bank[i % 2], KT * norm if i == 0 else None)
                        mm.then_inc(unit_used, 1)
                    elif st == "ada":
                        ada(e[1], e[2])
                    elif st == "latents":
                        pe.wait_ge(ki_ready, l + 1)
                        for t in range(TT):
                            pe.transpose(bank[4][:, t * P:(t + 1) * P],
                                         ki_twice[:, t, :, :].rearrange("p a d -> p (a d)"), ident[:, :])
                        pe.wait_ge(lat_ready, l + 1)
                        for w in range(2):
                            for t in range(TT):
                                mm = pe.transpose(bank[6][:, w * SEQ + t * P:w * SEQ + (t + 1) * P], latn[:, t, w, :],
                                                  ident[:, :])
                        mm.then_inc(latT_ready, 1)
                    elif st == "latents_up":
                        pe.wait_ge(latT_read, 2 * l + 2)
                        a = direct_at[("dsa", l, 0)]
                        pe.wait_ge(direct_in[a % DSLOTS], direct_value(a))
                        w = direct[a % DSLOTS]
                        for b, c0, src in ((2, 0, 0), (3, 256, 0), (4, 512, 1)):
                            for t in range(2):
                                mm = pe.matmul(bank[b][:, t * SEQ:(t + 1) * SEQ], w[:, c0 + t * P:c0 + (t + 1) * P],
                                               latT[:, src, :], start=True, stop=True)
                            mm.then_inc(up_ready, 1)
                        for t in range(TT):
                            mm = pe.matmul(bank[5][:, t * GROUP:(t + 1) * GROUP], latT[:, 1, t * P:(t + 1) * P],
                                           w[:, 768:1024], start=True, stop=True)
                        mm.then_inc(direct_used, 1)
                    elif st == "index":
                        pe.wait_ge(up_read, 4 * l + 4)
                        for h in range(HEADS):
                            s = SC * l + h
                            if h >= 2:
                                pe.wait_ge(idx_relu, HEADS * l + h - 1)
                            r = slice((h % 2) * HEAD, (h % 2) * HEAD + HEAD)
                            b = bank[2 + s % 2]
                            pe.matmul(b[:, 0:P], qiT[r, h // 2, 0:P], kiT[r, 0:P], start=True, stop=True)
                            pe.matmul(b[:, P:3 * P], qiT[r, h // 2, P:2 * P], kiT[r, :], start=True,
                                      stop=True).then_inc(s_ready, 1)
                    elif st == "forget_up":
                        pe.wait_ge(lf_ready, l + 1)
                        lf = fz[:, 3, :].rearrange("p (t h) -> p t h", t=TT)
                        pe.matmul(bank[7][:, 128:132], upto[:, 0:P], lf[:, 0, :], start=True, stop=True)
                        pe.matmul(bank[7][:, 132:136], upto[:, P:2 * P], lf[:, 0, :], start=True, stop=False)
                        pe.matmul(bank[7][:, 132:136], upto[:, 0:P], lf[:, 1, :], start=False,
                                  stop=True).then_inc(cum_ready, 1)
                        pe.wait_ge(lfw_ready, l + 1)
                        for h in range(HEADS):
                            b = bank[4 + h // 2][:, (h % 2) * SEQ:(h % 2 + 1) * SEQ]
                            pe.matmul(b, lf_wide[:, h, :], upto[:, :], start=True, stop=False)
                            mm = pe.matmul(b[:, P:2 * P], lf_wide[:, HEADS + h, :], upto[:, 0:P], start=False, stop=True)
                        mm.then_inc(cum_ready, 1)
                        pe.wait_ge(ncq_ready, l + 1)
                    elif st == "scores":
                        scores(l, i)
                    elif st == "probs":
                        n = turn_no[("probs", i)]
                        if n >= 2:
                            wait_turned(pe, l, n - 2)
                        else:
                            pe.wait_ge(ck_ready, HEADS * (l + 1))
                        pe.wait_ge(exp_ready, 2 * (NM * l + i) + 2)
                        for b in range(3):
                            mm = pe.transpose(bank[4 + n % 2][:, b * P:(b + 1) * P], soft[i % 3][:, b, :], ident[:, :])
                        mm.then_inc(t_ready, 1)
                    elif st == "values":
                        g, h, comp = MAPS[i]
                        slot, quad = i % 4, i // 4
                        wait_turned(pe, l, turn_no[("probs", i)])
                        if slot == 0 and quad > 0:
                            pe.wait_ge(o_read, 5 * l + quad)
                        pt = probT[i % 2]
                        o = bank[6][:, :].rearrange("p (t s d) -> p t s d", t=TT, s=4)
                        v = v_sb[:, g, :, h * HEAD:(h + 1) * HEAD]
                        pe.matmul(o[:, 0, slot, :], pt[:, 0, :], v[:, 0, :], start=True, stop=True)
                        pe.matmul(o[:, 1, slot, :], pt[:, 1, :], v[:, 0, :], start=True, stop=False)
                        pe.matmul(o[:, 1, slot, :], pt[:, 2, :], v[:, 1, :], start=False, stop=True).then_inc(
                            pv_ready, 1)
                    elif st == "turn":
                        n = turn_no[("turn", i, 0)]
                        wait_turned(pe, l, n - 2)
                        pe.wait_ge(group_ready, 4 * l + i + 1)
                        for w in range(2):
                            for t in range(TT):
                                mm = pe.transpose(bank[4 + n % 2][:, w * SEQ + t * P:w * SEQ + (t + 1) * P],
                                                  heads_out[:, i, t, w * P:(w + 1) * P], ident[:, :])
                        mm.then_inc(t_ready, 1)
                mean_square(norm + 1)
                down = [bank[3 + ct // 2][:, (ct % 2) * SEQ:(ct % 2 + 1) * SEQ] for ct in range(KT)]

                def up(j, which):
                    o = 0 if j == 0 and which == 0 else 1 if j == 0 else 3 * j - 1 + which
                    if j > 0:
                        pe.wait_ge(conv_read, 2 * (STEPS * l + j - 1) + which + 1)
                    mm = unit_product(l, NI + NO + o, bank[which], KT * (norm + 1) if j == 0 and which == 0 else None)
                    mm.then_inc(unit_used, 1)

                def down_product(j):
                    o = 3 * j + 4 if j < STEPS - 1 else 3 * STEPS - 1
                    n = unit_no(l, NI + NO + o)
                    pe.wait_ge(lo_done, n + 1)
                    pe.wait_ge(mlp_lo_ready, STEPS * l + j + 1)
                    wh = w_hi[n % RAW][:, :].rearrange("p (f n) -> p f n", f=2)
                    wl = w_lo[n % RAW][:, :].rearrange("p (f n) -> p f n", f=2)
                    for ct in range(KT):
                        for f in range(2):
                            s = slice(ct * P, (ct + 1) * P)
                            mm = product3(down[ct], (wh[:, f, s], wl[:, f, s]), (mlp_hi[:, f, :], mlp_lo[:, f, :]),
                                          j == 0 and f == 0 and ct % 2 == 0, j == STEPS - 1 and f == 1, True)
                        if j == STEPS - 1 and ct in (1, 3, 5):
                            mm.then_inc(down_ready, 1)
                    mm.then_inc(unit_used, 1)

                for j in range(STEPS):
                    up(j, 0)
                    up(j, 1)
                    if j > 0:
                        if l + 1 < DEPTH:
                            ada(l + 1, 2 * j)
                            ada(l + 1, 2 * j + 1)
                        down_product(j - 1)
                if l + 1 < DEPTH:
                    ada(l + 1, 22)
                    ada(l + 1, 23)
                down_product(STEPS - 1)
            mean_square(2 * DEPTH)
            for t in range(TT):
                for q in range(2):
                    pe.wait_ge(fin_ready, 4 * (q + 1))
                    for k in range(4):
                        mm = pe.transpose(bank[2 * t + q][:, k * P:(k + 1) * P], wide[:, 4 * q + k, t * P:(t + 1) * P],
                                          ident[:, :])
                    mm.then_inc(finT_ready, 1)

        @block.scalar
        def _(act):
            def split_hi(n, width=UC):
                wait_raw(act, n)
                if n >= RAW:
                    act.wait_ge(unit_used, n - RAW + 1)
                nc.scalar.activation(w_hi[n % RAW][:, 0:KT * width], raw[n % RAW][:, 0:KT * width],
                                     ACT.Copy).then_inc(hi_done, 1)

            def squares_of(n):
                for p in range(KT // 2):
                    act.wait_ge(x_new, 4 * n + p + 1)
                    nc.scalar.activation(wide[:, 2 * p:2 * p + 2, :], xT[:, 2 * p:2 * p + 2, :], ACT.Square).then_inc(
                        squares, 1)

            def root(n):
                act.wait_ge(ms_inv, n + 1)
                nc.scalar.activation(rstd[:, :], rstd[:, :], ACT.Sqrt).then_inc(rstd_ready, 1)

            def modulated(n, l, shift):
                for k in range(KT):
                    act.wait_ge(scaled, KT * n + k + 1)
                    nc.scalar.activation(act_hi[:, k, :], wide[:, k, :], ACT.Identity,
                                         bias=mod[:, l, shift + k:shift + k + 1]).then_inc(act_hi_ready, 1)

            act.wait_ge(setup_pe, 1)
            for l in range(DEPTH):
                for t in range(3):
                    ins = nc.scalar.activation(vec[:, l, P * t:P * t + VROWS[t]], bank[l][:, P * t:P * t + VROWS[t]],
                                               ACT.Copy)
                    ins.then_inc(vec_in, 1)
            act.wait_ge(vec_in, 3 * DEPTH)
            nc.scalar.activation(cond[:, :], vec[:, 0, V_C:V_C + KT], ACT.Silu).then_inc(cond_ready, 1)
            act.wait_ge(lam_sem, 1)
            nc.scalar.activation(lam_ex[:, :], lam_ex[:, :], ACT.Exp).then_inc(lam_exp, 1)
            act.wait_ge(setup_pe, 6)
            nc.scalar.activation(diag[:, :], bank[6][0:3 * HEADS, 0:384], ACT.Copy, scale=-1.0).then_inc(diag_ready, 1)
            act.wait_ge(diag_ready, 1)
            act.dma_start(toeplitz, diag[:, :]).then_inc(toep_out, 16)
            act.wait_ge(toep_out, 16)
            act.dma_start(flipped, bass.AP(tensor=toeplitz.tensor, offset=0,
                                           ap=[[1, P], [384, 3 * HEADS], [1, SEQ]])).then_inc(bias_in, 16)
            squares_of(0)
            root(0)
            for i in range(RAW):
                split_hi(i, unit_width(i))

            for l in range(DEPTH):
                if l > 0:
                    squares_of(2 * l)
                    root(2 * l)
                    for i in range(RAW):
                        split_hi(unit_no(l, i), unit_width(i))
                modulated(2 * l, l, 0)
                if l == 0:
                    for i, b in enumerate(FLIP_BANKS):
                        act.wait_ge(flip_ready, i + 1)
                        nc.scalar.activation(bias[:, 2 * i:2 * i + 2, :],
                                             bank[b][:, :].rearrange("p (h k) -> p h k", h=2), ACT.Copy).then_inc(
                            flip_read, 1)
                for e in schedules[l]:
                    st, i = e[0], e[1]
                    if st == "split":
                        split_hi(unit_no(l, i), unit_width(i))
                    elif st == "evac":
                        kind, g, width = IN_UNITS[i]
                        act.wait_ge(unit_used, unit_no(l, i) + 1)
                        src = bank[i % 2][:, 0:2 * width].rearrange("p (t n) -> p t n", t=2)
                        if kind == "tail":
                            nc.scalar.activation(tail[:, :, g:g + width], src, ACT.Copy).then_inc(in_read, 1)
                        elif kind == "v":
                            nc.scalar.activation(v_sb[:, g, :, :], src, ACT.Copy).then_inc(in_read, 1)
                        else:
                            nc.scalar.activation(qkT[:, g, "qk".index(kind), :, :], src, ACT.Copy,
                                                 scale=-SCALE[g] if kind == "q" else 1.0).then_inc(in_read, 1)
                    elif st == "latents":
                        act.wait_ge(in_read, NI * l + 2)
                        nc.scalar.activation(ki_twice, tail[:, :, T_KIDX:T_KIDX + HEAD].unsqueeze(2).to_broadcast(
                            [P, TT, 2, HEAD]), ACT.Copy).then_inc(ki_ready, 1)
                        act.wait_ge(latT_ready, l + 1)
                        nc.scalar.activation(latT[:, :, :], bank[6][:, :].rearrange("p (w t) -> p w t", w=2),
                                             ACT.Copy).then_inc(latT_read, 1)
                        nc.scalar.activation(kiT[:, :], bank[4][:, 0:SEQ], ACT.Copy).then_inc(latT_read, 1)
                    elif st == "latents_up":
                        two = lambda b: bank[b][:, :].rearrange("p (t n) -> p t n", t=2)
                        act.wait_ge(up_ready, 3 * l + 1)
                        nc.scalar.activation(qkT[:, 3, 0, :, :], two(2), ACT.Copy, scale=-SCALE[3]).then_inc(up_read, 1)
                        act.wait_ge(up_ready, 3 * l + 2)
                        nc.scalar.activation(qiT[:, :, :], two(3), ACT.Copy,
                                             scale=HEAD ** -0.5 * HEADS ** -0.5).then_inc(up_read, 1)
                        act.wait_ge(up_ready, 3 * l + 3)
                        nc.scalar.activation(qkT[:, 3, 1, :, :], two(4), ACT.Copy).then_inc(up_read, 1)
                        act.wait_ge(direct_used, direct_at[("dsa", l, 0)] + 1)
                        nc.scalar.activation(v_sb[:, 3, :, :], two(5), ACT.Copy).then_inc(up_read, 1)
                    elif st == "forget":
                        act.wait_ge(fz_ready, 2 * l + 2)
                        nc.scalar.activation(fz[:, 1, :], fz[:, 1, :], ACT.Exp, scale=-1.0).then_inc(fe_ready, 1)
                        nc.scalar.activation(gate_c[:, :, :], tail[:, :, T_GC:T_GC + GROUP], ACT.Exp,
                                             scale=-1.0).then_inc(gate_exp, 1)
                        act.wait_ge(fe_ready, 2 * l + 1)
                        nc.scalar.activation(fz[:, 1, :], fz[:, 1, :], ACT.Ln, bias=one[:, :]).then_inc(fe_ready, 1)
                    elif st == "index":
                        for h in range(HEADS):
                            act.wait_ge(s_ready, SC * l + h + 1)
                            if h >= 2:
                                act.wait_ge(idx_acc, 2 * (HEADS * l + h - 1))
                            nc.scalar.activation(relu[h % 2], bank[2 + h % 2][:, 0:384].rearrange("p (b k) -> p b k", b=3),
                                                 ACT.Relu).then_inc(idx_relu, 1)
                    elif st == "forget_up":
                        act.wait_ge(cum_ready, 2 * l + 1)
                        nc.scalar.activation(ncq[:, :], bank[7][:, 128:128 + TT * HEADS], ACT.Copy,
                                             scale=-1.0).then_inc(ncq_ready, 1)
                        act.wait_ge(ncq_ready, l + 1)
                        act.wait_ge(cum_ready, 2 * l + 2)
                        for h in range(HEADS):
                            ck = bank[4 + h // 2][:, (h % 2) * SEQ:(h % 2 + 1) * SEQ]
                            nc.scalar.activation(own_bias[:, h, 0, :], ck[:, 0:P], ACT.Identity, bias=ncq[:, h:h + 1])
                            nc.scalar.activation(own_bias[:, h, 1:3, :], ck.rearrange("p (b k) -> p b k", b=2),
                                                 ACT.Identity, bias=ncq[:, HEADS + h:HEADS + h + 1]).then_inc(ck_ready, 1)
                    elif st == "softmax":
                        m = NM * l + i
                        dst = soft[i % 3]
                        for t, part in ((0, dst[:, 0, :]), (1, dst[:, 1:3, :])):
                            act.wait_ge(low_ready, 2 * m + t + 1)
                            nc.scalar.activation(part, part, ACT.Exp, bias=low[:, i % 3, t:t + 1], scale=-1.0,
                                                 accum_out=rsum[:, (i // 4) % 2, t, i % 4:i % 4 + 1]).then_inc(
                                exp_ready, 1)
                    elif st == "probs":
                        n = turn_no[("probs", i)]
                        if n % 2 == 0:
                            act.wait_ge(t_ready, NT * l + n + 1)
                            if i >= 2:
                                act.wait_ge(pv_ready, NM * l + i - 1)
                            nc.scalar.activation(probT[i % 2], bank[4][:, 0:384].rearrange("p (b q) -> p b q", b=3),
                                                 ACT.Copy).then_inc(pt_act, 1)
                    elif st == "turn":
                        n = turn_no[("turn", i, 0)]
                        act.wait_ge(t_ready, NT * l + n + 1)
                        act.wait_ge(unit_used, unit_no(l, NI))
                        nc.scalar.activation(act_hi[:, 2 * i:2 * i + 2, :],
                                             bank[4 + n % 2][:, :].rearrange("p (w t) -> p w t", w=2),
                                             ACT.Copy).then_inc(turn_hi, 1)
                    elif st == "resid":
                        act.wait_ge(x_new, 4 * (2 * l + 1) + i + 1)
                        p = i
                        nc.scalar.activation(wide[:, 2 * p:2 * p + 2, :], xT[:, 2 * p:2 * p + 2, :],
                                             ACT.Square).then_inc(squares, 1)
                first = unit_no(l, NI + NO)
                root(2 * l + 1)
                modulated(2 * l + 1, l, 3 * KT)

                def last_tap(j, which):
                    o = which if j == 0 else 3 * j - 1 + which
                    act.wait_ge(unit_used, first + o + 1)
                    if j > 0:
                        act.wait_ge(prod_done, STEPS * l + j)
                    for f in range(2):
                        ch = which * FT + 2 * j + f
                        nc.scalar.activation(conv[:, which, f, :], bank[which][:, f * SEQ:(f + 1) * SEQ], ACT.Identity,
                                             scale=vec[:, l, V_W2 + ch:V_W2 + ch + 1],
                                             bias=vec[:, l, V_CB + ch:V_CB + ch + 1]).then_inc(tap_ready, 1)

                for j in range(STEPS):
                    if j < STEPS - 1:
                        split_hi(first + 3 * j + 2)
                    last_tap(j, 0)
                    if j < STEPS - 1:
                        split_hi(first + 3 * j + 3)
                    last_tap(j, 1)
                    act.wait_ge(conv_read, 2 * (STEPS * l + j) + 1)
                    nc.scalar.activation(silu, conv[:, 0, :, :], ACT.Silu).then_inc(silu_ready, 1)
                    split_hi(first + (3 * j + 4 if j < STEPS - 1 else 3 * STEPS - 1))
                    act.wait_ge(prod_done, STEPS * l + j + 1)
                    if j > 0:
                        act.wait_ge(unit_used, first + 3 * j + 2)
                    nc.scalar.activation(mlp_hi[:, :, :], prod, ACT.Copy).then_inc(mlp_hi_ready, 1)
            squares_of(2 * DEPTH)
            root(2 * DEPTH)
            for t in range(TT):
                for q in range(2):
                    act.wait_ge(finT_ready, 2 * t + q + 1)
                    nc.scalar.activation(x_tok[:, t, 512 * q:512 * q + 512], bank[2 * t + q][:, :],
                                         ACT.Copy).then_inc(out_part, 1)

        @block.vector
        def _(dve):
            count = [0]

            def own(ins):
                count[0] += 1
                ins.then_inc(dve_own, 1)
                dve.wait_ge(dve_own, count[0])

            def split_lo(n, width=UC):
                dve.wait_ge(hi_done, n + 1)
                s = slice(0, KT * width)
                nc.vector.tensor_tensor(w_lo[n % RAW][:, s], raw[n % RAW][:, s], w_hi[n % RAW][:, s].bitcast(F32),
                                        ALU.subtract).then_inc(lo_done, 1)

            def inverse(n):
                dve.wait_ge(ms_ready, n + 1)
                own(nc.vector.tensor_scalar(rstd[:, :], bank[7][:, SEQ:2 * SEQ], EPS, None, ALU.add))
                nc.vector.reciprocal(rstd[:, :], rstd[:, :]).then_inc(ms_inv, 1)

            def modulated(n, l, which):
                dve.wait_ge(rstd_ready, n + 1)
                shift = 3 * KT * which

                def low_half(k):
                    dve.wait_ge(act_hi_ready, KT * n + k + 1)
                    nc.vector.scalar_tensor_tensor(act_lo[:, k, :], wide[:, k, :], mod[:, l, shift + k:shift + k + 1],
                                                   act_hi[:, k, :].bitcast(F32), ALU.add, ALU.subtract).then_inc(
                        act_lo_ready, 1)
                for k in range(KT):
                    nc.vector.scalar_tensor_tensor(wide[:, k, :], xT[:, k, :], amp[:, which, k:k + 1], rstd[:, :],
                                                   ALU.mult, ALU.mult).then_inc(scaled, 1)
                    if k >= 2:
                        low_half(k - 2)
                low_half(KT - 2)
                low_half(KT - 1)

            def residual(l, gate, p, src):
                for k in range(2):
                    kt = 2 * p + k
                    ins = nc.vector.scalar_tensor_tensor(xT[:, kt, :], src[:, k * SEQ:(k + 1) * SEQ],
                                                         mod[:, l, gate * KT + kt:gate * KT + kt + 1], xT[:, kt, :],
                                                         ALU.mult, ALU.add)
                ins.then_inc(x_new, 1)

            def take_mod(l, c0, c1, units):
                dve.wait_ge(direct_used, units)
                own(nc.vector.tensor_tensor(mod[:, l, c0:c1], bank[7][:, 48 * l + c0:48 * l + c1],
                                            vec[:, l, V_BADA + c0:V_BADA + c1], ALU.add))

            def amplitudes(l, which):
                v = V_N2 if which else V_N1
                own(nc.vector.scalar_tensor_tensor(amp[:, which, :], mod[:, l, KT * (3 * which + 1):KT * (3 * which + 2)],
                                                   1.0, vec[:, l, v:v + KT], ALU.add, ALU.mult))

            nc.vector.memset(tab[BUCKETS:BUCKETS + 1, :], -BIG).then_inc(tab_ready, 1)
            for p in range(KT // 2):
                dve.wait_ge(setup_pe, 2 + p)
                nc.vector.tensor_copy(xT[:, 2 * p:2 * p + 2, :],
                                      bank[2 + p][:, :].rearrange("p (k t) -> p k t", k=2)).then_inc(x_new, 1)
            dve.wait_ge(small_in, 16 * 5)
            own(nc.vector.tensor_tensor(lam_pr[:, :, :], lam_in[:, :, 0::2, :].rearrange("p l a d -> p (l a) d"),
                                        lam_in[:, :, 1::2, :].rearrange("p l a d -> p (l a) d"), ALU.mult))
            nc.vector.tensor_reduce(lam_ex[:, :], lam_pr[:, :, :], AX.X, ALU.add).then_inc(lam_sem, 1)
            for l in range(DEPTH):
                nc.vector.tensor_scalar(gain64[:, l, :], gain64[:, l, :], 1.0 - lam_init[l], None, ALU.mult)
            dve.wait_ge(lam_exp, 1)
            for l in range(DEPTH):
                own(nc.vector.tensor_tensor(nlam[:, l:l + 1], lam_ex[:, 2 * l + 1:2 * l + 2], lam_ex[:, 2 * l:2 * l + 1],
                                            ALU.subtract))
                own(nc.vector.tensor_scalar(nlam[:, l:l + 1], nlam[:, l:l + 1], -lam_init[l], None, ALU.add))
            inverse(0)
            dve.wait_ge(vec_in, 3 * DEPTH)
            take_mod(0, 0, 2 * KT, 8)
            amplitudes(0, 0)

            for l in range(DEPTH):
                if l > 0:
                    inverse(2 * l)
                    amplitudes(l, 0)
                modulated(2 * l, l, 0)
                for i in range(RAW):
                    split_lo(unit_no(l, i), unit_width(i))
                for e in schedules[l]:
                    st, i = e[0], e[1]
                    if st == "split":
                        split_lo(unit_no(l, i), unit_width(i))
                    elif st == "latents":
                        dve.wait_ge(in_read, NI * l + 2)
                        for t in range(TT):
                            for w in range(2):
                                src = tail[:, t, T_LAT + w * P:T_LAT + (w + 1) * P]
                                last = nc.vector.tensor_tensor_reduce(latn[:, t, w, :], src, src, 1.0, 0.0, ALU.mult,
                                                                      ALU.add, lat_ss[:, 2 * t + w:2 * t + w + 1])
                                if (t, w) != (1, 1):
                                    last.then_inc(dve_own, 1)
                                    count[0] += 1
                        own(last)
                        own(nc.vector.tensor_scalar(lat_ss[:, :], lat_ss[:, :], 1.0 / P, EPS, ALU.mult, ALU.add))
                        nc.vector.reciprocal(lat_ss[:, :], lat_ss[:, :]).then_inc(lat_inv, 1)
                        dve.wait_ge(lat_root, l + 1)
                        for t in range(TT):
                            for w in range(2):
                                last = nc.vector.tensor_scalar(latn[:, t, w, :], tail[:, t, T_LAT + w * P:T_LAT + (w + 1) * P],
                                                               lat_ss[:, 2 * t + w:2 * t + w + 1], None, ALU.mult)
                        last.then_inc(lat_ready, 1)
                    elif st == "forget":
                        dve.wait_ge(in_read, NI * l + 3)
                        own(nc.vector.tensor_tensor(fz[:, 0, :].rearrange("p (t h) -> p t h", t=TT), tail[:, :, 0:HEADS],
                                                    fb[:, l, :].unsqueeze(1).to_broadcast([P, TT, HEADS]), ALU.add))
                        nc.vector.scalar_tensor_tensor(fz[:, 1, :], fz[:, 0, :], -1.0, fz[:, 0, :], ALU.mult, ALU.max).then_inc(fz_ready, 1)
                        nc.vector.tensor_scalar(fz[:, 2, :], fz[:, 0, :], 0.0, None, ALU.min).then_inc(fz_ready, 1)
                        dve.wait_ge(fe_ready, 2 * l + 2)
                        nc.vector.tensor_tensor(fz[:, 3, :], fz[:, 2, :], fz[:, 1, :], ALU.subtract).then_inc(lf_ready, 1)
                        dve.wait_ge(gate_exp, l + 1)
                        own(nc.vector.tensor_scalar(gate_c[:, :, :], gate_c[:, :, :], 1.0, None, ALU.add))
                        own(nc.vector.reciprocal(gate_c[:, :, :], gate_c[:, :, :]))
                    elif st == "index":
                        for h in range(HEADS):
                            dve.wait_ge(idx_relu, HEADS * l + h + 1)
                            if h:
                                dve.wait_ge(idx_acc, 2 * (HEADS * l + h))
                            for t, b in ((0, slice(0, 1)), (1, slice(1, 3))):
                                w = tail[:, t, T_WIDX + h:T_WIDX + h + 1]
                                if h == 0:
                                    nc.vector.tensor_scalar(score[:, b, :], relu[0][:, b, :], w, None,
                                                            ALU.mult).then_inc(idx_acc, 1)
                                else:
                                    nc.vector.scalar_tensor_tensor(score[:, b, :], relu[h % 2][:, b, :], w,
                                                                   score[:, b, :], ALU.mult, ALU.add).then_inc(idx_acc, 1)
                    elif st == "choose":
                        if i == 0:
                            dve.wait_ge(score_masked, l + 1)
                        for _ in range(TOPK // 8 // 4):
                            for b in (slice(0, 1), slice(1, 3)):
                                part = score[:, b, :].rearrange("p b k -> p (b k)")
                                own(nc.vector.max(top8[:, :], part))
                                own(nc.vector.match_replace(part, top8[:, :], part, TAKEN))
                        if i == 3:
                            nc.vector.tensor_scalar(score[:, :, :], score[:, :, :], TAKEN / 2, BIG, ALU.is_gt,
                                                    ALU.mult).then_inc(chosen, 1)
                    elif st == "softmax":
                        g, h, comp = MAPS[i]
                        dve.wait_ge(s_ready, SC * l + HEADS + i + 1)
                        if g < 2:
                            if l == 0 and i == 0:
                                dve.wait_ge(flip_read, 6)
                            b = bias[:, 4 * g + h, :]
                            biases = b[:, P:2 * P], b.rearrange("p (b k) -> p b k", b=2)
                        else:
                            dve.wait_ge(own_ready, 8 * l + 4 * (g - 2) + h + 1)
                            biases = own_bias[:, h, 0, :], own_bias[:, h, 1:3, :]
                        if i >= 3:
                            dve.wait_ge(t_ready, NT * l + turn_no[("probs", i - 3)] + 1)
                        s = bank[2 + i % 2][:, 0:384].rearrange("p (b k) -> p b k", b=3)
                        nc.vector.tensor_tensor_reduce(soft[i % 3][:, 0, :], s[:, 0, :], biases[0], 1.0, 3e38, ALU.add,
                                                       ALU.min, low[:, i % 3, 0:1]).then_inc(low_ready, 1)
                        nc.vector.tensor_tensor_reduce(soft[i % 3][:, 1:3, :], s[:, 1:3, :], biases[1], 1.0, 3e38,
                                                       ALU.add, ALU.min, low[:, i % 3, 1:2]).then_inc(low_ready, 1)
                    elif st == "probs":
                        n = turn_no[("probs", i)]
                        if n % 2:
                            dve.wait_ge(t_ready, NT * l + n + 1)
                            if i >= 2:
                                dve.wait_ge(pv_ready, NM * l + i - 1)
                            nc.vector.tensor_copy(probT[i % 2], bank[5][:, 0:384].rearrange("p (b q) -> p b q", b=3)).then_inc(
                                pt_dve, 1)
                    elif st == "heads":
                        own(nc.vector.reciprocal(rinv[:, :, :], rsum[:, i % 2, :, :]))
                        dve.wait_ge(pv_ready, NM * l + 4 * i + 4)
                        o = bank[6][:, :].rearrange("p (t s d) -> p t s d", t=TT, s=4)
                        r = rinv[:, :, :].unsqueeze(3).to_broadcast([P, TT, 4, HEAD])
                        g = max(i - 1, 0)
                        dst = pair[:, :, :, :] if i < 2 else heads_out[:, g, :, :].rearrange("p t (s d) -> p t s d", s=4)
                        ins = nc.vector.tensor_tensor(dst, o, r, ALU.mult)
                        ins.then_inc(o_read, 1)
                        if i < 2:
                            dve.wait_ge(o_read, 5 * l + i + 1)
                            for t in range(TT):
                                last = nc.vector.scalar_tensor_tensor(
                                    heads_out[:, 0, t, i * P:(i + 1) * P].rearrange("p (h d) -> p h d", h=2),
                                    pair[:, t, 1::2, :], nlam[:, l:l + 1], pair[:, t, 0::2, :], ALU.mult, ALU.add)
                                own(last)
                        elif g == 2:
                            dve.wait_ge(o_read, 5 * l + i + 1)
                            nc.vector.tensor_tensor(heads_out[:, 2, :, :], heads_out[:, 2, :, :], gate_c[:, :, :],
                                                    ALU.mult).then_inc(group_ready, 1)
                        else:
                            dve.wait_ge(o_read, 5 * l + i + 1)
                            nc.vector.tensor_copy(rinv[:, 0, 0:1], rinv[:, 0, 0:1]).then_inc(group_ready, 1)
                    elif st == "subln":
                        a_heads = heads_out[:, 0, :, :].rearrange("p t (h d) -> p (t h) d", h=HEADS)
                        sq = pair[:, :, :, :].rearrange("p t s d -> p (t s) d")
                        own(nc.vector.tensor_tensor(sq, a_heads, a_heads, ALU.mult))
                        own(nc.vector.tensor_reduce(nrm[:, :], sq, AX.X, ALU.add))
                        own(nc.vector.tensor_scalar(nrm[:, :], nrm[:, :], 1.0 / HEAD, EPS, ALU.mult, ALU.add))
                        nc.vector.reciprocal(nrm[:, :], nrm[:, :]).then_inc(sub_ss, 1)
                    elif st == "subln_end":
                        dve.wait_ge(sub_root, l + 1)
                        a_heads = heads_out[:, 0, :, :].rearrange("p t (h d) -> p (t h) d", h=HEADS)
                        own(nc.vector.tensor_tensor(a_heads, a_heads, nrm[:, :].unsqueeze(2).to_broadcast(
                            [P, TT * HEADS, HEAD]), ALU.mult))
                        nc.vector.tensor_tensor(a_heads, a_heads, gain64[:, l, :].unsqueeze(1).to_broadcast(
                            [P, TT * HEADS, HEAD]), ALU.mult).then_inc(group_ready, 1)
                    elif st == "turn":
                        n = turn_no[("turn", i, 0)]
                        dve.wait_ge(turn_hi, 4 * l + i + 1)
                        nc.vector.tensor_tensor(act_lo[:, 2 * i:2 * i + 2, :],
                                                bank[4 + n % 2][:, :].rearrange("p (w t) -> p w t", w=2),
                                                act_hi[:, 2 * i:2 * i + 2, :].bitcast(F32),
                                                ALU.subtract).then_inc(turn_lo, 1)
                    elif st == "resid":
                        if l == 0 and i == 0:
                            take_mod(0, 2 * KT, 6 * KT, direct_at[("ada", 0, 23)] + 1)
                        if i == 0:
                            amplitudes(l, 1)
                        dve.wait_ge(unit_used, unit_no(l, NI + i) + 1)
                        residual(l, 2, i, bank[(NI + i) % 2])
                first = unit_no(l, NI + NO)
                inverse(2 * l + 1)
                modulated(2 * l + 1, l, 1)

                def taps(j, which):
                    dve.wait_ge(tap_ready, 4 * (STEPS * l + j) + 2 * which + 2)
                    for tap, lag in ((V_W1, 1), (V_W0, 2)):
                        for f in range(2):
                            ch = which * FT + 2 * j + f
                            dst = conv[:, which, f, lag:SEQ]
                            ins = nc.vector.scalar_tensor_tensor(
                                dst, bank[which][:, f * SEQ:(f + 1) * SEQ - lag], vec[:, l, tap + ch:tap + ch + 1], dst,
                                ALU.mult, ALU.add)
                            if lag == 1:
                                ins.then_inc(dve_own, 1)
                                count[0] += 1
                        if lag == 1:
                            dve.wait_ge(dve_own, count[0])
                    ins.then_inc(conv_read, 1)

                for j in range(STEPS):
                    if j < STEPS - 1:
                        split_lo(first + 3 * j + 2)
                    taps(j, 0)
                    if j < STEPS - 1:
                        split_lo(first + 3 * j + 3)
                    taps(j, 1)
                    dve.wait_ge(silu_ready, STEPS * l + j + 1)
                    dve.wait_ge(conv_read, 2 * (STEPS * l + j) + 2)
                    nc.vector.tensor_tensor(prod, silu, conv[:, 1, :, :], ALU.mult).then_inc(prod_done, 1)
                    split_lo(first + (3 * j + 4 if j < STEPS - 1 else 3 * STEPS - 1))
                    dve.wait_ge(mlp_hi_ready, STEPS * l + j + 1)
                    nc.vector.tensor_tensor(mlp_lo[:, :, :], prod, mlp_hi[:, :, :].bitcast(F32),
                                            ALU.subtract).then_inc(mlp_lo_ready, 1)
                if l + 1 < DEPTH:
                    take_mod(l + 1, 0, 6 * KT, direct_at[("ada", l + 1, 23)] + 1)
                for p in range(KT // 2):
                    if p < 3:
                        dve.wait_ge(down_ready, 3 * l + p + 1)
                    else:
                        dve.wait_ge(unit_used, unit_no(l + 1, 0))
                    residual(l, 5, p, bank[3 + p])
            inverse(2 * DEPTH)
            dve.wait_ge(rstd_ready, 2 * DEPTH + 1)
            for k in range(KT):
                nc.vector.scalar_tensor_tensor(wide[:, k, :], xT[:, k, :], vec[:, 0, V_FIN + k:V_FIN + k + 1],
                                               rstd[:, :], ALU.mult, ALU.mult).then_inc(fin_ready, 1)


def kernel(**inputs):
    import concourse.bacc as bacc
    from concourse.bass_utils import run_bass_kernel_spmd

    names = ["x", "c", "w_ada", "b_ada", "norm1_gain", "w_in", "f_bias", "diff_lambda", "diff_subln_gain",
             "w_dq_up", "w_didx_q", "w_dkv_up", "w_out", "t5_table", "norm2_gain", "w_ffn_up", "ffn_conv_w",
             "ffn_conv_b", "w_ffn_down", "final_gain"]
    nc = bacc.Bacc("TRN2", target_bir_lowering=False, num_devices=1)
    arrays = {f"in_{n}": np.ascontiguousarray(inputs[n]) for n in names}
    arrays["in_buckets"] = bucket_rows()
    args = [nc.dram_tensor(n, a.shape, mybir.dt.from_np(a.dtype), kind="ExternalInput").ap() for n, a in arrays.items()]
    args.append(nc.dram_tensor("out_0", (1, SEQ, D_MODEL), F32, kind="ExternalOutput").ap())
    trunk(nc, *args)
    r = run_bass_kernel_spmd(nc, [arrays], core_ids=[0])
    return r.results[0]["out_0"]
```

```python
import math
from contextlib import ExitStack

import concourse.bass as bass
import numpy as np
from concourse import mybir

F32 = mybir.dt.float32
F32R = mybir.dt.float32r
ACT = mybir.ActivationFunctionType
ALU = mybir.AluOpType
AX = mybir.AxisListType

P = 128
EPS = 1e-6
BIG = 1e30
TAKEN = -3e38

D_MODEL, SEQ, DEPTH, D_FF = 1024, 256, 2, 2816
HEAD, HALF, HEADS = 64, 32, 4
GROUP = HEADS * HEAD
KT = D_MODEL // P
TT = SEQ // P
UC = 256
FT = D_FF // P
STEPS = FT // 2
BUCKETS, T5_MAX = 32, 128
TOPK = min(256, SEQ // 4)

C_FC = 9 * GROUP
IN_COLS = C_FC + HEADS + GROUP + 2 * P + HEAD + HEADS
TAIL = IN_COLS - C_FC
T_GC, T_LAT = HEADS, HEADS + GROUP
T_KIDX = T_LAT + 2 * P
T_WIDX = T_KIDX + HEAD

IN_UNITS = [("tail", 256, 256), ("tail", 512, TAIL - 512), ("tail", 0, 256)]
IN_UNITS += [(what, g, UC) for g in range(3) for what in "qkv"]
NI = len(IN_UNITS)
NO = D_MODEL // UC
PER_LAYER = NI + NO + 3 * STEPS
RAW = 3

MAPS = [(0, h, c) for h in range(4) for c in range(2)] + [(g, h, 0) for g in (1, 2, 3) for h in range(4)]
NM = len(MAPS)
SCALE = [HALF ** -0.5, HEAD ** -0.5, HEAD ** -0.5, HEAD ** -0.5]

V_BADA, V_N1, V_N2, V_CB = 0, 48, 56, 64
V_W0, V_W1 = 128, 128 + 2 * FT
V_W2, V_FIN, V_C = 256, 256 + 2 * FT, 256 + 2 * FT + KT
VROWS = [64 + 2 * FT, 4 * FT, 2 * FT + 2 * KT]


def bucket_rows():
    y = np.arange(384)
    dist = SEQ - 1 - y
    exact = BUCKETS // 2
    d = np.maximum(dist, 0)
    ratio = np.maximum(d, 1).astype(np.float32) / np.float32(exact)
    large = exact + (np.log(ratio) / np.float32(math.log(T5_MAX / exact)) * np.float32(BUCKETS - exact)).astype(np.int32)
    bucket = np.where(d < exact, d, np.minimum(large, BUCKETS - 1))
    rows = np.zeros((BUCKETS + 1, 384), np.float32)
    rows[bucket, y] = dist >= 0
    rows[BUCKETS] = dist < 0
    return rows


def direct_units():
    ada = [[("ada", l, u) for u in range(6 * D_MODEL // UC)] for l in range(DEPTH)]
    return ada[0][:8] + [("dsa", 0, 0)] + ada[0][8:] + ada[1] + [("dsa", 1, 0)]


def layer_schedule(l):
    s = []
    late = [("ada", 0, u) for u in range(8, 24, 2)] if l == 0 else []
    fill = [("ada", 1, u) for u in range(0, 8, 2)] if l == 0 else []
    choose = [("choose", r) for r in range(TOPK // 8)]
    scored, turned = [], []
    at = [0]

    def values(ms):
        for m in ms:
            s.append(("values", m))
            if m % 4 == 3:
                s.append(("heads", m // 4))
            if m == 7:
                s.append(("subln", 0))
            if m == 9:
                s.append(("subln_end", 0))

    def maps(n):
        nonlocal scored, turned
        for m in scored:
            s.append(("probs", m))
        values(turned)
        turned = scored
        scored = list(range(at[0], min(at[0] + n, NM)))
        at[0] += len(scored)
        for m in scored:
            s.append(("scores", m))
        for m in scored:
            s.append(("softmax", m))

    for i in range(NI):
        ada = late.pop(0) if i >= 4 and late else None
        if ada:
            s.append(ada)
        s += [("unit", i, 0, KT), ("evac", i)]
        if ada:
            s.append(("ada_turn",) + ada[1:])
        if i == 1:
            s += [("split", 4), ("latents_norm", 0)]
        if i == 2:
            s += [("latents", 0), ("split", 5), ("forget", 0)]
        if i == 3:
            s.append(("latents_up", 0))
        if i == 4:
            s += [("forget_up", 0), ("index", 0), ("index", 1)]
        if i == 5:
            s += [("index", 2), ("index", 3)]
        if i >= 5:
            maps(2)
        if i not in (1, 2):
            s.append(("split", i + RAW))
        if i >= 5 and choose:
            s.append(choose.pop(0))
    s += choose
    maps(2)
    s += [("turn", 0), ("turn", 1), ("unit", NI, 0, 4)]
    s += fill[0:1]
    maps(2)
    s += [("ada_turn",) + e[1:] for e in fill[0:1]]
    s.append(("unit", NI + 1, 0, 4))
    maps(2)
    s += [("turn", 2), ("unit", NI + 2, 0, 4)]
    s += fill[1:2]
    maps(0)
    s += [("ada_turn",) + e[1:] for e in fill[1:2]]
    s += [("unit", NI, 4, 6), ("unit", NI + 1, 4, 6), ("unit", NI + 2, 4, 6)]
    maps(0)
    s += fill[2:3]
    s += [("turn", 3)]
    s += [("ada_turn",) + e[1:] for e in fill[2:3]]
    s += fill[3:4]
    s += [("ada_turn",) + e[1:] for e in fill[3:4]]
    for i in range(NI, NI + NO):
        s.append(("unit", i, 6 if i < NI + 3 else 0, KT))
        s.append(("resid", i - NI))
        if i > NI:
            s.append(("mean", i - NI - 1))
        if i + RAW < NI + NO + 2:
            s.append(("split", i + RAW))
    s.append(("mean", NO - 1))
    return s


def trunk(nc, x, c, w_ada, b_ada, norm1_gain, w_in, f_bias, diff_lambda, diff_subln_gain, w_dq_up,
          w_didx_q, w_dkv_up, w_out, t5_table, norm2_gain, w_ffn_up, ffn_conv_w, ffn_conv_b,
          w_ffn_down, final_gain, buckets, out):
    DIRECT = direct_units()
    DSLOTS = 3
    direct_at = {u: a for a, u in enumerate(DIRECT)}
    schedules = [layer_schedule(l) for l in range(DEPTH)]
    lam_init = [0.8 - 0.6 * math.exp(-0.3 * l) for l in range(DEPTH)]

    with ExitStack() as ctx:
        def sb(name, shape, dt=F32):
            return ctx.enter_context(nc.sbuf_tensor(name, shape, dt))

        def sem(name):
            return ctx.enter_context(nc.semaphore(name))

        bank = [ctx.enter_context(nc.psum_tensor(f"bank{i}", [P, 512], F32)) for i in range(8)]
        raw = [sb(f"raw{i}", [P, KT * UC]) for i in range(RAW)]
        w_hi = [sb(f"w_hi{i}", [P, KT * UC], F32R) for i in range(RAW)]
        w_lo = [sb(f"w_lo{i}", [P, KT * UC], F32R) for i in range(RAW)]
        direct = [sb(f"direct{i}", [P, KT * UC]) for i in range(DSLOTS)]
        xT = sb("xT", [P, KT, SEQ])
        act_hi = sb("act_hi", [P, KT, SEQ], F32R)
        act_lo = sb("act_lo", [P, KT, SEQ], F32R)
        mlp_hi = sb("mlp_hi", [P, 2, SEQ], F32R)
        mlp_lo = sb("mlp_lo", [P, 2, SEQ], F32R)
        qkT = sb("qkT", [P, 4, 2, 2, SEQ])
        qiT = sb("qiT", [P, 2, SEQ])
        kiT = sb("kiT", [P, SEQ])
        v_sb = sb("v_sb", [P, 4, TT, GROUP])
        tail = sb("tail", [P, TT, TAIL])
        bias = sb("bias", [P, 3 * HEADS, SEQ])
        own_bias = sb("own_bias", [P, HEADS, 3, P])
        work = sb("work", [P, 6 * 384])
        heads_out = sb("heads_out", [P, 4, TT, GROUP])
        vec = sb("vec", [P, DEPTH, 384])
        mod = sb("mod", [P, DEPTH, 48])
        amp = sb("amp", [P, 2, KT])
        cond = sb("cond", [P, KT, 32])
        ada_row = sb("ada_row", [P, 512])
        ident = sb("ident", [P, P])
        reverse = sb("reverse", [P, P])
        mean_w = sb("mean_w", [P, P])
        upto = sb("upto", [P, SEQ])
        one = sb("one", [P, 1])
        rstd = sb("rstd", [P, SEQ])
        lam_in = sb("lam_in", [P, DEPTH, 4, HALF])
        lam_pr = sb("lam_pr", [P, DEPTH * 2, HALF])
        lam_ex = sb("lam_ex", [P, DEPTH * 2])
        nlam = sb("nlam", [P, DEPTH])
        gain64 = sb("gain64", [P, DEPTH, HEAD])
        fb = sb("fb", [P, DEPTH, HEADS])
        tab = sb("tab", [BUCKETS + 1, 3 * HEADS])
        lat_ss = sb("lat_ss", [P, 4])
        fz = sb("fz", [P, 4, TT * HEADS])
        ncq = sb("ncq", [P, TT * HEADS])
        low = sb("low", [P, 3, 2])
        rsum = sb("rsum", [P, 2, TT, 4])
        rinv = sb("rinv", [P, TT, 4])
        top8 = sb("top8", [P, 8])
        pair = sb("pair", [P, TT, 4, HEAD])
        half = sb("half", [P, 8])
        nrm = sb("nrm", [P, TT * HEADS])
        score = sb("score", [P, 3, P])
        toeplitz = nc.dram_tensor("toeplitz", (3 * HEADS, 384), F32, kind="Internal").ap()

        soft = [work[:, 384 * i:384 * i + 384].rearrange("p (b k) -> p b k", b=3) for i in range(3)]
        probT = [work[:, 1152 + 384 * i:1536 + 384 * i].rearrange("p (b q) -> p b q", b=3) for i in range(3)]
        relu = [work[:, 384 * i:384 * i + 384].rearrange("p (b k) -> p b k", b=3) for i in range(2)]
        latT = work[:, 0:512].rearrange("p (w t) -> p w t", w=2)
        ki_twice = work[:, 1664:1920].rearrange("p (t a d) -> p t a d", t=TT, a=2)
        latn = work[:, 1152:1664].rearrange("p (t w d) -> p t w d", t=TT, w=2)
        lf_wide = work[:, 1024:2048].rearrange("p (c q) -> p c q", c=TT * HEADS)
        conv = work[:, 0:1024].rearrange("p (w f t) -> p w f t", w=2, f=2)
        silu = work[:, 1024:1536].rearrange("p (f t) -> p f t", f=2)
        prod = work[:, 1536:2048].rearrange("p (f t) -> p f t", f=2)
        wide = work[:, 0:KT * SEQ].rearrange("p (k t) -> p k t", k=KT)
        buck = own_bias[0:BUCKETS + 1, 0, :, :].rearrange("p b k -> p (b k)")
        diag = own_bias[0:3 * HEADS, 1, :, :].rearrange("p b k -> p (b k)")
        gate_c = tail[:, :, T_GC:T_GC + GROUP]
        flipped = qkT[:, :, :, :, :].rearrange("p g w h t -> p (g w h t)")[:, 0:3 * HEADS * SEQ].rearrange(
            "p (h k) -> p h k", k=SEQ)
        FLIP_BANKS = [1, 2, 3, 4, 5, 6]
        x_tok = heads_out[:, :, :, :].rearrange("p g t n -> p (g t n)").rearrange("p (t n) -> p t n", t=TT)
        rows_in = v_sb[:, 0:3, :, :].rearrange("p g t n -> p (g t n)")[:, 0:DEPTH * 384].rearrange(
            "p (l r n) -> p l r n", l=DEPTH, r=3)

        raw_in = [sem(f"raw_in{i}") for i in range(RAW)]
        direct_in = [sem(f"direct_in{i}") for i in range(DSLOTS)]
        small_in = sem("small_in")
        x_in = sem("x_in")
        rows_sem = sem("rows_in")
        consts = sem("consts")
        diag_ready = sem("diag_ready")
        toep_out = sem("toep_out")
        bias_in = sem("bias_in")
        flip_ready = sem("flip_ready")
        flip_read = sem("flip_read")
        setup_pe = sem("setup_pe")
        cond_ready = sem("cond_ready")
        lam_sem = sem("lam_sem")
        tab_ready = sem("tab_ready")
        lam_exp = sem("lam_exp")
        vec_in = sem("vec_in")
        tap_ready = sem("tap_ready")
        out_part = sem("out_part")
        hi_done = sem("hi_done")
        lo_done = sem("lo_done")
        unit_used = sem("unit_used")
        direct_used = sem("direct_used")
        mod_ready = sem("mod_ready")
        mod_done = sem("mod_done")
        ada_rows = sem("ada_rows")
        ada_turned = sem("ada_turned")
        x_new = sem("x_new")
        squares = sem("squares")
        ms_ready = sem("ms_ready")
        ms_inv = sem("ms_inv")
        rstd_ready = sem("rstd_ready")
        scaled = sem("scaled")
        act_hi_ready = sem("act_hi_ready")
        act_lo_ready = sem("act_lo_ready")
        in_read = sem("in_read")
        lat_root = sem("lat_root")
        lat_ready = sem("lat_ready")
        latT_ready = sem("latT_ready")
        latT_read = sem("latT_read")
        up_read = sem("up_read")
        s_ready = sem("s_ready")
        idx_relu = sem("idx_relu")
        score_masked = sem("score_masked")
        chosen = sem("chosen")
        fz_ready = sem("fz_ready")
        fe_ready = sem("fe_ready")
        lf_ready = sem("lf_ready")
        lfw_ready = sem("lfw_ready")
        cum_ready = sem("cum_ready")
        ncq_ready = sem("ncq_ready")
        ck_ready = sem("ck_ready")
        own_ready = sem("own_ready")
        low_ready = sem("low_ready")
        exp_ready = sem("exp_ready")
        t_ready = sem("t_ready")
        pt_act = sem("pt_act")
        pt_dve = sem("pt_dve")
        pv_ready = sem("pv_ready")
        o_read = sem("o_read")
        group_ready = sem("group_ready")
        idx_acc = sem("idx_acc")
        lat_inv = sem("lat_inv")
        ki_ready = sem("ki_ready")
        up_ready = sem("up_ready")
        gate_exp = sem("gate_exp")
        finT_ready = sem("finT_ready")
        down_ready = sem("down_ready")
        sub_done = sem("sub_done")
        sub_ss = sem("sub_ss")
        sub_root = sem("sub_root")
        turn_hi = sem("turn_hi")
        turn_lo = sem("turn_lo")
        conv_read = sem("conv_read")
        silu_ready = sem("silu_ready")
        prod_done = sem("prod_done")
        mlp_hi_ready = sem("mlp_hi_ready")
        mlp_lo_ready = sem("mlp_lo_ready")
        fin_ready = sem("fin_ready")
        stored = sem("stored")
        dve_own = sem("dve_own")

        def unit_no(l, i):
            return PER_LAYER * l + i

        def wait_raw(eng, n):
            eng.wait_ge(raw_in[n % RAW], 16 * (n // RAW + 1))

        def unit_bank(i):
            return bank[i % 2 if i < NI else i - NI]

        def ada_no(l, u):
            return 12 * l + u // 2

        def mlp_ada(l, j):
            return (l + 1, 8 + 2 * (j - 1)) if l + 1 < DEPTH and 1 <= j <= 8 else None

        def unit_width(i):
            return IN_UNITS[i][2] if i < NI else UC

        def unit_shape(i):
            return KT * unit_width(i)

        SC = HEADS + NM
        turn_order = []
        for st, i in [e[:2] for e in schedules[0]]:
            if st == "probs":
                turn_order.append(("probs", i))
            elif st == "turn":
                turn_order += [("turn", i, 0)]
        NT = len(turn_order)
        turn_no = {k: n for n, k in enumerate(turn_order)}
        act_frees, dve_frees, freed_by = 0, 0, []
        for n, k in enumerate(turn_order):
            if k[0] == "turn":
                freed_by.append(("lo", k[1]))
            elif n % 2 == 0:
                act_frees += 1
                freed_by.append(("act", act_frees))
            else:
                dve_frees += 1
                freed_by.append(("dve", dve_frees))

        def wait_turned(eng, l, n, slack=0):
            kind, k = freed_by[n]
            if kind == "act":
                eng.wait_ge(pt_act, act_frees * l + k)
            elif kind == "dve":
                eng.wait_ge(pt_dve, dve_frees * l + k)
            else:
                eng.wait_ge(turn_lo, 4 * l + k + 1)

        block = ctx.enter_context(nc.Block())

        @block.sync
        def _(sp):
            for l in range(DEPTH):
                def rows(t, first, src, n):
                    sp.dma_start(rows_in[first:first + n, l, t, :], src.rearrange("(r n) -> r n", n=P)).then_inc(
                        rows_sem, 16)
                rows(0, V_BADA, b_ada[l], 48)
                rows(0, V_N1, norm1_gain[l], KT)
                rows(0, V_N2, norm2_gain[l], KT)
                rows(0, V_CB, ffn_conv_b[l], 2 * FT)
                rows(1, 0, ffn_conv_w[l, 0], 2 * FT)
                rows(1, 2 * FT, ffn_conv_w[l, 1], 2 * FT)
                rows(2, 0, ffn_conv_w[l, 2], 2 * FT)
                rows(2, 2 * FT, final_gain, KT)
                rows(2, 2 * FT + KT, c[0], KT)
            sp.dma_start(x_tok, x[0].rearrange("(t p) n -> p t n", p=P)).then_inc(x_in, 16)

            def load_direct(a):
                kind, l, u = DIRECT[a]
                if a >= DSLOTS:
                    sp.wait_ge(direct_used, a - DSLOTS + 1)
                slot = direct[a % DSLOTS]
                if kind == "ada":
                    sp.dma_start(slot[:, :].rearrange("p (k n) -> p k n", k=KT),
                                 w_ada[l].rearrange("(k p) n -> p k n", p=P)[:, :, u * UC:(u + 1) * UC]).then_inc(
                        direct_in[a % DSLOTS], 16)
                else:
                    sp.dma_start(slot[:, 0:256], w_dq_up[l]).then_inc(direct_in[a % DSLOTS], 16)
                    sp.dma_start(slot[:, 256:512], w_didx_q[l]).then_inc(direct_in[a % DSLOTS], 16)
                    sp.dma_start(slot[:, 512:1024], w_dkv_up[l]).then_inc(direct_in[a % DSLOTS], 16)

            def load_unit(l, i):
                n = unit_no(l, i)
                if n >= RAW:
                    sp.wait_ge(lo_done, n - RAW + 1)
                dst, j = raw[n % RAW], i - NI - NO
                if i < NI:
                    kind, g, width = IN_UNITS[i]
                    c0 = C_FC + g if kind == "tail" else 3 * GROUP * g + GROUP * "qkv".index(kind)
                    src = w_in[l].rearrange("(k p) n -> p k n", p=P)[:, :, c0:c0 + width]
                    dst = dst[:, 0:KT * width].rearrange("p (k n) -> p k n", k=KT)
                else:
                    src = w_out[l].rearrange("(k p) n -> p k n", p=P)[:, :, (i - NI) * UC:(i - NI + 1) * UC]
                    dst = dst[:, :].rearrange("p (k n) -> p k n", k=KT)
                sp.dma_start(dst, src).then_inc(raw_in[n % RAW], 16)

            def load_mlp(l, o, what, j):
                n = unit_no(l, NI + NO + o)
                sp.wait_ge(lo_done, n - RAW + 1)
                dst = raw[n % RAW]
                if what == "down":
                    src = w_ffn_down[l, j * UC:(j + 1) * UC, :].rearrange("(f p) n -> p f n", p=P)
                    dst = dst[:, :].rearrange("p (f n) -> p f n", f=2)
                else:
                    c0 = j * UC + (D_FF if what == "value" else 0)
                    src = w_ffn_up[l].rearrange("(k p) n -> p k n", p=P)[:, :, c0:c0 + UC]
                    dst = dst[:, :].rearrange("p (k n) -> p k n", k=KT)
                sp.dma_start(dst, src).then_inc(raw_in[n % RAW], 16)

            for a in range(4):
                if a < DSLOTS:
                    load_direct(a)
            sp.dma_start(tab[0:BUCKETS, :], t5_table).then_inc(small_in, 16)
            sp.dma_start(buck[:, :], buckets).then_inc(small_in, 16)
            sp.dma_start(lam_in[:, :, :, :], diff_lambda.rearrange("l a d -> (l a d)").partition_broadcast(P)).then_inc(
                small_in, 16)
            sp.dma_start(gain64[:, :, :], diff_subln_gain.rearrange("l d -> (l d)").partition_broadcast(P)).then_inc(
                small_in, 16)
            sp.dma_start(fb[:, :, :], f_bias.rearrange("l d -> (l d)").partition_broadcast(P)).then_inc(small_in, 16)
            for a in range(DSLOTS, 8):
                load_direct(a)
            for i in range(RAW):
                load_unit(0, i)
            a = 8
            for l in range(DEPTH):
                uses = 0
                for e in schedules[l]:
                    if e[0] == "latents":
                        load_direct(direct_at[("dsa", l, 0)])
                    elif e[0] == "ada":
                        load_direct(direct_at[e])
                        load_direct(direct_at[("ada", e[1], e[2] + 1)])
                    elif e[0] == "split" and e[1] < NI + NO:
                        load_unit(l, e[1])
                load_mlp(l, 0, "gate", 0)
                load_mlp(l, 1, "value", 0)
                for j in range(STEPS - 1):
                    load_mlp(l, 3 * j + 2, "gate", j + 1)
                    if mlp_ada(l, j + 1):
                        la, u = mlp_ada(l, j + 1)
                        load_direct(direct_at[("ada", la, u)])
                        load_direct(direct_at[("ada", la, u + 1)])
                    load_mlp(l, 3 * j + 3, "value", j + 1)
                    load_mlp(l, 3 * j + 4, "down", j)
                load_mlp(l, 3 * STEPS - 1, "down", STEPS - 1)
                if l + 1 < DEPTH:
                    for i in range(RAW):
                        load_unit(l + 1, i)
            for t in range(TT):
                sp.wait_ge(out_part, 2 * t + 2)
                sp.dma_start(out[0, t * P:(t + 1) * P, :], x_tok[:, t, :]).then_inc(stored, 16)
            sp.wait_ge(stored, 16 * TT)

        @block.gpsimd
        def _(pool):
            nc.gpsimd.memset(ident[:, :], 0.0)
            nc.gpsimd.memset(reverse[:, :], 0.0)
            nc.gpsimd.memset(upto[:, :], 1.0)
            nc.gpsimd.memset(mean_w[:, :], 1.0 / D_MODEL)
            nc.gpsimd.memset(one[:, :], 1.0)
            nc.gpsimd.memset(half[:, :], 0.5).then_inc(consts, 1)
            pool.wait_ge(consts, 1)
            nc.gpsimd.affine_select(out=ident[:, :], in_=ident[:, :], compare_op=ALU.not_equal, fill=1.0, base=0,
                                    pattern=[[-1, P]], channel_multiplier=1)
            nc.gpsimd.affine_select(out=upto[:, :], in_=upto[:, :], compare_op=ALU.is_ge, fill=0.0, base=0,
                                    pattern=[[1, SEQ]], channel_multiplier=-1).then_inc(consts, 1)
            nc.gpsimd.affine_select(out=reverse[:, :], in_=reverse[:, :], compare_op=ALU.not_equal, fill=1.0,
                                    base=1 - P, pattern=[[1, P]], channel_multiplier=1).then_inc(consts, 1)
            for l in range(DEPTH):
                for e in schedules[l]:
                    if e[0] == "latents_norm":
                        pool.wait_ge(lat_inv, l + 1)
                        nc.gpsimd.tensor_tensor(lat_ss[:, :], lat_ss[:, :], half[:, 0:4], ALU.pow).then_inc(lat_root, 1)
                    elif e[0] == "subln":
                        pool.wait_ge(sub_ss, l + 1)
                        nc.gpsimd.tensor_tensor(nrm[:, :], nrm[:, :], half[:, :], ALU.pow).then_inc(sub_root, 1)
                    elif e[0] == "forget":
                        pool.wait_ge(lf_ready, l + 1)
                        nc.gpsimd.tensor_copy(lf_wide, fz[:, 3, :].unsqueeze(2).to_broadcast([P, TT * HEADS, P])).then_inc(
                            lfw_ready, 1)
                    elif e[0] == "choose" and e[1] == 0:
                        pool.wait_ge(idx_acc, 2 * HEADS * (l + 1))
                        nc.gpsimd.affine_select(out=score[:, 0::2, :], in_=score[:, 0::2, :], compare_op=ALU.is_ge,
                                                fill=-BIG, base=0, pattern=[[0, 2], [-1, P]],
                                                channel_multiplier=1).then_inc(score_masked, 1)
                    elif e[0] == "forget_up":
                        for h in range(HEADS):
                            pool.wait_ge(ck_ready, HEADS * l + h + 1)
                            nc.gpsimd.affine_select(out=own_bias[:, h, 0::2, :], in_=own_bias[:, h, 0::2, :],
                                                    compare_op=ALU.is_ge, fill=BIG, base=0,
                                                    pattern=[[0, 2], [-1, P]], channel_multiplier=1).then_inc(
                                own_ready, 1)
                    elif e[0] == "softmax" and MAPS[e[1]][0] == 2:
                        h = MAPS[e[1]][1]
                        pool.wait_ge(chosen, l + 1)
                        if l == 0 and h == 0:
                            pool.wait_ge(flip_read, 6)
                        pool.wait_ge(low_ready, 2 * (NM * l + e[1]) + 2)
                        nc.gpsimd.tensor_tensor(own_bias[:, h, 0, :], score[:, 0, :], bias[:, 2 * HEADS + h, P:2 * P],
                                                ALU.add)
                        nc.gpsimd.tensor_tensor(own_bias[:, h, 1:3, :], score[:, 1:3, :],
                                                bias[:, 2 * HEADS + h, :].rearrange("p (b k) -> p b k", b=2),
                                                ALU.add).then_inc(own_ready, 1)

        @block.tensor
        def _(pe):
            def product3(dst, lhs, rhs, first, last, check=False):
                (lh, ll), (rh, rl) = lhs, rhs
                pe.matmul(dst, lh, rh, start=first, stop=False, skip_group_check=check)
                pe.matmul(dst, lh, rl, start=False, stop=False, skip_group_check=check)
                return pe.matmul(dst, ll, rh, start=False, stop=last, skip_group_check=check)

            def ada(l, u):
                n = ada_no(l, u)
                if n:
                    pe.wait_ge(mod_ready, n)
                for half in range(2):
                    a = direct_at[("ada", l, u + half)]
                    pe.wait_ge(direct_in[a % DSLOTS], direct_value(a))
                    w = direct[a % DSLOTS][:, :].rearrange("p (k n) -> p k n", k=KT)
                    for i in range(2):
                        for g in range(4):
                            k = 4 * i + g
                            mm = pe.matmul(bank[7][32 * g:32 * g + 32, half * UC:(half + 1) * UC], cond[:, k, :],
                                           w[:, k, :], start=(i == 0), stop=(i == 1))
                    mm.then_inc(direct_used, 1)

            def ada_turn(l, u):
                n = ada_no(l, u)
                pe.wait_ge(ada_rows, n + 1)
                for ct in range(4):
                    mm = pe.transpose(bank[7][:, ct * P:(ct + 1) * P], ada_row[:, ct * P:(ct + 1) * P], ident[:, :])
                mm.then_inc(ada_turned, 1)

            def direct_value(a):
                return 16 * sum(3 if DIRECT[b][0] == "dsa" else 1 for b in range(a % DSLOTS, a + 1, DSLOTS))

            def mean_of(n, p):
                pe.wait_ge(squares, 4 * n + p + 1)
                for k in (2 * p, 2 * p + 1):
                    mm = pe.matmul(bank[7][:, SEQ:2 * SEQ], mean_w[:, :], wide[:, k, :],
                                   start=(k == 0), stop=(k == KT - 1), skip_group_check=True)
                if p == KT // 2 - 1:
                    mm.then_inc(ms_ready, 1)
                    pe.wait_ge(ms_inv, n + 1)

            def mean_square(n):
                for p in range(KT // 2):
                    mean_of(n, p)

            def unit_product(l, i, bk, wait_act=None, k0=0, k1=KT):
                n = unit_no(l, i)
                pe.wait_ge(lo_done, n + 1)
                width = unit_width(i) if i < NI else UC
                wh = w_hi[n % RAW][:, 0:KT * width].rearrange("p (k n) -> p k n", k=KT)
                wl = w_lo[n % RAW][:, 0:KT * width].rearrange("p (k n) -> p k n", k=KT)
                token_rows = i < NI and IN_UNITS[i][0] in ("tail", "v")
                for t in range(2):
                    for k in range(k0, k1):
                        if wait_act is not None and t == 0:
                            pe.wait_ge(act_lo_ready, wait_act + k + 1)
                        s = slice(t * P, (t + 1) * P)
                        if token_rows:
                            mm = product3(bk[:, t * width:(t + 1) * width],
                                          (act_hi[:, k, s], act_lo[:, k, s]), (wh[:, k, :], wl[:, k, :]),
                                          k == 0 and t == 0, k == KT - 1, True)
                        else:
                            mm = product3(bk[:, t * SEQ:(t + 1) * SEQ], (wh[:, k, s], wl[:, k, s]),
                                          (act_hi[:, k, :], act_lo[:, k, :]), k == 0 and t == 0, k == KT - 1, True)
                return mm

            pe.wait_ge(consts, 2)
            pe.wait_ge(rows_sem, 16 * 9 * DEPTH)
            for l in range(DEPTH):
                for t in range(3):
                    mm = pe.transpose(bank[l][:, P * t:P * t + VROWS[t]], rows_in[0:VROWS[t], l, t, :],
                                      ident[0:VROWS[t], 0:VROWS[t]])
            mm.then_inc(setup_pe, 1)
            pe.wait_ge(x_in, 16)
            for k in range(KT):
                for t in range(TT):
                    mm = pe.transpose(bank[2 + k // 2][:, (k % 2) * SEQ + t * P:(k % 2) * SEQ + (t + 1) * P],
                                      x_tok[:, t, k * P:(k + 1) * P], ident[:, :])
                if k % 2:
                    mm.then_inc(setup_pe, 1)
            pe.wait_ge(small_in, 16 * 5)
            pe.wait_ge(tab_ready, 1)
            pe.matmul(bank[6][0:3 * HEADS, 0:384], tab[:, :], buck[:, :], start=True, stop=True).then_inc(setup_pe, 1)
            mean_square(0)
            pe.wait_ge(cond_ready, 1)
            for u in range(0, 8, 2):
                ada(0, u)
                ada_turn(0, u)
            pe.wait_ge(mod_ready, 4)
            pe.wait_ge(bias_in, 16)
            pe.wait_ge(consts, 3)
            for i, b in enumerate(FLIP_BANKS):
                pe.matmul(bank[b][:, :], reverse[:, :], flipped[:, 2 * i:2 * i + 2, :], start=True,
                          stop=True).then_inc(flip_ready, 1)

            def scores(l, m):
                s = SC * l + HEADS + m
                g, h, comp = MAPS[m]
                if m < 2:
                    pe.wait_ge(idx_relu, HEADS * l + HEADS - 1 + m)
                else:
                    pe.wait_ge(low_ready, 2 * (NM * l + m - 2) + 2)
                p0, width = ((h % 2) * HEAD + comp * HALF, HALF) if g == 0 else ((h % 2) * HEAD, HEAD)
                q = qkT[p0:p0 + width, g, 0, h // 2, :]
                k = qkT[p0:p0 + width, g, 1, h // 2, :]
                pe.matmul(bank[2 + s % 2][:, 0:P], q[:, 0:P], k[:, 0:P], start=True, stop=True)
                pe.matmul(bank[2 + s % 2][:, P:3 * P], q[:, P:2 * P], k, start=True, stop=True).then_inc(s_ready, 1)

            for l in range(DEPTH):
                norm = 2 * l
                if l > 0:
                    mean_square(norm)
                for e in schedules[l]:
                    st, i = e[0], e[1]
                    if st == "unit":
                        if l == 0 and i == 1:
                            pe.wait_ge(flip_read, 1)
                        if 2 <= i < NI + 2:
                            pe.wait_ge(in_read, NI * l + i - 1)
                        elif i >= NI + 2:
                            pe.wait_ge(low_ready, 2 * NM * (l + 1))
                        if i >= NI:
                            pe.wait_ge(turn_lo, 4 * l + e[3] // 2)
                        mm = unit_product(l, i, unit_bank(i), KT * norm if i == 0 else None, e[2], e[3])
                        if e[3] == KT:
                            mm.then_inc(unit_used, 1)
                    elif st == "mean":
                        mean_of(norm + 1, i)
                    elif st == "ada":
                        ada(e[1], e[2])
                    elif st == "ada_turn":
                        ada_turn(e[1], e[2])
                    elif st == "latents":
                        pe.wait_ge(ki_ready, l + 1)
                        for t in range(TT):
                            pe.transpose(bank[4][:, t * P:(t + 1) * P],
                                         ki_twice[:, t, :, :].rearrange("p a d -> p (a d)"), ident[:, :])
                        pe.wait_ge(lat_ready, l + 1)
                        for w in range(2):
                            for t in range(TT):
                                mm = pe.transpose(bank[6][:, w * SEQ + t * P:w * SEQ + (t + 1) * P], latn[:, t, w, :],
                                                  ident[:, :])
                        mm.then_inc(latT_ready, 1)
                    elif st == "latents_up":
                        pe.wait_ge(latT_read, 2 * l + 2)
                        a = direct_at[("dsa", l, 0)]
                        pe.wait_ge(direct_in[a % DSLOTS], direct_value(a))
                        w = direct[a % DSLOTS]
                        for b, c0, src in ((2, 0, 0), (3, 256, 0), (4, 512, 1)):
                            for t in range(2):
                                mm = pe.matmul(bank[b][:, t * SEQ:(t + 1) * SEQ], w[:, c0 + t * P:c0 + (t + 1) * P],
                                               latT[:, src, :], start=True, stop=True)
                            mm.then_inc(up_ready, 1)
                        for t in range(TT):
                            mm = pe.matmul(bank[5][:, t * GROUP:(t + 1) * GROUP], latT[:, 1, t * P:(t + 1) * P],
                                           w[:, 768:1024], start=True, stop=True)
                        mm.then_inc(direct_used, 1)
                    elif st == "index":
                        pe.wait_ge(up_read, 4 * l + 4)
                        for h in (i,):
                            s = SC * l + h
                            if h >= 2:
                                pe.wait_ge(idx_relu, HEADS * l + h - 1)
                            r = slice((h % 2) * HEAD, (h % 2) * HEAD + HEAD)
                            b = bank[2 + s % 2]
                            pe.matmul(b[:, 0:P], qiT[r, h // 2, 0:P], kiT[r, 0:P], start=True, stop=True)
                            pe.matmul(b[:, P:3 * P], qiT[r, h // 2, P:2 * P], kiT[r, :], start=True,
                                      stop=True).then_inc(s_ready, 1)
                    elif st == "forget_up":
                        pe.wait_ge(lf_ready, l + 1)
                        if l == 0:
                            pe.wait_ge(mod_ready, 5)
                        lf = fz[:, 3, :].rearrange("p (t h) -> p t h", t=TT)
                        pe.matmul(bank[7][:, 128:132], upto[:, 0:P], lf[:, 0, :], start=True, stop=True)
                        pe.matmul(bank[7][:, 132:136], upto[:, P:2 * P], lf[:, 0, :], start=True, stop=False)
                        pe.matmul(bank[7][:, 132:136], upto[:, 0:P], lf[:, 1, :], start=False,
                                  stop=True).then_inc(cum_ready, 1)
                        pe.wait_ge(up_read, 4 * l + 4)
                        pe.wait_ge(lfw_ready, l + 1)
                        for h in range(HEADS):
                            b = bank[4 + h // 2][:, (h % 2) * SEQ:(h % 2 + 1) * SEQ]
                            pe.matmul(b, lf_wide[:, h, :], upto[:, :], start=True, stop=False)
                            mm = pe.matmul(b[:, P:2 * P], lf_wide[:, HEADS + h, :], upto[:, 0:P], start=False, stop=True)
                        mm.then_inc(cum_ready, 1)
                        pe.wait_ge(ncq_ready, l + 1)
                    elif st == "scores":
                        scores(l, i)
                    elif st == "probs":
                        n = turn_no[("probs", i)]
                        if n >= 2:
                            wait_turned(pe, l, n - 2)
                        else:
                            pe.wait_ge(ck_ready, HEADS * (l + 1))
                        pe.wait_ge(exp_ready, 2 * (NM * l + i) + 2)
                        for b in range(3):
                            mm = pe.transpose(bank[4 + n % 2][:, b * P:(b + 1) * P], soft[i % 3][:, b, :], ident[:, :])
                        mm.then_inc(t_ready, 1)
                    elif st == "values":
                        g, h, comp = MAPS[i]
                        slot, quad = i % 4, i // 4
                        wait_turned(pe, l, turn_no[("probs", i)])
                        if slot == 0 and quad > 0:
                            pe.wait_ge(o_read, 5 * l + quad)
                        pt = probT[i % 3]
                        o = bank[6][:, :].rearrange("p (t s d) -> p t s d", t=TT, s=4)
                        v = v_sb[:, g, :, h * HEAD:(h + 1) * HEAD]
                        pe.matmul(o[:, 0, slot, :], pt[:, 0, :], v[:, 0, :], start=True, stop=True)
                        pe.matmul(o[:, 1, slot, :], pt[:, 1, :], v[:, 0, :], start=True, stop=False)
                        pe.matmul(o[:, 1, slot, :], pt[:, 2, :], v[:, 1, :], start=False, stop=True).then_inc(
                            pv_ready, 1)
                    elif st == "turn":
                        n = turn_no[("turn", i, 0)]
                        wait_turned(pe, l, n - 2)
                        pe.wait_ge(group_ready, 4 * l + i + 1)
                        for w in range(2):
                            for t in range(TT):
                                mm = pe.transpose(bank[4 + n % 2][:, w * SEQ + t * P:w * SEQ + (t + 1) * P],
                                                  heads_out[:, i, t, w * P:(w + 1) * P], ident[:, :])
                        mm.then_inc(t_ready, 1)
                down = [bank[3 + ct // 2][:, (ct % 2) * SEQ:(ct % 2 + 1) * SEQ] for ct in range(KT)]

                def up(j, which):
                    o = 0 if j == 0 and which == 0 else 1 if j == 0 else 3 * j - 1 + which
                    if j > 0:
                        pe.wait_ge(conv_read, 2 * (STEPS * l + j - 1) + which + 1)
                    mm = unit_product(l, NI + NO + o, bank[which], KT * (norm + 1) if j == 0 and which == 0 else None)
                    mm.then_inc(unit_used, 1)
                    if which == 0 and mlp_ada(l, j):
                        ada(*mlp_ada(l, j))

                def down_product(j):
                    o = 3 * j + 4 if j < STEPS - 1 else 3 * STEPS - 1
                    n = unit_no(l, NI + NO + o)
                    pe.wait_ge(lo_done, n + 1)
                    pe.wait_ge(mlp_lo_ready, STEPS * l + j + 1)
                    wh = w_hi[n % RAW][:, :].rearrange("p (f n) -> p f n", f=2)
                    wl = w_lo[n % RAW][:, :].rearrange("p (f n) -> p f n", f=2)
                    for ct in range(KT):
                        for f in range(2):
                            s = slice(ct * P, (ct + 1) * P)
                            mm = product3(down[ct], (wh[:, f, s], wl[:, f, s]), (mlp_hi[:, f, :], mlp_lo[:, f, :]),
                                          j == 0 and f == 0 and ct % 2 == 0, j == STEPS - 1 and f == 1, True)
                        if j == STEPS - 1 and ct in (1, 3, 5):
                            mm.then_inc(down_ready, 1)
                    mm.then_inc(unit_used, 1)

                for j in range(STEPS):
                    up(j, 0)
                    up(j, 1)
                    if j > 0:
                        down_product(j - 1)
                        if mlp_ada(l, j):
                            ada_turn(*mlp_ada(l, j))
                down_product(STEPS - 1)
            mean_square(2 * DEPTH)
            for t in range(TT):
                for q in range(2):
                    pe.wait_ge(fin_ready, 4 * (q + 1))
                    for k in range(4):
                        mm = pe.transpose(bank[2 * t + q][:, k * P:(k + 1) * P], wide[:, 4 * q + k, t * P:(t + 1) * P],
                                          ident[:, :])
                    mm.then_inc(finT_ready, 1)

        @block.scalar
        def _(act):
            def split_hi(n, width=UC):
                wait_raw(act, n)
                if n >= RAW:
                    act.wait_ge(unit_used, n - RAW + 1)
                nc.scalar.activation(w_hi[n % RAW][:, 0:KT * width], raw[n % RAW][:, 0:KT * width],
                                     ACT.Copy).then_inc(hi_done, 1)

            def squares_of(n):
                for p in range(KT // 2):
                    act.wait_ge(x_new, 4 * n + p + 1)
                    nc.scalar.activation(wide[:, 2 * p:2 * p + 2, :], xT[:, 2 * p:2 * p + 2, :], ACT.Square).then_inc(
                        squares, 1)

            def take_rows(l, u):
                act.wait_ge(direct_used, direct_at[("ada", l, u + 1)] + 1)
                nc.scalar.activation(ada_row[:, :], bank[7][:, :], ACT.Copy).then_inc(ada_rows, 1)

            def root(n):
                act.wait_ge(ms_inv, n + 1)
                nc.scalar.activation(rstd[:, :], rstd[:, :], ACT.Sqrt).then_inc(rstd_ready, 1)

            def modulated(n, l, shift):
                for k in range(KT):
                    act.wait_ge(scaled, KT * n + k + 1)
                    nc.scalar.activation(act_hi[:, k, :], wide[:, k, :], ACT.Identity,
                                         bias=mod[:, l, shift + k:shift + k + 1]).then_inc(act_hi_ready, 1)

            act.wait_ge(setup_pe, 1)
            for l in range(DEPTH):
                for t in range(3):
                    ins = nc.scalar.activation(vec[:, l, P * t:P * t + VROWS[t]], bank[l][:, P * t:P * t + VROWS[t]],
                                               ACT.Copy)
                    ins.then_inc(vec_in, 1)
            act.wait_ge(vec_in, 3 * DEPTH)
            nc.scalar.activation(cond[:, :, :], vec[:, 0, V_C:V_C + KT].unsqueeze(2).to_broadcast([P, KT, 32]),
                                 ACT.Silu).then_inc(cond_ready, 1)
            act.wait_ge(lam_sem, 1)
            nc.scalar.activation(lam_ex[:, :], lam_ex[:, :], ACT.Exp).then_inc(lam_exp, 1)
            act.wait_ge(setup_pe, 6)
            nc.scalar.activation(diag[:, :], bank[6][0:3 * HEADS, 0:384], ACT.Copy, scale=-1.0).then_inc(diag_ready, 1)
            act.wait_ge(diag_ready, 1)
            act.dma_start(toeplitz, diag[:, :]).then_inc(toep_out, 16)
            act.wait_ge(toep_out, 16)
            act.dma_start(flipped, bass.AP(tensor=toeplitz.tensor, offset=0,
                                           ap=[[1, P], [384, 3 * HEADS], [1, SEQ]])).then_inc(bias_in, 16)
            squares_of(0)
            root(0)
            for u in range(0, 8, 2):
                take_rows(0, u)
            for i in range(RAW):
                split_hi(i, unit_width(i))

            for l in range(DEPTH):
                if l > 0:
                    squares_of(2 * l)
                    root(2 * l)
                modulated(2 * l, l, 0)
                if l > 0:
                    split_hi(unit_no(l, 2), unit_width(2))
                if l == 0:
                    for i, b in enumerate(FLIP_BANKS):
                        act.wait_ge(flip_ready, i + 1)
                        nc.scalar.activation(bias[:, 2 * i:2 * i + 2, :],
                                             bank[b][:, :].rearrange("p (h k) -> p h k", h=2), ACT.Copy).then_inc(
                            flip_read, 1)
                for e in schedules[l]:
                    st, i = e[0], e[1]
                    if st == "split":
                        split_hi(unit_no(l, i), unit_width(i))
                    elif st == "ada_turn":
                        take_rows(e[1], e[2])
                    elif st == "evac":
                        kind, g, width = IN_UNITS[i]
                        act.wait_ge(unit_used, unit_no(l, i) + 1)
                        src = bank[i % 2][:, 0:2 * width].rearrange("p (t n) -> p t n", t=2)
                        if kind == "tail":
                            nc.scalar.activation(tail[:, :, g:g + width], src, ACT.Copy).then_inc(in_read, 1)
                        elif kind == "v":
                            nc.scalar.activation(v_sb[:, g, :, :], src, ACT.Copy).then_inc(in_read, 1)
                        else:
                            nc.scalar.activation(qkT[:, g, "qk".index(kind), :, :], src, ACT.Copy,
                                                 scale=-SCALE[g] if kind == "q" else 1.0).then_inc(in_read, 1)
                    elif st == "latents_norm":
                        act.wait_ge(in_read, NI * l + 2)
                        nc.scalar.activation(ki_twice, tail[:, :, T_KIDX:T_KIDX + HEAD].unsqueeze(2).to_broadcast(
                            [P, TT, 2, HEAD]), ACT.Copy).then_inc(ki_ready, 1)
                    elif st == "latents":
                        act.wait_ge(latT_ready, l + 1)
                        nc.scalar.activation(latT[:, :, :], bank[6][:, :].rearrange("p (w t) -> p w t", w=2),
                                             ACT.Copy).then_inc(latT_read, 1)
                        nc.scalar.activation(kiT[:, :], bank[4][:, 0:SEQ], ACT.Copy).then_inc(latT_read, 1)
                    elif st == "latents_up":
                        two = lambda b: bank[b][:, :].rearrange("p (t n) -> p t n", t=2)
                        act.wait_ge(up_ready, 3 * l + 1)
                        nc.scalar.activation(qkT[:, 3, 0, :, :], two(2), ACT.Copy, scale=-SCALE[3]).then_inc(up_read, 1)
                        act.wait_ge(up_ready, 3 * l + 2)
                        nc.scalar.activation(qiT[:, :, :], two(3), ACT.Copy,
                                             scale=HEAD ** -0.5 * HEADS ** -0.5).then_inc(up_read, 1)
                        act.wait_ge(up_ready, 3 * l + 3)
                        nc.scalar.activation(qkT[:, 3, 1, :, :], two(4), ACT.Copy).then_inc(up_read, 1)
                        act.wait_ge(direct_used, direct_at[("dsa", l, 0)] + 1)
                        nc.scalar.activation(v_sb[:, 3, :, :], two(5), ACT.Copy).then_inc(up_read, 1)
                    elif st == "forget":
                        act.wait_ge(fz_ready, 2 * l + 2)
                        nc.scalar.activation(fz[:, 1, :], fz[:, 1, :], ACT.Exp, scale=-1.0).then_inc(fe_ready, 1)
                        nc.scalar.activation(gate_c, gate_c, ACT.Tanh,
                                             scale=0.5).then_inc(gate_exp, 1)
                        act.wait_ge(fe_ready, 2 * l + 1)
                        nc.scalar.activation(fz[:, 1, :], fz[:, 1, :], ACT.Ln, bias=one[:, :]).then_inc(fe_ready, 1)
                    elif st == "index":
                        for h in (i,):
                            act.wait_ge(s_ready, SC * l + h + 1)
                            if h >= 2:
                                act.wait_ge(idx_acc, 2 * (HEADS * l + h - 1))
                            nc.scalar.activation(relu[h % 2], bank[2 + h % 2][:, 0:384].rearrange("p (b k) -> p b k", b=3),
                                                 ACT.Relu).then_inc(idx_relu, 1)
                    elif st == "forget_up":
                        act.wait_ge(cum_ready, 2 * l + 1)
                        nc.scalar.activation(ncq[:, :], bank[7][:, 128:128 + TT * HEADS], ACT.Copy,
                                             scale=-1.0).then_inc(ncq_ready, 1)
                        act.wait_ge(ncq_ready, l + 1)
                        act.wait_ge(cum_ready, 2 * l + 2)
                        for h in range(HEADS):
                            ck = bank[4 + h // 2][:, (h % 2) * SEQ:(h % 2 + 1) * SEQ]
                            nc.scalar.activation(own_bias[:, h, 0, :], ck[:, 0:P], ACT.Identity, bias=ncq[:, h:h + 1])
                            nc.scalar.activation(own_bias[:, h, 1:3, :], ck.rearrange("p (b k) -> p b k", b=2),
                                                 ACT.Identity, bias=ncq[:, HEADS + h:HEADS + h + 1]).then_inc(ck_ready, 1)
                    elif st == "softmax":
                        m = NM * l + i
                        dst = soft[i % 3]
                        for t, part in ((0, dst[:, 0, :]), (1, dst[:, 1:3, :])):
                            act.wait_ge(low_ready, 2 * m + t + 1)
                            nc.scalar.activation(part, part, ACT.Exp, bias=low[:, i % 3, t:t + 1], scale=-1.0,
                                                 accum_out=rsum[:, (i // 4) % 2, t, i % 4:i % 4 + 1]).then_inc(
                                exp_ready, 1)
                    elif st == "probs":
                        n = turn_no[("probs", i)]
                        if n % 2 == 0:
                            act.wait_ge(t_ready, NT * l + n + 1)
                            if i >= 3:
                                act.wait_ge(pv_ready, NM * l + i - 2)
                            nc.scalar.activation(probT[i % 3], bank[4][:, 0:384].rearrange("p (b q) -> p b q", b=3),
                                                 ACT.Copy).then_inc(pt_act, 1)
                    elif st == "turn":
                        n = turn_no[("turn", i, 0)]
                        act.wait_ge(t_ready, NT * l + n + 1)
                        act.wait_ge(unit_used, unit_no(l, NI))
                        nc.scalar.activation(act_hi[:, 2 * i:2 * i + 2, :],
                                             bank[4 + n % 2][:, :].rearrange("p (w t) -> p w t", w=2),
                                             ACT.Copy).then_inc(turn_hi, 1)
                    elif st == "resid":
                        act.wait_ge(x_new, 4 * (2 * l + 1) + i + 1)
                        p = i
                        nc.scalar.activation(wide[:, 2 * p:2 * p + 2, :], xT[:, 2 * p:2 * p + 2, :],
                                             ACT.Square).then_inc(squares, 1)
                first = unit_no(l, NI + NO)
                root(2 * l + 1)
                modulated(2 * l + 1, l, 3 * KT)

                def last_tap(j, which):
                    o = which if j == 0 else 3 * j - 1 + which
                    act.wait_ge(unit_used, first + o + 1)
                    if j > 0:
                        act.wait_ge(prod_done, STEPS * l + j)
                    for f in range(2):
                        ch = which * FT + 2 * j + f
                        nc.scalar.activation(conv[:, which, f, :], bank[which][:, f * SEQ:(f + 1) * SEQ], ACT.Identity,
                                             scale=vec[:, l, V_W2 + ch:V_W2 + ch + 1],
                                             bias=vec[:, l, V_CB + ch:V_CB + ch + 1]).then_inc(tap_ready, 1)

                for j in range(STEPS):
                    if j < STEPS - 1:
                        split_hi(first + 3 * j + 2)
                    last_tap(j, 0)
                    if mlp_ada(l, j):
                        take_rows(*mlp_ada(l, j))
                    if j < STEPS - 1:
                        split_hi(first + 3 * j + 3)
                    last_tap(j, 1)
                    act.wait_ge(conv_read, 2 * (STEPS * l + j) + 1)
                    nc.scalar.activation(silu, conv[:, 0, :, :], ACT.Silu).then_inc(silu_ready, 1)
                    split_hi(first + (3 * j + 4 if j < STEPS - 1 else 3 * STEPS - 1))
                    act.wait_ge(prod_done, STEPS * l + j + 1)
                    if j > 0:
                        act.wait_ge(unit_used, first + 3 * j + 2)
                    nc.scalar.activation(mlp_hi[:, :, :], prod, ACT.Copy).then_inc(mlp_hi_ready, 1)
                if l + 1 < DEPTH:
                    for i in range(2):
                        split_hi(unit_no(l + 1, i), unit_width(i))
            squares_of(2 * DEPTH)
            root(2 * DEPTH)
            for t in range(TT):
                for q in range(2):
                    act.wait_ge(finT_ready, 2 * t + q + 1)
                    nc.scalar.activation(x_tok[:, t, 512 * q:512 * q + 512], bank[2 * t + q][:, :],
                                         ACT.Copy).then_inc(out_part, 1)

        @block.vector
        def _(dve):
            count = [0]

            def own(ins):
                count[0] += 1
                ins.then_inc(dve_own, 1)
                dve.wait_ge(dve_own, count[0])

            def split_lo(n, width=UC):
                dve.wait_ge(hi_done, n + 1)
                s = slice(0, KT * width)
                nc.vector.tensor_tensor(w_lo[n % RAW][:, s], raw[n % RAW][:, s], w_hi[n % RAW][:, s].bitcast(F32),
                                        ALU.subtract).then_inc(lo_done, 1)

            def inverse(n):
                dve.wait_ge(ms_ready, n + 1)
                own(nc.vector.tensor_scalar(rstd[:, :], bank[7][:, SEQ:2 * SEQ], EPS, None, ALU.add))
                nc.vector.reciprocal(rstd[:, :], rstd[:, :]).then_inc(ms_inv, 1)

            def modulated(n, l, which):
                dve.wait_ge(rstd_ready, n + 1)
                shift = 3 * KT * which

                def low_half(k):
                    dve.wait_ge(act_hi_ready, KT * n + k + 1)
                    nc.vector.scalar_tensor_tensor(act_lo[:, k, :], wide[:, k, :], mod[:, l, shift + k:shift + k + 1],
                                                   act_hi[:, k, :].bitcast(F32), ALU.add, ALU.subtract).then_inc(
                        act_lo_ready, 1)
                for k in range(KT):
                    nc.vector.scalar_tensor_tensor(wide[:, k, :], xT[:, k, :], amp[:, which, k:k + 1], rstd[:, :],
                                                   ALU.mult, ALU.mult).then_inc(scaled, 1)
                    if k >= 2:
                        low_half(k - 2)
                low_half(KT - 2)
                low_half(KT - 1)

            def residual(l, gate, p, src):
                for k in range(2):
                    kt = 2 * p + k
                    ins = nc.vector.scalar_tensor_tensor(xT[:, kt, :], src[:, k * SEQ:(k + 1) * SEQ],
                                                         mod[:, l, gate * KT + kt:gate * KT + kt + 1], xT[:, kt, :],
                                                         ALU.mult, ALU.add)
                ins.then_inc(x_new, 1)

            def take_mod(l, u):
                n = ada_no(l, u)
                dve.wait_ge(ada_turned, n + 1)
                s = slice(2 * u, 2 * u + 4)
                nc.vector.tensor_reduce(mod[:, l, s], bank[7][:, :].rearrange("p (c g r) -> p c g r", g=4, r=32)[:, :, :, 0],
                                        AX.X, ALU.add).then_inc(mod_ready, 1)
                dve.wait_ge(mod_ready, n + 1)
                nc.vector.tensor_tensor(mod[:, l, s], mod[:, l, s], vec[:, l, V_BADA + 2 * u:V_BADA + 2 * u + 4],
                                        ALU.add).then_inc(mod_done, 1)

            def amplitudes(l, which):
                v = V_N2 if which else V_N1
                own(nc.vector.scalar_tensor_tensor(amp[:, which, :], mod[:, l, KT * (3 * which + 1):KT * (3 * which + 2)],
                                                   1.0, vec[:, l, v:v + KT], ALU.add, ALU.mult))

            nc.vector.memset(tab[BUCKETS:BUCKETS + 1, :], -BIG).then_inc(tab_ready, 1)
            for p in range(KT // 2):
                dve.wait_ge(setup_pe, 2 + p)
                nc.vector.tensor_copy(xT[:, 2 * p:2 * p + 2, :],
                                      bank[2 + p][:, :].rearrange("p (k t) -> p k t", k=2)).then_inc(x_new, 1)
            dve.wait_ge(small_in, 16 * 5)
            own(nc.vector.tensor_tensor(lam_pr[:, :, :], lam_in[:, :, 0::2, :].rearrange("p l a d -> p (l a) d"),
                                        lam_in[:, :, 1::2, :].rearrange("p l a d -> p (l a) d"), ALU.mult))
            nc.vector.tensor_reduce(lam_ex[:, :], lam_pr[:, :, :], AX.X, ALU.add).then_inc(lam_sem, 1)
            for l in range(DEPTH):
                nc.vector.tensor_scalar(gain64[:, l, :], gain64[:, l, :], 1.0 - lam_init[l], None, ALU.mult)
            dve.wait_ge(lam_exp, 1)
            for l in range(DEPTH):
                own(nc.vector.tensor_tensor(nlam[:, l:l + 1], lam_ex[:, 2 * l + 1:2 * l + 2], lam_ex[:, 2 * l:2 * l + 1],
                                            ALU.subtract))
                own(nc.vector.tensor_scalar(nlam[:, l:l + 1], nlam[:, l:l + 1], -lam_init[l], None, ALU.add))
            inverse(0)
            dve.wait_ge(vec_in, 3 * DEPTH)
            for u in range(0, 8, 2):
                take_mod(0, u)
            dve.wait_ge(mod_done, 4)
            amplitudes(0, 0)

            for l in range(DEPTH):
                if l > 0:
                    inverse(2 * l)
                    dve.wait_ge(mod_done, 12 * (l + 1))
                    amplitudes(l, 0)
                modulated(2 * l, l, 0)
                for i in range(RAW) if l == 0 else (2,):
                    split_lo(unit_no(l, i), unit_width(i))
                for e in schedules[l]:
                    st, i = e[0], e[1]
                    if st == "split":
                        split_lo(unit_no(l, i), unit_width(i))
                    elif st == "ada_turn":
                        take_mod(e[1], e[2])
                    elif st == "latents_norm":
                        dve.wait_ge(in_read, NI * l + 2)
                        for t in range(TT):
                            for w in range(2):
                                src = tail[:, t, T_LAT + w * P:T_LAT + (w + 1) * P]
                                last = nc.vector.tensor_tensor_reduce(latn[:, t, w, :], src, src, 1.0, 0.0, ALU.mult,
                                                                      ALU.add, lat_ss[:, 2 * t + w:2 * t + w + 1])
                                if (t, w) != (1, 1):
                                    last.then_inc(dve_own, 1)
                                    count[0] += 1
                        own(last)
                        own(nc.vector.tensor_scalar(lat_ss[:, :], lat_ss[:, :], 1.0 / P, EPS, ALU.mult, ALU.add))
                        nc.vector.reciprocal(lat_ss[:, :], lat_ss[:, :]).then_inc(lat_inv, 1)
                        dve.wait_ge(lat_root, l + 1)
                        for t in range(TT):
                            for w in range(2):
                                last = nc.vector.tensor_scalar(latn[:, t, w, :], tail[:, t, T_LAT + w * P:T_LAT + (w + 1) * P],
                                                               lat_ss[:, 2 * t + w:2 * t + w + 1], None, ALU.mult)
                        last.then_inc(lat_ready, 1)
                    elif st == "forget":
                        dve.wait_ge(in_read, NI * l + 3)
                        own(nc.vector.tensor_tensor(fz[:, 0, :].rearrange("p (t h) -> p t h", t=TT), tail[:, :, 0:HEADS],
                                                    fb[:, l, :].unsqueeze(1).to_broadcast([P, TT, HEADS]), ALU.add))
                        nc.vector.scalar_tensor_tensor(fz[:, 1, :], fz[:, 0, :], -1.0, fz[:, 0, :], ALU.mult, ALU.max).then_inc(fz_ready, 1)
                        nc.vector.tensor_scalar(fz[:, 2, :], fz[:, 0, :], 0.0, None, ALU.min).then_inc(fz_ready, 1)
                        dve.wait_ge(fe_ready, 2 * l + 2)
                        nc.vector.tensor_tensor(fz[:, 3, :], fz[:, 2, :], fz[:, 1, :], ALU.subtract).then_inc(lf_ready, 1)
                        dve.wait_ge(gate_exp, l + 1)
                        own(nc.vector.tensor_scalar(gate_c, gate_c, 0.5, 0.5, ALU.mult, ALU.add))
                    elif st == "index":
                        for h in (i,):
                            dve.wait_ge(idx_relu, HEADS * l + h + 1)
                            if h:
                                dve.wait_ge(idx_acc, 2 * (HEADS * l + h))
                            for t, b in ((0, slice(0, 1)), (1, slice(1, 3))):
                                w = tail[:, t, T_WIDX + h:T_WIDX + h + 1]
                                if h == 0:
                                    nc.vector.tensor_scalar(score[:, b, :], relu[0][:, b, :], w, None,
                                                            ALU.mult).then_inc(idx_acc, 1)
                                else:
                                    nc.vector.scalar_tensor_tensor(score[:, b, :], relu[h % 2][:, b, :], w,
                                                                   score[:, b, :], ALU.mult, ALU.add).then_inc(idx_acc, 1)
                    elif st == "choose":
                        if i == 0:
                            dve.wait_ge(score_masked, l + 1)
                        for b in (slice(0, 1), slice(1, 3)):
                            part = score[:, b, :].rearrange("p b k -> p (b k)")
                            own(nc.vector.max(top8[:, :], part))
                            own(nc.vector.match_replace(part, top8[:, :], part, TAKEN))
                        if i == TOPK // 8 - 1:
                            nc.vector.tensor_scalar(score[:, :, :], score[:, :, :], TAKEN / 2, BIG, ALU.is_gt,
                                                    ALU.mult).then_inc(chosen, 1)
                    elif st == "softmax":
                        g, h, comp = MAPS[i]
                        dve.wait_ge(s_ready, SC * l + HEADS + i + 1)
                        if g < 2:
                            if l == 0 and i == 0:
                                dve.wait_ge(flip_read, 6)
                            b = bias[:, 4 * g + h, :]
                            biases = b[:, P:2 * P], b.rearrange("p (b k) -> p b k", b=2)
                        else:
                            dve.wait_ge(own_ready, 8 * l + 4 * (g - 2) + h + 1)
                            biases = own_bias[:, h, 0, :], own_bias[:, h, 1:3, :]
                        if i < 3:
                            dve.wait_ge(idx_acc, 2 * HEADS * (l + 1))
                        else:
                            dve.wait_ge(t_ready, NT * l + turn_no[("probs", i - 3)] + 1)
                        s = bank[2 + i % 2][:, 0:384].rearrange("p (b k) -> p b k", b=3)
                        nc.vector.tensor_tensor_reduce(soft[i % 3][:, 0, :], s[:, 0, :], biases[0], 1.0, 3e38, ALU.add,
                                                       ALU.min, low[:, i % 3, 0:1]).then_inc(low_ready, 1)
                        nc.vector.tensor_tensor_reduce(soft[i % 3][:, 1:3, :], s[:, 1:3, :], biases[1], 1.0, 3e38,
                                                       ALU.add, ALU.min, low[:, i % 3, 1:2]).then_inc(low_ready, 1)
                    elif st == "probs":
                        n = turn_no[("probs", i)]
                        if n % 2:
                            dve.wait_ge(t_ready, NT * l + n + 1)
                            if i >= 3:
                                dve.wait_ge(pv_ready, NM * l + i - 2)
                            nc.vector.tensor_copy(probT[i % 3], bank[5][:, 0:384].rearrange("p (b q) -> p b q", b=3)).then_inc(
                                pt_dve, 1)
                    elif st == "heads":
                        own(nc.vector.reciprocal(rinv[:, :, :], rsum[:, i % 2, :, :]))
                        dve.wait_ge(pv_ready, NM * l + 4 * i + 4)
                        o = bank[6][:, :].rearrange("p (t s d) -> p t s d", t=TT, s=4)
                        r = rinv[:, :, :].unsqueeze(3).to_broadcast([P, TT, 4, HEAD])
                        g = max(i - 1, 0)
                        dst = pair[:, :, :, :] if i < 2 else heads_out[:, g, :, :].rearrange("p t (s d) -> p t s d", s=4)
                        ins = nc.vector.tensor_tensor(dst, o, r, ALU.mult)
                        ins.then_inc(o_read, 1)
                        if i < 2:
                            dve.wait_ge(o_read, 5 * l + i + 1)
                            for t in range(TT):
                                last = nc.vector.scalar_tensor_tensor(
                                    heads_out[:, 0, t, i * P:(i + 1) * P].rearrange("p (h d) -> p h d", h=2),
                                    pair[:, t, 1::2, :], nlam[:, l:l + 1], pair[:, t, 0::2, :], ALU.mult, ALU.add)
                                own(last)
                        elif g == 2:
                            dve.wait_ge(o_read, 5 * l + i + 1)
                            nc.vector.tensor_tensor(heads_out[:, 2, :, :], heads_out[:, 2, :, :], gate_c,
                                                    ALU.mult).then_inc(group_ready, 1)
                        else:
                            dve.wait_ge(o_read, 5 * l + i + 1)
                            nc.vector.tensor_copy(rinv[:, 0, 0:1], rinv[:, 0, 0:1]).then_inc(group_ready, 1)
                    elif st == "subln":
                        a_heads = heads_out[:, 0, :, :].rearrange("p t (h d) -> p (t h) d", h=HEADS)
                        sq = pair[:, :, :, :].rearrange("p t s d -> p (t s) d")
                        own(nc.vector.tensor_tensor(sq, a_heads, a_heads, ALU.mult))
                        own(nc.vector.tensor_reduce(nrm[:, :], sq, AX.X, ALU.add))
                        own(nc.vector.tensor_scalar(nrm[:, :], nrm[:, :], 1.0 / HEAD, EPS, ALU.mult, ALU.add))
                        nc.vector.reciprocal(nrm[:, :], nrm[:, :]).then_inc(sub_ss, 1)
                    elif st == "subln_end":
                        dve.wait_ge(sub_root, l + 1)
                        a_heads = heads_out[:, 0, :, :].rearrange("p t (h d) -> p (t h) d", h=HEADS)
                        own(nc.vector.tensor_tensor(a_heads, a_heads, nrm[:, :].unsqueeze(2).to_broadcast(
                            [P, TT * HEADS, HEAD]), ALU.mult))
                        nc.vector.tensor_tensor(a_heads, a_heads, gain64[:, l, :].unsqueeze(1).to_broadcast(
                            [P, TT * HEADS, HEAD]), ALU.mult).then_inc(group_ready, 1)
                    elif st == "turn":
                        n = turn_no[("turn", i, 0)]
                        dve.wait_ge(turn_hi, 4 * l + i + 1)
                        nc.vector.tensor_tensor(act_lo[:, 2 * i:2 * i + 2, :],
                                                bank[4 + n % 2][:, :].rearrange("p (w t) -> p w t", w=2),
                                                act_hi[:, 2 * i:2 * i + 2, :].bitcast(F32),
                                                ALU.subtract).then_inc(turn_lo, 1)
                    elif st == "resid":
                        if i == 0:
                            dve.wait_ge(mod_done, 12 * (l + 1))
                            amplitudes(l, 1)
                        dve.wait_ge(unit_used, unit_no(l, NI + i) + 1)
                        residual(l, 2, i, unit_bank(NI + i))
                first = unit_no(l, NI + NO)
                inverse(2 * l + 1)
                modulated(2 * l + 1, l, 1)

                def taps(j, which):
                    dve.wait_ge(tap_ready, 4 * (STEPS * l + j) + 2 * which + 2)
                    for tap, lag in ((V_W1, 1), (V_W0, 2)):
                        for f in range(2):
                            ch = which * FT + 2 * j + f
                            dst = conv[:, which, f, lag:SEQ]
                            ins = nc.vector.scalar_tensor_tensor(
                                dst, bank[which][:, f * SEQ:(f + 1) * SEQ - lag], vec[:, l, tap + ch:tap + ch + 1], dst,
                                ALU.mult, ALU.add)
                            if lag == 1:
                                ins.then_inc(dve_own, 1)
                                count[0] += 1
                        if lag == 1:
                            dve.wait_ge(dve_own, count[0])
                    ins.then_inc(conv_read, 1)

                for j in range(STEPS):
                    if j < STEPS - 1:
                        split_lo(first + 3 * j + 2)
                    taps(j, 0)
                    if j < STEPS - 1:
                        split_lo(first + 3 * j + 3)
                    taps(j, 1)
                    if mlp_ada(l, j):
                        take_mod(*mlp_ada(l, j))
                    dve.wait_ge(silu_ready, STEPS * l + j + 1)
                    dve.wait_ge(conv_read, 2 * (STEPS * l + j) + 2)
                    nc.vector.tensor_tensor(prod, silu, conv[:, 1, :, :], ALU.mult).then_inc(prod_done, 1)
                    split_lo(first + (3 * j + 4 if j < STEPS - 1 else 3 * STEPS - 1))
                    dve.wait_ge(mlp_hi_ready, STEPS * l + j + 1)
                    nc.vector.tensor_tensor(mlp_lo[:, :, :], prod, mlp_hi[:, :, :].bitcast(F32),
                                            ALU.subtract).then_inc(mlp_lo_ready, 1)
                if l + 1 < DEPTH:
                    for i in range(2):
                        split_lo(unit_no(l + 1, i), unit_width(i))
                for p in range(KT // 2):
                    if p < 3:
                        dve.wait_ge(down_ready, 3 * l + p + 1)
                    else:
                        dve.wait_ge(unit_used, unit_no(l + 1, 0))
                    residual(l, 5, p, bank[3 + p])
            inverse(2 * DEPTH)
            dve.wait_ge(rstd_ready, 2 * DEPTH + 1)
            for k in range(KT):
                nc.vector.scalar_tensor_tensor(wide[:, k, :], xT[:, k, :], vec[:, 0, V_FIN + k:V_FIN + k + 1],
                                               rstd[:, :], ALU.mult, ALU.mult).then_inc(fin_ready, 1)


def kernel(**inputs):
    import concourse.bacc as bacc
    from concourse.bass_utils import run_bass_kernel_spmd

    names = ["x", "c", "w_ada", "b_ada", "norm1_gain", "w_in", "f_bias", "diff_lambda", "diff_subln_gain",
             "w_dq_up", "w_didx_q", "w_dkv_up", "w_out", "t5_table", "norm2_gain", "w_ffn_up", "ffn_conv_w",
             "ffn_conv_b", "w_ffn_down", "final_gain"]
    nc = bacc.Bacc("TRN2", target_bir_lowering=False, num_devices=1)
    arrays = {f"in_{n}": np.ascontiguousarray(inputs[n]) for n in names}
    arrays["in_buckets"] = bucket_rows()
    args = [nc.dram_tensor(n, a.shape, mybir.dt.from_np(a.dtype), kind="ExternalInput").ap() for n, a in arrays.items()]
    args.append(nc.dram_tensor("out_0", (1, SEQ, D_MODEL), F32, kind="ExternalOutput").ap())
    trunk(nc, *args)
    r = run_bass_kernel_spmd(nc, [arrays], core_ids=[0])
    return r.results[0]["out_0"]
```

```python
import math
from contextlib import ExitStack

import concourse.bass as bass
import numpy as np
from concourse import mybir

F32 = mybir.dt.float32
F32R = mybir.dt.float32r
ACT = mybir.ActivationFunctionType
ALU = mybir.AluOpType
AX = mybir.AxisListType

P = 128
EPS = 1e-6
BIG = 1e30
TAKEN = -3e38

D_MODEL, SEQ, DEPTH, D_FF = 1024, 256, 2, 2816
HEAD, HALF, HEADS = 64, 32, 4
GROUP = HEADS * HEAD
KT = D_MODEL // P
TT = SEQ // P
UC = 256
FT = D_FF // P
STEPS = FT // 2
BUCKETS, T5_MAX = 32, 128
TOPK = min(256, SEQ // 4)

C_FC = 9 * GROUP
IN_COLS = C_FC + HEADS + GROUP + 2 * P + HEAD + HEADS
TAIL = IN_COLS - C_FC
T_GC, T_LAT = HEADS, HEADS + GROUP
T_KIDX = T_LAT + 2 * P
T_WIDX = T_KIDX + HEAD

IN_UNITS = [("tail", 512, TAIL - 512), ("tail", 256, 256), ("tail", 0, 256)]
NARROW = TAIL - 512
IN_UNITS += [(what, g, UC) for g in range(3) for what in "qkv"]
NI = len(IN_UNITS)
NO = D_MODEL // UC
PER_LAYER = NI + NO + 3 * STEPS
RAW = 3

MAPS = [(0, h, c) for h in range(4) for c in range(2)] + [(g, h, 0) for g in (1, 2, 3) for h in range(4)]
NM = len(MAPS)
SCALE = [HALF ** -0.5, HEAD ** -0.5, HEAD ** -0.5, HEAD ** -0.5]

V_BADA, V_N1, V_N2, V_CB = 0, 48, 56, 64
V_W0, V_W1 = 128, 128 + 2 * FT
V_W2, V_FIN = 256, 256 + 2 * FT
VROWS = [64 + 2 * FT, 4 * FT, 2 * FT + KT]


def bucket_rows():
    y = np.arange(384)
    dist = SEQ - 1 - y
    exact = BUCKETS // 2
    d = np.maximum(dist, 0)
    ratio = np.maximum(d, 1).astype(np.float32) / np.float32(exact)
    large = exact + (np.log(ratio) / np.float32(math.log(T5_MAX / exact)) * np.float32(BUCKETS - exact)).astype(np.int32)
    bucket = np.where(d < exact, d, np.minimum(large, BUCKETS - 1))
    rows = np.zeros((BUCKETS + 1, 384), np.float32)
    rows[bucket, y] = dist >= 0
    rows[BUCKETS] = dist < 0
    return rows


NA = 6 * D_MODEL // UC
SETUP_ADA = NA // 3


MLP_ADA = NA - 4


def mlp_ada(l, j):
    first = 2 * j
    return [("ada", l + 1, u) for u in range(first, first + 2)] if l + 1 < DEPTH and first < MLP_ADA else []


def direct_units():
    units = [("ada", 0, u) for u in range(SETUP_ADA)]
    for l in range(DEPTH):
        for e in layer_schedule(l):
            if e[0] == "latents":
                units.append(("dsa", l, 0))
            elif e[0] == "ada":
                units.append(e)
            elif e[0] == "pair":
                units += [("ada", e[1], e[2]), ("ada", e[1], e[2] + 1)]
        for j in range(STEPS):
            units += mlp_ada(l, j)
    return units


def layer_schedule(l):
    s = []
    pairs = [("pair", 0, u) for u in (SETUP_ADA, SETUP_ADA + 2)] if l == 0 else []
    late = [("ada", l, u) for u in range(MLP_ADA if l else SETUP_ADA + 4, NA)]
    summed = []
    choose = [("choose", r) for r in range(TOPK // 8)]
    scored, turned = [], []
    at = [0]

    def next_sum():
        if len(summed) == 2 or not late:
            s.extend(("column",) + e[1:] for e in summed[:1])
            del summed[:1]
        if late:
            summed.append(late.pop(0))
            s.append(summed[-1])

    def values(ms):
        for m in ms:
            s.append(("values", m))
            if m % 4 == 3:
                s.append(("heads", m // 4))
            if m == 7:
                s.append(("subln", 0))
            if m == 9:
                s.append(("subln_end", 0))

    def maps(n):
        nonlocal scored, turned
        for m in scored:
            s.append(("probs", m))
        values(turned)
        turned = scored
        scored = list(range(at[0], min(at[0] + n, NM)))
        at[0] += len(scored)
        if scored:
            s.append(("scores", scored[0]))
        for m in scored:
            s.append(("softmax", m))

    for k in range(KT):
        s += [("unit", 0, k, k + 1), ("unit", 1, k, k + 1)]
    s += [("evac", 0), ("evac", 1), ("narrow", 0)]
    s += pairs[0:1]
    s += [("flip", 0)] if l == 0 else []
    s += [("split_hi", 3), ("latents_norm", 0), ("split_lo", 3), ("unit", 2, 0, 4)]
    s += [("pair_turn",) + e[1:] for e in pairs[0:1]]
    s += pairs[1:2]
    s += [("unit", 2, 4, KT), ("evac", 2), ("latents", 0)]
    s += [("pair_turn",) + e[1:] for e in pairs[1:2]]
    s += [("split_hi", 4), ("split_lo", 4)]
    s += [("split_hi", 5), ("split_lo", 5), ("forget", 0)]
    for i in range(3, NI):
        s += [("unit", i, 0, KT), ("evac", i)]
        if i == 3:
            s.append(("latents_up", 0))
        if i == 4:
            s += [("forget_up", 0), ("index", 0), ("index", 1)]
        if i == 5:
            s += [("index", 2), ("index", 3)]
        s.append(("split_hi", i + RAW))
        if i >= 5:
            maps(2)
        if l == 0 or i >= 5:
            next_sum()
        if i != NI - 1:
            s.append(("split_lo", i + RAW))
        if i >= 5:
            s += choose[:2 if i in (6, 7) else 1]
            choose = choose[2 if i in (6, 7) else 1:]
    s.append(("turn", 0))
    maps(2)
    s.append(("split_lo", NI + 2))
    s.append(("unit", NI, 0, 2))
    next_sum()
    s.append(("turn", 1))
    maps(2)
    s += [("unit", NI, 2, 4), ("unit", NI + 1, 0, 4)]
    next_sum()
    maps(2)
    s += [("turn", 2), ("unit", NI + 2, 0, 4)]
    next_sum()
    maps(0)
    s += [("unit", NI, 4, 6)]
    maps(0)
    s += [("unit", NI + 1, 4, 6), ("turn", 3)]
    next_sum()
    next_sum()
    assert not late and not summed
    for i in range(NI, NI + NO):
        s.append(("unit", i, {NI: 6, NI + 1: 6, NI + 2: 4}.get(i, 0), KT))
        if i + RAW < NI + NO + 2:
            s.append(("split_hi", i + RAW))
        s.append(("resid", i - NI))
        if i + RAW < NI + NO + 2:
            s.append(("split_lo", i + RAW))
    s.append(("mean", 0))
    return s


def trunk(nc, x, c, w_ada, b_ada, norm1_gain, w_in, f_bias, diff_lambda, diff_subln_gain, w_dq_up,
          w_didx_q, w_dkv_up, w_out, t5_table, norm2_gain, w_ffn_up, ffn_conv_w, ffn_conv_b,
          w_ffn_down, final_gain, buckets, out):
    DIRECT = direct_units()
    DSLOTS = 3
    direct_at = {u: a for a, u in enumerate(DIRECT)}
    schedules = [layer_schedule(l) for l in range(DEPTH)]
    lam_init = [0.8 - 0.6 * math.exp(-0.3 * l) for l in range(DEPTH)]

    with ExitStack() as ctx:
        def sb(name, shape, dt=F32):
            return ctx.enter_context(nc.sbuf_tensor(name, shape, dt))

        def sem(name):
            return ctx.enter_context(nc.semaphore(name))

        bank = [ctx.enter_context(nc.psum_tensor(f"bank{i}", [P, 512], F32)) for i in range(8)]
        raw = [sb(f"raw{i}", [P, KT * UC]) for i in range(RAW)]
        w_hi = [sb(f"w_hi{i}", [P, KT * UC], F32R) for i in range(RAW)]
        w_lo = [sb(f"w_lo{i}", [P, KT * UC], F32R) for i in range(RAW)]
        direct = [sb(f"direct{i}", [P, KT * UC]) for i in range(DSLOTS)]
        xT = sb("xT", [P, KT, SEQ])
        act_hi = sb("act_hi", [P, KT, SEQ], F32R)
        act_lo = sb("act_lo", [P, KT, SEQ], F32R)
        mlp_hi = sb("mlp_hi", [P, 2, SEQ], F32R)
        mlp_lo = sb("mlp_lo", [P, 2, SEQ], F32R)
        qkT = sb("qkT", [P, 4, 2, 2, SEQ])
        qiT = sb("qiT", [P, 2, SEQ])
        kiT = sb("kiT", [P, SEQ])
        v_sb = sb("v_sb", [P, 4, TT, GROUP])
        tail = sb("tail", [P, TT, TAIL])
        bias = sb("bias", [P, 3 * HEADS, SEQ])
        own_bias = sb("own_bias", [P, HEADS, 3, P])
        work = sb("work", [P, 6 * 384])
        heads_out = sb("heads_out", [P, 4, TT, GROUP])
        vec = sb("vec", [P, DEPTH, 384])
        mod = sb("mod", [P, DEPTH, 48])
        amp = sb("amp", [P, 2, KT])
        cond = sb("cond", [P, KT, 32])
        ada_row = sb("ada_row", [P, 512])
        ident = sb("ident", [P, P])
        reverse = sb("reverse", [P, P])
        mean_w = sb("mean_w", [P, 1])
        ones = sb("ones", [P, P])
        minus_half = sb("minus_half", [P, TT])
        root = sb("root", [P, TT])
        diagonal = sb("diagonal", [P, TT, P])
        upto = sb("upto", [P, SEQ])
        one = sb("one", [P, 1])
        lam_in = sb("lam_in", [P, DEPTH, 4, HALF])
        lam_pr = sb("lam_pr", [P, DEPTH * 2, HALF])
        lam_ex = sb("lam_ex", [P, DEPTH * 2])
        nlam = sb("nlam", [P, DEPTH])
        gain64 = sb("gain64", [P, DEPTH, HEAD])
        fb = sb("fb", [P, DEPTH, HEADS])
        tab = sb("tab", [BUCKETS + 1, 3 * HEADS])
        lat_ss = sb("lat_ss", [P, 4])
        fz = sb("fz", [P, 4, TT * HEADS])
        ncq = sb("ncq", [P, TT * HEADS])
        low = sb("low", [P, 3, 2])
        rsum = sb("rsum", [P, 2, TT, 4])
        rinv = sb("rinv", [P, TT, 4])
        top8 = sb("top8", [P, 8])
        c_rows = sb("c_rows", [KT, P])
        pair = sb("pair", [P, TT, 4, HEAD])
        half = sb("half", [P, 8])
        nrm = sb("nrm", [P, TT * HEADS])
        score = sb("score", [P, 3, P])
        toeplitz = nc.dram_tensor("toeplitz", (3 * HEADS, 384), F32, kind="Internal").ap()

        soft = [work[:, 384 * i:384 * i + 384].rearrange("p (b k) -> p b k", b=3) for i in range(3)]
        probT = [work[:, 1152 + 384 * i:1536 + 384 * i].rearrange("p (b q) -> p b q", b=3) for i in range(3)]
        relu = [work[:, 384 * i:384 * i + 384].rearrange("p (b k) -> p b k", b=3) for i in range(2)]
        latT = work[:, 0:512].rearrange("p (w t) -> p w t", w=2)
        narrow = work[0:NARROW, 768:768 + SEQ]
        ki_twice = work[:, 1664:1920].rearrange("p (t a d) -> p t a d", t=TT, a=2)
        latn = work[:, 1152:1664].rearrange("p (t w d) -> p t w d", t=TT, w=2)
        lf_wide = work[:, 1024:2048].rearrange("p (c q) -> p c q", c=TT * HEADS)
        conv = work[:, 0:1024].rearrange("p (w f t) -> p w f t", w=2, f=2)
        silu = work[:, 1024:1536].rearrange("p (f t) -> p f t", f=2)
        prod = work[:, 1536:2048].rearrange("p (f t) -> p f t", f=2)
        wide = work[:, 0:KT * SEQ].rearrange("p (k t) -> p k t", k=KT)
        buck = own_bias[0:BUCKETS + 1, 0, :, :].rearrange("p b k -> p (b k)")
        diag = own_bias[0:3 * HEADS, 1, :, :].rearrange("p b k -> p (b k)")
        gate_c = tail[:, :, T_GC:T_GC + GROUP]
        flipped = qkT[:, :, :, :, :].rearrange("p g w h t -> p (g w h t)")[:, 0:3 * HEADS * SEQ].rearrange(
            "p (h k) -> p h k", k=SEQ)
        FLIP_BANKS = [2, 3, 4, 5, 6, 2]
        x_tok = heads_out[:, :, :, :].rearrange("p g t n -> p (g t n)").rearrange("p (t n) -> p t n", t=TT)
        rows_in = v_sb[:, 0:3, :, :].rearrange("p g t n -> p (g t n)")[:, 0:DEPTH * 384].rearrange(
            "p (l r n) -> p l r n", l=DEPTH, r=3)

        rstd = bank[7][:, SEQ:2 * SEQ]

        final = v_sb[:, :, :, :].rearrange("p g t n -> p (g t n)").rearrange("p (k t) -> p k t", k=KT)

        raw_in = [sem(f"raw_in{i}") for i in range(RAW)]
        direct_in = [sem(f"direct_in{i}") for i in range(DSLOTS)]
        small_in = sem("small_in")
        x_in = sem("x_in")
        rows_sem = [sem("rows_early"), sem("rows_late")]
        consts = sem("consts")
        diag_ready = sem("diag_ready")
        toep_out = sem("toep_out")
        bias_in = sem("bias_in")
        flip_ready = sem("flip_ready")
        flip_read = sem("flip_read")
        c_in = sem("c_in")
        c_turned = sem("c_turned")
        table_in = sem("table_in")
        diag_up = sem("diag_up")
        vec_turned = sem("vec_turned")
        x_turned = sem("x_turned")
        cond_ready = sem("cond_ready")
        lam_sem = sem("lam_sem")
        tab_ready = sem("tab_ready")
        lam_exp = sem("lam_exp")
        vec_in = sem("vec_in")
        tap_ready = sem("tap_ready")
        out_part = [sem(f"out_part{t}") for t in range(TT)]
        hi_done = sem("hi_done")
        lo_done = sem("lo_done")
        unit_used = sem("unit_used")
        direct_used = sem("direct_used")
        ada_summed = sem("ada_summed")
        ada_scaled = sem("ada_scaled")
        pool_scaled = sem("pool_scaled")
        ada_added = sem("ada_added")
        mod_ready = sem("mod_ready")
        mod_done = sem("mod_done")
        ada_rows = sem("ada_rows")
        ada_turned = sem("ada_turned")
        x_new = sem("x_new")
        squares = sem("squares")
        pair_summed = sem("pair_summed")
        squares_summed = sem("squares_summed")
        ms_ready = sem("ms_ready")
        ms_inv = sem("ms_inv")
        rooted = sem("rooted")
        diagonal_ready = sem("diagonal_ready")
        rstd_ready = sem("rstd_ready")
        scaled = sem("scaled")
        act_hi_ready = sem("act_hi_ready")
        act_lo_ready = sem("act_lo_ready")
        in_read = sem("in_read")
        narrow_turned = sem("narrow_turned")
        narrow_read = sem("narrow_read")
        lat_root = sem("lat_root")
        lat_ready = sem("lat_ready")
        latT_ready = sem("latT_ready")
        latT_read = sem("latT_read")
        up_read = sem("up_read")
        s_ready = sem("s_ready")
        idx_relu = sem("idx_relu")
        score_masked = sem("score_masked")
        chosen = sem("chosen")
        fz_ready = sem("fz_ready")
        fe_ready = sem("fe_ready")
        lf_ready = sem("lf_ready")
        lfw_ready = sem("lfw_ready")
        cum_ready = sem("cum_ready")
        ncq_ready = sem("ncq_ready")
        ck_ready = sem("ck_ready")
        own_ready = sem("own_ready")
        low_ready = sem("low_ready")
        exp_ready = sem("exp_ready")
        t_ready = sem("t_ready")
        pt_act = sem("pt_act")
        pt_dve = sem("pt_dve")
        pv_ready = sem("pv_ready")
        o_read = sem("o_read")
        group_ready = sem("group_ready")
        idx_acc = sem("idx_acc")
        lat_inv = sem("lat_inv")
        ki_ready = sem("ki_ready")
        up_ready = sem("up_ready")
        gate_exp = sem("gate_exp")
        finT_ready = sem("finT_ready")
        down_ready = sem("down_ready")
        sub_done = sem("sub_done")
        sub_ss = sem("sub_ss")
        sub_root = sem("sub_root")
        turn_hi = sem("turn_hi")
        turn_lo = sem("turn_lo")
        conv_read = sem("conv_read")
        silu_ready = sem("silu_ready")
        prod_done = sem("prod_done")
        mlp_hi_ready = sem("mlp_hi_ready")
        mlp_lo_ready = sem("mlp_lo_ready")
        fin_ready = sem("fin_ready")
        stored = sem("stored")
        dve_own = sem("dve_own")

        def unit_no(l, i):
            return PER_LAYER * l + i

        def vector_rows(l, t):
            return 2 * FT if (l, t) == (1, 2) else VROWS[t]

        def wait_raw(eng, n):
            eng.wait_ge(raw_in[n % RAW], 16 * (n // RAW + 1))

        def wait_used(eng, a):
            if DIRECT[a][1:] in sum_no and DIRECT[a][0] == "ada":
                eng.wait_ge(ada_summed, sum_no[DIRECT[a][1:]] + 1)
            else:
                eng.wait_ge(direct_used, product_no[DIRECT[a]] + 1)

        def direct_value(a):
            return 16 * sum(3 if DIRECT[b][0] == "dsa" else 1 for b in range(a % DSLOTS, a + 1, DSLOTS))

        def unit_bank(i):
            return bank[i % 2 if i < NI else i - NI]

        def pair_bank(l, u):
            return bank[(6, 1)[u // 2 % 2]] if l == 0 and u < SETUP_ADA else bank[7]

        def ada_no(l, u):
            return NA * l + u

        def unit_width(i):
            return IN_UNITS[i][2] if i < NI else UC

        pair_no, sum_no = {}, {}
        for u in range(0, SETUP_ADA, 2):
            pair_no[(0, u)] = len(pair_no)
        for l in range(DEPTH):
            for e in schedules[l] + [e for j in range(STEPS) for e in mlp_ada(l, j)]:
                if e[0] == "pair":
                    pair_no[e[1:]] = len(pair_no)
                elif e[0] == "ada":
                    sum_no[e[1:]] = len(sum_no)
        scaled_no = {k: n for n, k in enumerate(k for k in sum_no if k[1] % 2 and not (k[0] == 0 and k[1] > NA - 4))}
        multiplied_no = {k: n for n, k in enumerate(k for k in sum_no if k not in scaled_no)}
        product_no = {}
        for e in DIRECT:
            if e[0] == "dsa" or e[1:] not in sum_no:
                product_no[e] = len(product_no)

        SC = HEADS + NM
        turn_order = []
        for st, i in [e[:2] for e in schedules[0]]:
            if st == "probs":
                turn_order.append(("probs", i))
            elif st == "turn":
                turn_order.append(("turn", i))
        NT = len(turn_order)
        turn_no = {k: n for n, k in enumerate(turn_order)}
        act_frees, dve_frees, freed_by = 0, 0, []
        for n, k in enumerate(turn_order):
            if k[0] == "turn":
                freed_by.append(("lo", k[1]))
            elif n % 2 == 0:
                act_frees += 1
                freed_by.append(("act", act_frees))
            else:
                dve_frees += 1
                freed_by.append(("dve", dve_frees))

        def wait_turned(eng, l, n, slack=0):
            kind, k = freed_by[n]
            if kind == "act":
                eng.wait_ge(pt_act, act_frees * l + k)
            elif kind == "dve":
                eng.wait_ge(pt_dve, dve_frees * l + k)
            else:
                eng.wait_ge(turn_lo, 4 * l + k + 1)

        block = ctx.enter_context(nc.Block())

        @block.sync
        def _(sp):
            def rows(t, first, src, n):
                sp.dma_start(rows_in[first:first + n, :, t, :], src.rearrange("l (r n) -> r l n", n=P)).then_inc(
                    rows_sem[min(t, 1)], 16)

            def load_direct(a):
                kind, l, u = DIRECT[a]
                if a >= DSLOTS:
                    wait_used(sp, a - DSLOTS)
                slot = direct[a % DSLOTS]
                if kind == "ada":
                    sp.dma_start(slot[:, :].rearrange("p (k n) -> p k n", k=KT),
                                 w_ada[l].rearrange("(k p) n -> p k n", p=P)[:, :, u * UC:(u + 1) * UC]).then_inc(
                        direct_in[a % DSLOTS], 16)
                else:
                    sp.dma_start(slot[:, 0:256], w_dq_up[l]).then_inc(direct_in[a % DSLOTS], 16)
                    sp.dma_start(slot[:, 256:512], w_didx_q[l]).then_inc(direct_in[a % DSLOTS], 16)
                    sp.dma_start(slot[:, 512:1024], w_dkv_up[l]).then_inc(direct_in[a % DSLOTS], 16)

            def load_unit(l, i):
                n = unit_no(l, i)
                if n >= RAW:
                    sp.wait_ge(lo_done, n - RAW + 1)
                dst, j = raw[n % RAW], i - NI - NO
                if i < NI:
                    kind, g, width = IN_UNITS[i]
                    c0 = C_FC + g if kind == "tail" else 3 * GROUP * g + GROUP * "qkv".index(kind)
                    src = w_in[l].rearrange("(k p) n -> p k n", p=P)[:, :, c0:c0 + width]
                    dst = dst[:, 0:KT * width].rearrange("p (k n) -> p k n", k=KT)
                else:
                    src = w_out[l].rearrange("(k p) n -> p k n", p=P)[:, :, (i - NI) * UC:(i - NI + 1) * UC]
                    dst = dst[:, :].rearrange("p (k n) -> p k n", k=KT)
                sp.dma_start(dst, src).then_inc(raw_in[n % RAW], 16)

            def load_mlp(l, o, what, j):
                n = unit_no(l, NI + NO + o)
                sp.wait_ge(lo_done, n - RAW + 1)
                dst = raw[n % RAW]
                if what == "down":
                    src = w_ffn_down[l, j * UC:(j + 1) * UC, :].rearrange("(f p) n -> p f n", p=P)
                    dst = dst[:, :].rearrange("p (f n) -> p f n", f=2)
                else:
                    c0 = j * UC + (D_FF if what == "value" else 0)
                    src = w_ffn_up[l].rearrange("(k p) n -> p k n", p=P)[:, :, c0:c0 + UC]
                    dst = dst[:, :].rearrange("p (k n) -> p k n", k=KT)
                sp.dma_start(dst, src).then_inc(raw_in[n % RAW], 16)

            sp.dma_start(c_rows[:, :], c[0].rearrange("(r n) -> r n", n=P)).then_inc(c_in, 16)
            load_direct(0)
            sp.dma_start(tab[0:BUCKETS, :], t5_table).then_inc(table_in, 16)
            sp.dma_start(buck[:, :], buckets).then_inc(table_in, 16)
            load_direct(1)
            rows(0, V_BADA, b_ada, 48)
            rows(0, V_N1, norm1_gain, KT)
            rows(0, V_N2, norm2_gain, KT)
            rows(0, V_CB, ffn_conv_b, 2 * FT)
            sp.dma_start(x_tok, x[0].rearrange("(t p) n -> p t n", p=P)).then_inc(x_in, 16)
            load_direct(2)
            rows(1, 0, ffn_conv_w[:, 0], 2 * FT)
            rows(1, 2 * FT, ffn_conv_w[:, 1], 2 * FT)
            rows(2, 0, ffn_conv_w[:, 2], 2 * FT)
            sp.dma_start(rows_in[2 * FT:2 * FT + KT, 0, 2, :], final_gain.rearrange("(r n) -> r n", n=P)).then_inc(
                rows_sem[1], 16)
            sp.dma_start(lam_in[:, :, :, :], diff_lambda.rearrange("l a d -> (l a d)").partition_broadcast(P)).then_inc(
                small_in, 16)
            sp.dma_start(gain64[:, :, :], diff_subln_gain.rearrange("l d -> (l d)").partition_broadcast(P)).then_inc(
                small_in, 16)
            sp.dma_start(fb[:, :, :], f_bias.rearrange("l d -> (l d)").partition_broadcast(P)).then_inc(small_in, 16)
            sp.wait_ge(diag_ready, 1)
            sp.dma_start(toeplitz, diag[:, :]).then_inc(toep_out, 16)
            for a in range(DSLOTS, 6):
                load_direct(a)
            load_unit(0, 0)
            load_unit(0, 1)
            load_direct(6)
            load_direct(7)
            sp.wait_ge(toep_out, 16)
            sp.dma_start(flipped, bass.AP(tensor=toeplitz.tensor, offset=0,
                                          ap=[[1, P], [384, 3 * HEADS], [1, SEQ]])).then_inc(bias_in, 16)
            load_unit(0, 2)
            a = 8
            for l in range(DEPTH):
                uses = 0
                for e in schedules[l]:
                    if e[0] == "latents":
                        load_direct(direct_at[("dsa", l, 0)])
                    elif e[0] == "ada":
                        load_direct(direct_at[e])
                    elif e[0] == "pair":
                        load_direct(direct_at[("ada", e[1], e[2])])
                        load_direct(direct_at[("ada", e[1], e[2] + 1)])
                    elif e[0] == "split_hi" and e[1] < NI + NO:
                        load_unit(l, e[1])
                load_mlp(l, 0, "gate", 0)
                load_mlp(l, 1, "value", 0)
                for j in range(STEPS - 1):
                    load_mlp(l, 3 * j + 2, "gate", j + 1)
                    for e in mlp_ada(l, j):
                        load_direct(direct_at[e])
                    load_mlp(l, 3 * j + 3, "value", j + 1)
                    load_mlp(l, 3 * j + 4, "down", j)
                load_mlp(l, 3 * STEPS - 1, "down", STEPS - 1)
                if l + 1 < DEPTH:
                    for i in range(RAW):
                        load_unit(l + 1, i)
            for t in range(TT):
                sp.wait_ge(out_part[t], 2)
                sp.dma_start(out[0, t * P:(t + 1) * P, :], x_tok[:, t, :]).then_inc(stored, 16)
            sp.wait_ge(stored, 16 * TT)

        @block.gpsimd
        def _(pool):
            nc.gpsimd.memset(ident[:, :], 0.0)
            nc.gpsimd.memset(reverse[:, :], 0.0)
            nc.gpsimd.memset(upto[:, :], 1.0)
            nc.gpsimd.memset(mean_w[:, :], 1.0 / D_MODEL)
            nc.gpsimd.memset(one[:, :], 1.0)
            nc.gpsimd.memset(minus_half[:, :], -0.5)
            nc.gpsimd.memset(ones[:, :], 1.0)
            nc.gpsimd.memset(half[:, :], 0.5).then_inc(consts, 1)
            pool.wait_ge(consts, 1)
            nc.gpsimd.affine_select(out=ident[:, :], in_=ident[:, :], compare_op=ALU.not_equal, fill=1.0, base=0,
                                    pattern=[[-1, P]], channel_multiplier=1)
            nc.gpsimd.affine_select(out=upto[:, :], in_=upto[:, :], compare_op=ALU.is_ge, fill=0.0, base=0,
                                    pattern=[[1, SEQ]], channel_multiplier=-1).then_inc(consts, 1)
            nc.gpsimd.affine_select(out=reverse[:, :], in_=reverse[:, :], compare_op=ALU.not_equal, fill=1.0,
                                    base=1 - P, pattern=[[1, P]], channel_multiplier=1).then_inc(consts, 1)
            def ada_sum(l, u):
                a, n = direct_at[("ada", l, u)], sum_no[(l, u)]
                w = direct[a % DSLOTS]
                if (l, u) in scaled_no:
                    pool.wait_ge(ada_scaled, scaled_no[(l, u)] + 1)
                else:
                    pool.wait_ge(direct_in[a % DSLOTS], direct_value(a))
                    nc.gpsimd.tensor_tensor(w[:, :].rearrange("p (k n) -> p k n", k=KT),
                                            w[:, :].rearrange("p (k n) -> p k n", k=KT),
                                            cond[:, :, 0:1].to_broadcast([P, KT, UC]), ALU.mult).then_inc(pool_scaled, 1)
                    pool.wait_ge(pool_scaled, multiplied_no[(l, u)] + 1)
                for step in range(1, 3):
                    if step > 1:
                        pool.wait_ge(ada_added, 2 * n + step - 1)
                    m = KT * UC >> step
                    nc.gpsimd.tensor_tensor(w[:, 0:m], w[:, 0:m], w[:, m:2 * m], ALU.add).then_inc(ada_added, 1)
                pool.wait_ge(ada_added, 2 * n + 2)
                pool.wait_ge(ada_turned, ada_no(l, u) - 1)
                cols = slice((u % 2) * UC, (u % 2 + 1) * UC)
                nc.gpsimd.tensor_tensor(ada_row[:, cols], w[:, 0:UC], w[:, UC:2 * UC], ALU.add).then_inc(ada_summed, 1)

            def inverse_root(n):
                pool.wait_ge(ms_inv, n + 1)
                nc.gpsimd.tensor_tensor(root[:, :], root[:, :], minus_half[:, :], ALU.pow).then_inc(rooted, 1)

            def sum_squares(n):
                for p in (1, 2):
                    pool.wait_ge(squares, 4 * n + p + 1)
                    if p > 1:
                        pool.wait_ge(pair_summed, 2 * n + 1)
                    nc.gpsimd.tensor_tensor(wide[:, 0:2, :], wide[:, 0:2, :], wide[:, 2 * p:2 * p + 2, :],
                                            ALU.add).then_inc(pair_summed, 1)
                pool.wait_ge(pair_summed, 2 * n + 2)
                nc.gpsimd.tensor_tensor(wide[:, 0, :], wide[:, 0, :], wide[:, 1, :], ALU.add).then_inc(squares_summed, 1)

            sum_squares(0)
            inverse_root(0)
            for l in range(DEPTH):
                if l:
                    sum_squares(2 * l)
                    inverse_root(2 * l)
                for e in schedules[l]:
                    if e[0] == "ada":
                        ada_sum(e[1], e[2])
                    elif e[0] == "latents_norm":
                        pool.wait_ge(lat_inv, l + 1)
                        nc.gpsimd.tensor_tensor(lat_ss[:, :], lat_ss[:, :], half[:, 0:4], ALU.pow).then_inc(lat_root, 1)
                    elif e[0] == "subln":
                        pool.wait_ge(sub_ss, l + 1)
                        nc.gpsimd.tensor_tensor(nrm[:, :], nrm[:, :], half[:, :], ALU.pow).then_inc(sub_root, 1)
                    elif e[0] == "choose" and e[1] == 0:
                        pool.wait_ge(idx_acc, 2 * HEADS * (l + 1))
                        nc.gpsimd.affine_select(out=score[:, 0::2, :], in_=score[:, 0::2, :], compare_op=ALU.is_ge,
                                                fill=-BIG, base=0, pattern=[[0, 2], [-1, P]],
                                                channel_multiplier=1).then_inc(score_masked, 1)
                    elif e[0] == "forget_up":
                        for h in range(HEADS):
                            pool.wait_ge(ck_ready, HEADS * l + h + 1)
                            nc.gpsimd.affine_select(out=own_bias[:, h, 0::2, :], in_=own_bias[:, h, 0::2, :],
                                                    compare_op=ALU.is_ge, fill=BIG, base=0,
                                                    pattern=[[0, 2], [-1, P]], channel_multiplier=1).then_inc(
                                own_ready, 1)
                    elif e[0] == "softmax" and MAPS[e[1]][0] == 2:
                        h = MAPS[e[1]][1]
                        pool.wait_ge(chosen, l + 1)
                        if l == 0 and h == 0:
                            pool.wait_ge(flip_read, 6)
                        pool.wait_ge(low_ready, 2 * (NM * l + e[1]) + 2)
                        nc.gpsimd.tensor_tensor(own_bias[:, h, 0, :], score[:, 0, :], bias[:, 2 * HEADS + h, P:2 * P],
                                                ALU.add)
                        nc.gpsimd.tensor_tensor(own_bias[:, h, 1:3, :], score[:, 1:3, :],
                                                bias[:, 2 * HEADS + h, :].rearrange("p (b k) -> p b k", b=2),
                                                ALU.add).then_inc(own_ready, 1)
                sum_squares(2 * l + 1)
                inverse_root(2 * l + 1)
                for j in range(STEPS):
                    for e in mlp_ada(l, j):
                        ada_sum(e[1], e[2])
            sum_squares(2 * DEPTH)
            inverse_root(2 * DEPTH)

        @block.tensor
        def _(pe):
            def product3(dst, lhs, rhs, first, last, check=False):
                (lh, ll), (rh, rl) = lhs, rhs
                pe.matmul(dst, lh, rh, start=first, stop=False, skip_group_check=check)
                pe.matmul(dst, lh, rl, start=False, stop=False, skip_group_check=check)
                return pe.matmul(dst, ll, rh, start=False, stop=last, skip_group_check=check)

            def ada(l, u):
                if l == 0 and u < SETUP_ADA:
                    if u >= 4:
                        pe.wait_ge(mod_ready, u - 2)
                else:
                    pe.wait_ge(mod_ready, ada_no(l, u))
                for half in range(2):
                    a = direct_at[("ada", l, u + half)]
                    pe.wait_ge(direct_in[a % DSLOTS], direct_value(a))
                    w = direct[a % DSLOTS][:, :].rearrange("p (k n) -> p k n", k=KT)
                    for i in range(2):
                        for g in range(4):
                            k = 4 * i + g
                            mm = pe.matmul(pair_bank(l, u)[32 * g:32 * g + 32, half * UC:(half + 1) * UC], cond[:, k, :],
                                           w[:, k, :], start=(i == 0), stop=(i == 1))
                    mm.then_inc(direct_used, 1)

            def ada_turn(l, u):
                pe.wait_ge(ada_rows, pair_no[(l, u)] + 1)
                for ct in range(4):
                    mm = pe.transpose(pair_bank(l, u)[:, ct * P:(ct + 1) * P], ada_row[:, ct * P:(ct + 1) * P], ident[:, :])
                mm.then_inc(ada_turned, 2)

            def ada_columns(l, u, n):
                pe.wait_ge(mod_ready, ada_no(l, u))
                pe.wait_ge(ada_summed, sum_no[(l, u)] + n)
                for ct in range(2 * n):
                    c0 = (u % 2) * UC + ct * P
                    mm = pe.matmul(bank[7][:, ct:ct + 1], ada_row[:, c0:c0 + P], ones[:, 0:1], start=True, stop=True)
                mm.then_inc(ada_turned, n)
                turned[0] = ada_no(l, u + n)

            turned = [SETUP_ADA]

            def mean_of(n):
                if n:
                    pe.wait_ge(mod_ready, turned[0])
                pe.wait_ge(squares, 4 * n + 4)
                for k in (KT - 2, KT - 1, 0):
                    if k == 0:
                        pe.wait_ge(squares_summed, n + 1)
                    for t in range(TT):
                        mm = pe.matmul(bank[7][:, t:t + 1], wide[:, k, t * P:(t + 1) * P], mean_w[:, :],
                                       start=(k == KT - 2 and t == 0), stop=(k == 0), skip_group_check=True)
                mm.then_inc(ms_ready, 1)

            def spread(n):
                for t in range(TT):
                    pe.wait_ge(diagonal_ready, TT * n + t + 1)
                    mm = pe.matmul(rstd[:, t * P:(t + 1) * P], ones[:, :], diagonal[:, t, :], start=True, stop=True,
                                   skip_group_check=True)
                mm.then_inc(rstd_ready, 1)

            def mean_square(n):
                mean_of(n)
                spread(n)

            def unit_product(l, i, bk, wait_act=None, k0=0, k1=KT):
                n = unit_no(l, i)
                pe.wait_ge(lo_done, n + 1)
                width = unit_width(i) if i < NI else UC
                wh = w_hi[n % RAW][:, 0:KT * width].rearrange("p (k n) -> p k n", k=KT)
                wl = w_lo[n % RAW][:, 0:KT * width].rearrange("p (k n) -> p k n", k=KT)
                if width < P:
                    for k in range(k0, k1):
                        if wait_act is not None:
                            pe.wait_ge(act_lo_ready, wait_act + k + 1)
                        mm = product3(bk[0:width, 0:SEQ], (wh[:, k, :], wl[:, k, :]), (act_hi[:, k, :], act_lo[:, k, :]),
                                      k == 0, k == KT - 1)
                    return mm
                token_rows = i < NI and IN_UNITS[i][0] in ("tail", "v")
                for k in range(k0, k1):
                    for t in range(2):
                        if wait_act is not None and t == 0:
                            pe.wait_ge(act_lo_ready, wait_act + k + 1)
                        s = slice(t * P, (t + 1) * P)
                        if token_rows:
                            mm = product3(bk[:, t * width:(t + 1) * width],
                                          (act_hi[:, k, s], act_lo[:, k, s]), (wh[:, k, :], wl[:, k, :]),
                                          k == 0 and t == 0, k == KT - 1, True)
                        else:
                            mm = product3(bk[:, t * SEQ:(t + 1) * SEQ], (wh[:, k, s], wl[:, k, s]),
                                          (act_hi[:, k, :], act_lo[:, k, :]), k == 0 and t == 0, k == KT - 1, True)
                return mm

            def turn_rows(b, c0, l, t):
                n = vector_rows(l, t)
                return pe.transpose(bank[b][:, c0:c0 + n], rows_in[0:n, l, t, :], ident[0:n, 0:n])

            pe.wait_ge(consts, 2)
            pe.wait_ge(c_in, 16)
            pe.transpose(bank[0][:, 0:KT], c_rows[:, :], ident[0:KT, 0:KT]).then_inc(c_turned, 1)
            pe.wait_ge(table_in, 16 * 2)
            pe.wait_ge(tab_ready, 1)
            pe.matmul(bank[6][0:3 * HEADS, 0:384], tab[:, :], buck[:, :], start=True, stop=True).then_inc(diag_up, 1)
            pe.wait_ge(cond_ready, 1)
            pe.wait_ge(diag_ready, 1)
            ada(0, 0)
            pe.wait_ge(rows_sem[0], 16 * 4)
            for l in range(DEPTH):
                mm = turn_rows(1, P * l, l, 0)
            mm.then_inc(vec_turned, 1)
            pe.wait_ge(x_in, 16)
            for k in range(KT):
                for t in range(TT):
                    mm = pe.transpose(bank[2 + k // 2][:, (k % 2) * SEQ + t * P:(k % 2) * SEQ + (t + 1) * P],
                                      x_tok[:, t, k * P:(k + 1) * P], ident[:, :])
                if k % 2:
                    mm.then_inc(x_turned, 1)
            pe.wait_ge(vec_in, 1)
            ada(0, 2)
            ada_turn(0, 0)
            pe.wait_ge(rows_sem[1], 16 * 4)
            for l in range(DEPTH):
                for t in (1, 2):
                    mm = turn_rows(0, P * (2 * l + t - 1), l, t)
            mm.then_inc(vec_turned, 1)
            ada_turn(0, 2)
            mean_of(0)
            ada(0, 4)
            ada(0, 6)
            ada_turn(0, 4)
            ada_turn(0, 6)
            pe.wait_ge(mod_ready, 8)
            spread(0)
            pe.wait_ge(vec_in, 5)

            def scores(l, first):
                for part in range(2):
                    for m in (first, first + 1):
                        g, h, comp = MAPS[m]
                        if part == 0 and m < 2:
                            pe.wait_ge(idx_relu, HEADS * l + HEADS - 1 + m)
                        elif part == 0:
                            pe.wait_ge(low_ready, 2 * (NM * l + m - 2) + 2)
                        p0, width = ((h % 2) * HEAD + comp * HALF, HALF) if g == 0 else ((h % 2) * HEAD, HEAD)
                        q = qkT[p0:p0 + width, g, 0, h // 2, :]
                        k = qkT[p0:p0 + width, g, 1, h // 2, :]
                        if part == 0:
                            pe.matmul(bank[2 + m % 2][:, 0:P], q[:, 0:P], k[:, 0:P], start=True, stop=True)
                        else:
                            pe.matmul(bank[2 + m % 2][:, P:3 * P], q[:, P:2 * P], k, start=True,
                                      stop=True).then_inc(s_ready, 1)

            for l in range(DEPTH):
                norm = 2 * l
                if l > 0:
                    mean_square(norm)
                for e in schedules[l]:
                    st, i = e[0], e[1]
                    if st == "unit":
                        if 2 <= i < NI + 2:
                            pe.wait_ge(in_read, NI * l + i - 1)
                        elif i >= NI + 2:
                            pe.wait_ge(low_ready, 2 * NM * (l + 1))
                        if i >= NI:
                            pe.wait_ge(turn_lo, 4 * l + e[3] // 2)
                        mm = unit_product(l, i, unit_bank(i), KT * norm if i < 2 else None, e[2], e[3])
                        if e[3] == KT:
                            mm.then_inc(unit_used, 1)
                    elif st == "mean":
                        mean_square(norm + 1)
                    elif st == "pair":
                        ada(e[1], e[2])
                    elif st == "pair_turn":
                        ada_turn(e[1], e[2])
                        turned[0] = ada_no(e[1], e[2] + 2)
                    elif st == "column":
                        ada_columns(e[1], e[2], 1)
                    elif st == "narrow":
                        pe.wait_ge(in_read, NI * l + 1)
                        for t in range(TT):
                            mm = pe.transpose(bank[6][:, t * NARROW:(t + 1) * NARROW], narrow[:, t * P:(t + 1) * P],
                                              ident[0:NARROW, 0:NARROW])
                        mm.then_inc(narrow_turned, 1)
                    elif st == "flip":
                        pe.wait_ge(narrow_read, 1)
                        pe.wait_ge(bias_in, 16)
                        pe.wait_ge(consts, 3)
                        for n, b in enumerate(FLIP_BANKS):
                            if n >= 5:
                                pe.wait_ge(flip_read, n - 4)
                            pe.matmul(bank[b][:, :], reverse[:, :], flipped[:, 2 * n:2 * n + 2, :], start=True,
                                      stop=True).then_inc(flip_ready, 1)
                    elif st == "latents":
                        if l == 0:
                            pe.wait_ge(flip_read, 6)
                        pe.wait_ge(ki_ready, l + 1)
                        for t in range(TT):
                            pe.transpose(bank[4][:, t * P:(t + 1) * P],
                                         ki_twice[:, t, :, :].rearrange("p a d -> p (a d)"), ident[:, :])
                        pe.wait_ge(lat_ready, l + 1)
                        for w in range(2):
                            for t in range(TT):
                                mm = pe.transpose(bank[6][:, w * SEQ + t * P:w * SEQ + (t + 1) * P], latn[:, t, w, :],
                                                  ident[:, :])
                        mm.then_inc(latT_ready, 1)
                    elif st == "latents_up":
                        pe.wait_ge(latT_read, 2 * l + 2)
                        a = direct_at[("dsa", l, 0)]
                        pe.wait_ge(direct_in[a % DSLOTS], direct_value(a))
                        w = direct[a % DSLOTS]
                        for b, c0, src in ((2, 0, 0), (3, 256, 0), (4, 512, 1)):
                            for t in range(2):
                                mm = pe.matmul(bank[b][:, t * SEQ:(t + 1) * SEQ], w[:, c0 + t * P:c0 + (t + 1) * P],
                                               latT[:, src, :], start=True, stop=True)
                            mm.then_inc(up_ready, 1)
                        for t in range(TT):
                            mm = pe.matmul(bank[5][:, t * GROUP:(t + 1) * GROUP], latT[:, 1, t * P:(t + 1) * P],
                                           w[:, 768:1024], start=True, stop=True)
                        mm.then_inc(direct_used, 1)
                    elif st == "index":
                        pe.wait_ge(up_read, 4 * l + 4)
                        if i >= 2:
                            pe.wait_ge(idx_relu, HEADS * l + i - 1)
                        r = slice((i % 2) * HEAD, (i % 2) * HEAD + HEAD)
                        b = bank[2 + i % 2]
                        pe.matmul(b[:, 0:P], qiT[r, i // 2, 0:P], kiT[r, 0:P], start=True, stop=True)
                        pe.matmul(b[:, P:3 * P], qiT[r, i // 2, P:2 * P], kiT[r, :], start=True,
                                  stop=True).then_inc(s_ready, 1)
                    elif st == "forget_up":
                        pe.wait_ge(lf_ready, l + 1)
                        pe.wait_ge(mod_ready, turned[0])
                        lf = fz[:, 3, :].rearrange("p (t h) -> p t h", t=TT)
                        pe.matmul(bank[7][:, 128:132], upto[:, 0:P], lf[:, 0, :], start=True, stop=True)
                        pe.matmul(bank[7][:, 132:136], upto[:, P:2 * P], lf[:, 0, :], start=True, stop=False)
                        pe.matmul(bank[7][:, 132:136], upto[:, 0:P], lf[:, 1, :], start=False,
                                  stop=True).then_inc(cum_ready, 1)
                        pe.wait_ge(up_read, 4 * l + 4)
                        pe.wait_ge(lfw_ready, l + 1)
                        for h in range(HEADS):
                            b = bank[4 + h // 2][:, (h % 2) * SEQ:(h % 2 + 1) * SEQ]
                            pe.matmul(b, lf_wide[:, h, :], upto[:, :], start=True, stop=False)
                            mm = pe.matmul(b[:, P:2 * P], lf_wide[:, HEADS + h, :], upto[:, 0:P], start=False, stop=True)
                        mm.then_inc(cum_ready, 1)
                        pe.wait_ge(ncq_ready, l + 1)
                    elif st == "scores":
                        scores(l, i)
                    elif st == "probs":
                        n = turn_no[("probs", i)]
                        if n >= 2:
                            wait_turned(pe, l, n - 2)
                        else:
                            pe.wait_ge(ck_ready, HEADS * (l + 1))
                        pe.wait_ge(exp_ready, 2 * (NM * l + i) + 2)
                        for b in range(3):
                            mm = pe.transpose(bank[4 + n % 2][:, b * P:(b + 1) * P], soft[i % 3][:, b, :], ident[:, :])
                        mm.then_inc(t_ready, 1)
                    elif st == "values":
                        g, h, comp = MAPS[i]
                        slot, quad = i % 4, i // 4
                        wait_turned(pe, l, turn_no[("probs", i)])
                        if slot == 0 and quad > 0:
                            pe.wait_ge(o_read, 5 * l + quad)
                        pt = probT[i % 3]
                        o = bank[6][:, :].rearrange("p (t s d) -> p t s d", t=TT, s=4)
                        v = v_sb[:, g, :, h * HEAD:(h + 1) * HEAD]
                        pe.matmul(o[:, 0, slot, :], pt[:, 0, :], v[:, 0, :], start=True, stop=True)
                        pe.matmul(o[:, 1, slot, :], pt[:, 1, :], v[:, 0, :], start=True, stop=False)
                        pe.matmul(o[:, 1, slot, :], pt[:, 2, :], v[:, 1, :], start=False, stop=True).then_inc(
                            pv_ready, 1)
                    elif st == "turn":
                        n = turn_no[("turn", i)]
                        wait_turned(pe, l, n - 2)
                        if i % 2 == 0:
                            pe.wait_ge(group_ready, 2 * l + i // 2 + 1)
                        else:
                            pe.wait_ge(o_read, 5 * l + i + 2)
                        for w in range(2):
                            for t in range(TT):
                                mm = pe.transpose(bank[4 + n % 2][:, w * SEQ + t * P:w * SEQ + (t + 1) * P],
                                                  heads_out[:, i, t, w * P:(w + 1) * P], ident[:, :])
                        mm.then_inc(t_ready, 1)
                down = [bank[3 + ct // 2][:, (ct % 2) * SEQ:(ct % 2 + 1) * SEQ] for ct in range(KT)]

                def up(j, which):
                    pe.wait_ge(conv_read, 2 * (STEPS * l + j - 1) + which + 1)
                    unit_product(l, NI + NO + 3 * j - 1 + which, bank[which]).then_inc(unit_used, 1)

                def down_product(j):
                    o = 3 * j + 4 if j < STEPS - 1 else 3 * STEPS - 1
                    n = unit_no(l, NI + NO + o)
                    pe.wait_ge(lo_done, n + 1)
                    pe.wait_ge(mlp_lo_ready, STEPS * l + j + 1)
                    wh = w_hi[n % RAW][:, :].rearrange("p (f n) -> p f n", f=2)
                    wl = w_lo[n % RAW][:, :].rearrange("p (f n) -> p f n", f=2)
                    for ct in range(KT):
                        for f in range(2):
                            s = slice(ct * P, (ct + 1) * P)
                            mm = product3(down[ct], (wh[:, f, s], wl[:, f, s]), (mlp_hi[:, f, :], mlp_lo[:, f, :]),
                                          j == 0 and f == 0 and ct % 2 == 0, j == STEPS - 1 and f == 1, True)
                        if j == STEPS - 1 and ct in (1, 3, 5):
                            mm.then_inc(down_ready, 1)
                    mm.then_inc(unit_used, 1)

                for which in range(2):
                    unit_product(l, NI + NO + which, bank[which],
                                 None if which else KT * (norm + 1)).then_inc(unit_used, 1)
                for j in range(1, STEPS):
                    up(j, 0)
                    up(j, 1)
                    down_product(j - 1)
                    for e in mlp_ada(l, j - 1)[:1]:
                        ada_columns(e[1], e[2], 2)
                down_product(STEPS - 1)
            for q in range(2):
                if q:
                    mean_of(2 * DEPTH)
                pe.wait_ge(fin_ready, 4 * (q + 1))
                for t in range(TT):
                    for k in range(4):
                        mm = pe.transpose(bank[2 * q + t][:, k * P:(k + 1) * P], final[:, 4 * q + k, t * P:(t + 1) * P],
                                          ident[:, :])
                    mm.then_inc(finT_ready, 1)

        @block.scalar
        def _(act):
            def split_hi(n, width=UC):
                wait_raw(act, n)
                if n >= RAW:
                    act.wait_ge(unit_used, n - RAW + 1)
                nc.scalar.activation(w_hi[n % RAW][:, 0:KT * width], raw[n % RAW][:, 0:KT * width],
                                     ACT.Copy).then_inc(hi_done, 1)

            def squares_of(n):
                for p in range(KT // 2):
                    act.wait_ge(x_new, 4 * n + p + 1)
                    nc.scalar.activation(wide[:, 2 * p:2 * p + 2, :], xT[:, 2 * p:2 * p + 2, :], ACT.Square).then_inc(
                        squares, 1)

            def take_rows(l, u):
                wait_used(act, direct_at[("ada", l, u)])
                wait_used(act, direct_at[("ada", l, u + 1)])
                act.wait_ge(ada_turned, ada_no(l, u))
                nc.scalar.activation(ada_row[:, :], pair_bank(l, u)[:, :], ACT.Copy).then_inc(ada_rows, 1)

            def ada_scale(l, u):
                a = direct_at[("ada", l, u)]
                w = direct[a % DSLOTS]
                act.wait_ge(direct_in[a % DSLOTS], direct_value(a))
                for k in range(KT):
                    ins = nc.scalar.activation(w[:, k * UC:(k + 1) * UC], w[:, k * UC:(k + 1) * UC], ACT.Identity,
                                               scale=cond[:, k, 0:1])
                ins.then_inc(ada_scaled, 1)

            def modulated(n, l, shift):
                for k in range(KT):
                    act.wait_ge(scaled, KT * n + k + 1)
                    nc.scalar.activation(act_hi[:, k, :], wide[:, k, :], ACT.Identity,
                                         bias=mod[:, l, shift + k:shift + k + 1]).then_inc(act_hi_ready, 1)

            act.wait_ge(c_turned, 1)
            nc.scalar.activation(cond[:, :, :], bank[0][:, 0:KT].unsqueeze(2).to_broadcast([P, KT, 32]),
                                 ACT.Silu).then_inc(cond_ready, 1)
            act.wait_ge(diag_up, 1)
            nc.scalar.activation(diag[:, :], bank[6][0:3 * HEADS, 0:384], ACT.Copy, scale=-1.0).then_inc(diag_ready, 1)
            act.wait_ge(vec_turned, 1)
            nc.scalar.activation(vec[:, :, 0:VROWS[0]], bank[1][:, 0:DEPTH * P].rearrange(
                "p (l r) -> p l r", l=DEPTH)[:, :, 0:VROWS[0]], ACT.Copy).then_inc(vec_in, 1)
            take_rows(0, 0)
            squares_of(0)
            act.wait_ge(vec_turned, 2)
            for l in range(DEPTH):
                for t in (1, 2):
                    n, c0 = vector_rows(l, t), P * (2 * l + t - 1)
                    nc.scalar.activation(vec[:, l, P * t:P * t + n], bank[0][:, c0:c0 + n], ACT.Copy).then_inc(vec_in, 1)
            take_rows(0, 2)
            act.wait_ge(lam_sem, 1)
            nc.scalar.activation(lam_ex[:, :], lam_ex[:, :], ACT.Exp).then_inc(lam_exp, 1)
            take_rows(0, 4)
            for i in range(2):
                split_hi(i, unit_width(i))
            take_rows(0, 6)

            for l in range(DEPTH):
                if l > 0:
                    squares_of(2 * l)
                modulated(2 * l, l, 0)
                split_hi(unit_no(l, 2), unit_width(2))
                for e in schedules[l]:
                    st, i = e[0], e[1]
                    if st == "split_hi":
                        split_hi(unit_no(l, i), unit_width(i))
                    elif st == "flip":
                        for n, b in enumerate(FLIP_BANKS):
                            act.wait_ge(flip_ready, n + 1)
                            nc.scalar.activation(bias[:, 2 * n:2 * n + 2, :],
                                                 bank[b][:, :].rearrange("p (h k) -> p h k", h=2), ACT.Copy).then_inc(
                                flip_read, 1)
                    elif st == "ada":
                        if e[1:] in scaled_no:
                            ada_scale(e[1], e[2])
                    elif st == "narrow":
                        act.wait_ge(narrow_turned, l + 1)
                        nc.scalar.activation(tail[:, :, TAIL - NARROW:TAIL], bank[6][:, 0:TT * NARROW].rearrange(
                            "p (t n) -> p t n", t=TT), ACT.Copy).then_inc(narrow_read, 1)
                    elif st == "pair_turn":
                        take_rows(e[1], e[2])
                    elif st == "evac":
                        kind, g, width = IN_UNITS[i]
                        act.wait_ge(unit_used, unit_no(l, i) + 1)
                        src = bank[i % 2][:, 0:2 * width].rearrange("p (t n) -> p t n", t=2)
                        if width < P:
                            nc.scalar.activation(narrow, bank[i % 2][0:width, 0:SEQ], ACT.Copy).then_inc(in_read, 1)
                        elif kind == "tail":
                            nc.scalar.activation(tail[:, :, g:g + width], src, ACT.Copy).then_inc(in_read, 1)
                        elif kind == "v":
                            nc.scalar.activation(v_sb[:, g, :, :], src, ACT.Copy).then_inc(in_read, 1)
                        else:
                            nc.scalar.activation(qkT[:, g, "qk".index(kind), :, :], src, ACT.Copy,
                                                 scale=-SCALE[g] if kind == "q" else 1.0).then_inc(in_read, 1)
                    elif st == "latents_norm":
                        act.wait_ge(narrow_read, l + 1)
                        nc.scalar.activation(ki_twice, tail[:, :, T_KIDX:T_KIDX + HEAD].unsqueeze(2).to_broadcast(
                            [P, TT, 2, HEAD]), ACT.Copy).then_inc(ki_ready, 1)
                    elif st == "latents":
                        act.wait_ge(latT_ready, l + 1)
                        nc.scalar.activation(latT[:, :, :], bank[6][:, :].rearrange("p (w t) -> p w t", w=2),
                                             ACT.Copy).then_inc(latT_read, 1)
                        nc.scalar.activation(kiT[:, :], bank[4][:, 0:SEQ], ACT.Copy).then_inc(latT_read, 1)
                    elif st == "latents_up":
                        two = lambda b: bank[b][:, :].rearrange("p (t n) -> p t n", t=2)
                        act.wait_ge(up_ready, 3 * l + 1)
                        nc.scalar.activation(qkT[:, 3, 0, :, :], two(2), ACT.Copy, scale=-SCALE[3]).then_inc(up_read, 1)
                        act.wait_ge(up_ready, 3 * l + 2)
                        nc.scalar.activation(qiT[:, :, :], two(3), ACT.Copy,
                                             scale=HEAD ** -0.5 * HEADS ** -0.5).then_inc(up_read, 1)
                        act.wait_ge(up_ready, 3 * l + 3)
                        nc.scalar.activation(qkT[:, 3, 1, :, :], two(4), ACT.Copy).then_inc(up_read, 1)
                        wait_used(act, direct_at[("dsa", l, 0)])
                        nc.scalar.activation(v_sb[:, 3, :, :], two(5), ACT.Copy).then_inc(up_read, 1)
                    elif st == "forget":
                        act.wait_ge(fz_ready, 2 * l + 2)
                        nc.scalar.activation(fz[:, 1, :], fz[:, 1, :], ACT.Exp, scale=-1.0).then_inc(fe_ready, 1)
                        nc.scalar.activation(gate_c, gate_c, ACT.Tanh,
                                             scale=0.5).then_inc(gate_exp, 1)
                        act.wait_ge(fe_ready, 2 * l + 1)
                        nc.scalar.activation(fz[:, 1, :], fz[:, 1, :], ACT.Ln, bias=one[:, :]).then_inc(fe_ready, 1)
                        act.wait_ge(lf_ready, l + 1)
                        nc.scalar.activation(lf_wide, fz[:, 3, :].unsqueeze(2).to_broadcast([P, TT * HEADS, P]),
                                             ACT.Copy).then_inc(lfw_ready, 1)
                    elif st == "index":
                        act.wait_ge(s_ready, SC * l + i + 1)
                        if i >= 2:
                            act.wait_ge(idx_acc, 2 * (HEADS * l + i - 1))
                        nc.scalar.activation(relu[i % 2], bank[2 + i % 2][:, 0:384].rearrange("p (b k) -> p b k", b=3),
                                             ACT.Relu).then_inc(idx_relu, 1)
                    elif st == "forget_up":
                        act.wait_ge(cum_ready, 2 * l + 1)
                        nc.scalar.activation(ncq[:, :], bank[7][:, 128:128 + TT * HEADS], ACT.Copy,
                                             scale=-1.0).then_inc(ncq_ready, 1)
                        act.wait_ge(ncq_ready, l + 1)
                        act.wait_ge(cum_ready, 2 * l + 2)
                        for h in range(HEADS):
                            ck = bank[4 + h // 2][:, (h % 2) * SEQ:(h % 2 + 1) * SEQ]
                            nc.scalar.activation(own_bias[:, h, 0, :], ck[:, 0:P], ACT.Identity, bias=ncq[:, h:h + 1])
                            nc.scalar.activation(own_bias[:, h, 1:3, :], ck.rearrange("p (b k) -> p b k", b=2),
                                                 ACT.Identity, bias=ncq[:, HEADS + h:HEADS + h + 1]).then_inc(ck_ready, 1)
                    elif st == "softmax":
                        m = NM * l + i
                        dst = soft[i % 3]
                        for t, part in ((0, dst[:, 0, :]), (1, dst[:, 1:3, :])):
                            act.wait_ge(low_ready, 2 * m + t + 1)
                            nc.scalar.activation(part, part, ACT.Exp, bias=low[:, i % 3, t:t + 1], scale=-1.0,
                                                 accum_out=rsum[:, (i // 4) % 2, t, i % 4:i % 4 + 1]).then_inc(
                                exp_ready, 1)
                    elif st == "probs":
                        n = turn_no[("probs", i)]
                        if n % 2 == 0:
                            act.wait_ge(t_ready, NT * l + n + 1)
                            if i >= 3:
                                act.wait_ge(pv_ready, NM * l + i - 2)
                            nc.scalar.activation(probT[i % 3], bank[4][:, 0:384].rearrange("p (b q) -> p b q", b=3),
                                                 ACT.Copy).then_inc(pt_act, 1)
                    elif st == "turn":
                        n = turn_no[("turn", i)]
                        act.wait_ge(t_ready, NT * l + n + 1)
                        act.wait_ge(unit_used, unit_no(l, NI))
                        nc.scalar.activation(act_hi[:, 2 * i:2 * i + 2, :],
                                             bank[4 + n % 2][:, :].rearrange("p (w t) -> p w t", w=2),
                                             ACT.Copy).then_inc(turn_hi, 1)
                    elif st == "resid":
                        act.wait_ge(x_new, 4 * (2 * l + 1) + i + 1)
                        nc.scalar.activation(wide[:, 2 * i:2 * i + 2, :], xT[:, 2 * i:2 * i + 2, :],
                                             ACT.Square).then_inc(squares, 1)
                first = unit_no(l, NI + NO)
                modulated(2 * l + 1, l, 3 * KT)

                def last_tap(j, which):
                    o = which if j == 0 else 3 * j - 1 + which
                    act.wait_ge(unit_used, first + o + 1)
                    if j > 0:
                        act.wait_ge(prod_done, STEPS * l + j)
                    for f in range(2):
                        ch = which * FT + 2 * j + f
                        nc.scalar.activation(conv[:, which, f, :], bank[which][:, f * SEQ:(f + 1) * SEQ], ACT.Identity,
                                             scale=vec[:, l, V_W2 + ch:V_W2 + ch + 1],
                                             bias=vec[:, l, V_CB + ch:V_CB + ch + 1]).then_inc(tap_ready, 1)

                for j in range(STEPS):
                    if j < STEPS - 1:
                        split_hi(first + 3 * j + 2)
                    last_tap(j, 0)
                    if j < STEPS - 1:
                        split_hi(first + 3 * j + 3)
                    last_tap(j, 1)
                    act.wait_ge(conv_read, 2 * (STEPS * l + j) + 1)
                    nc.scalar.activation(silu, conv[:, 0, :, :], ACT.Silu).then_inc(silu_ready, 1)
                    split_hi(first + (3 * j + 4 if j < STEPS - 1 else 3 * STEPS - 1))
                    act.wait_ge(prod_done, STEPS * l + j + 1)
                    if j > 0:
                        act.wait_ge(unit_used, first + 3 * j + 2)
                    nc.scalar.activation(mlp_hi[:, :, :], prod, ACT.Copy).then_inc(mlp_hi_ready, 1)
                    for e in mlp_ada(l, j):
                        if e[1:] in scaled_no:
                            ada_scale(e[1], e[2])
                if l + 1 < DEPTH:
                    for i in range(2):
                        split_hi(unit_no(l + 1, i), unit_width(i))
            squares_of(2 * DEPTH)
            act.wait_ge(rooted, 2 * DEPTH + 1)
            for q in range(2):
                act.wait_ge(finT_ready, 2 * q + 2)
                nc.scalar.activation(x_tok[:, 1, 512 * q:512 * q + 512], bank[2 * q + 1][:, :], ACT.Identity,
                                     scale=root[:, 1:2]).then_inc(out_part[1], 1)

        @block.vector
        def _(dve):
            count = [0]

            def own(ins):
                count[0] += 1
                ins.then_inc(dve_own, 1)
                dve.wait_ge(dve_own, count[0])

            def split_lo(n, width=UC):
                dve.wait_ge(hi_done, n + 1)
                s = slice(0, KT * width)
                nc.vector.tensor_tensor(w_lo[n % RAW][:, s], raw[n % RAW][:, s], w_hi[n % RAW][:, s].bitcast(F32),
                                        ALU.subtract).then_inc(lo_done, 1)

            def mean_plus(n):
                dve.wait_ge(ms_ready, n + 1)
                nc.vector.tensor_scalar(root[:, :], bank[7][:, 0:TT], EPS, None, ALU.add).then_inc(ms_inv, 1)

            def inverse(n):
                mean_plus(n)
                dve.wait_ge(rooted, n + 1)
                for t in range(TT):
                    nc.vector.tensor_scalar(diagonal[:, t, :], ident[:, :], root[:, t:t + 1], None,
                                            ALU.mult).then_inc(diagonal_ready, 1)

            def modulated(n, l, which):
                dve.wait_ge(rstd_ready, n + 1)
                shift = 3 * KT * which

                def low_half(k):
                    dve.wait_ge(act_hi_ready, KT * n + k + 1)
                    nc.vector.scalar_tensor_tensor(act_lo[:, k, :], wide[:, k, :], mod[:, l, shift + k:shift + k + 1],
                                                   act_hi[:, k, :].bitcast(F32), ALU.add, ALU.subtract).then_inc(
                        act_lo_ready, 1)
                for k in range(KT):
                    nc.vector.scalar_tensor_tensor(wide[:, k, :], xT[:, k, :], amp[:, which, k:k + 1], rstd,
                                                   ALU.mult, ALU.mult).then_inc(scaled, 1)
                    if k >= 2:
                        low_half(k - 2)
                low_half(KT - 2)
                low_half(KT - 1)

            def residual(l, gate, p, src):
                for k in range(2):
                    kt = 2 * p + k
                    ins = nc.vector.scalar_tensor_tensor(xT[:, kt, :], src[:, k * SEQ:(k + 1) * SEQ],
                                                         mod[:, l, gate * KT + kt:gate * KT + kt + 1], xT[:, kt, :],
                                                         ALU.mult, ALU.add)
                ins.then_inc(x_new, 1)

            def take_mod(l, u):
                n = ada_no(l, u + 2)
                dve.wait_ge(ada_turned, n)
                s = slice(2 * u, 2 * u + 4)
                nc.vector.tensor_reduce(mod[:, l, s], pair_bank(l, u)[:, :].rearrange("p (c g r) -> p c g r", g=4, r=32)[:, :, :, 0],
                                        AX.X, ALU.add).then_inc(mod_ready, 2)
                dve.wait_ge(mod_ready, n)
                nc.vector.tensor_tensor(mod[:, l, s], mod[:, l, s], vec[:, l, V_BADA + 2 * u:V_BADA + 2 * u + 4],
                                        ALU.add).then_inc(mod_done, 1)

            def take_columns(l, u, n):
                dve.wait_ge(ada_turned, ada_no(l, u + n))
                nc.vector.tensor_tensor(mod[:, l, 2 * u:2 * (u + n)], bank[7][:, 0:2 * n],
                                        vec[:, l, V_BADA + 2 * u:V_BADA + 2 * (u + n)], ALU.add).then_inc(mod_ready, n)

            def wait_mod(n):
                dve.wait_ge(mod_ready, n)
                dve.wait_ge(mod_done, sum(ada_no(*p) < n for p in pair_no))

            def amplitudes(l, which):
                v = V_N2 if which else V_N1
                own(nc.vector.scalar_tensor_tensor(amp[:, which, :], mod[:, l, KT * (3 * which + 1):KT * (3 * which + 2)],
                                                   1.0, vec[:, l, v:v + KT], ALU.add, ALU.mult))

            nc.vector.memset(tab[BUCKETS:BUCKETS + 1, :], -BIG).then_inc(tab_ready, 1)
            for p in range(KT // 2):
                dve.wait_ge(x_turned, p + 1)
                nc.vector.tensor_copy(xT[:, 2 * p:2 * p + 2, :],
                                      bank[2 + p][:, :].rearrange("p (k t) -> p k t", k=2)).then_inc(x_new, 1)
            dve.wait_ge(vec_in, 1)
            take_mod(0, 0)
            dve.wait_ge(small_in, 16 * 3)
            own(nc.vector.tensor_tensor(lam_pr[:, :, :], lam_in[:, :, 0::2, :].rearrange("p l a d -> p (l a) d"),
                                        lam_in[:, :, 1::2, :].rearrange("p l a d -> p (l a) d"), ALU.mult))
            nc.vector.tensor_reduce(lam_ex[:, :], lam_pr[:, :, :], AX.X, ALU.add).then_inc(lam_sem, 1)
            for l in range(DEPTH):
                nc.vector.tensor_scalar(gain64[:, l, :], gain64[:, l, :], 1.0 - lam_init[l], None, ALU.mult)
            take_mod(0, 2)
            inverse(0)
            dve.wait_ge(lam_exp, 1)
            for l in range(DEPTH):
                own(nc.vector.tensor_tensor(nlam[:, l:l + 1], lam_ex[:, 2 * l + 1:2 * l + 2], lam_ex[:, 2 * l:2 * l + 1],
                                            ALU.subtract))
                own(nc.vector.tensor_scalar(nlam[:, l:l + 1], nlam[:, l:l + 1], -lam_init[l], None, ALU.add))
            for i in range(2):
                split_lo(i, unit_width(i))
            take_mod(0, 4)
            take_mod(0, 6)
            wait_mod(SETUP_ADA)
            amplitudes(0, 0)

            for l in range(DEPTH):
                if l > 0:
                    inverse(2 * l)
                    wait_mod(NA * l + SETUP_ADA)
                    amplitudes(l, 0)
                modulated(2 * l, l, 0)
                split_lo(unit_no(l, 2), unit_width(2))
                for e in schedules[l]:
                    st, i = e[0], e[1]
                    if st == "split_lo":
                        split_lo(unit_no(l, i), unit_width(i))
                    elif st == "pair_turn":
                        take_mod(e[1], e[2])
                    elif st == "column":
                        take_columns(e[1], e[2], 1)
                    elif st == "latents_norm":
                        dve.wait_ge(in_read, NI * l + 2)
                        dve.wait_ge(narrow_read, l + 1)
                        for t in range(TT):
                            for w in range(2):
                                src = tail[:, t, T_LAT + w * P:T_LAT + (w + 1) * P]
                                last = nc.vector.tensor_tensor_reduce(latn[:, t, w, :], src, src, 1.0, 0.0, ALU.mult,
                                                                      ALU.add, lat_ss[:, 2 * t + w:2 * t + w + 1])
                                if (t, w) != (1, 1):
                                    last.then_inc(dve_own, 1)
                                    count[0] += 1
                        own(last)
                        own(nc.vector.tensor_scalar(lat_ss[:, :], lat_ss[:, :], 1.0 / P, EPS, ALU.mult, ALU.add))
                        nc.vector.reciprocal(lat_ss[:, :], lat_ss[:, :]).then_inc(lat_inv, 1)
                        dve.wait_ge(lat_root, l + 1)
                        for t in range(TT):
                            for w in range(2):
                                last = nc.vector.tensor_scalar(latn[:, t, w, :], tail[:, t, T_LAT + w * P:T_LAT + (w + 1) * P],
                                                               lat_ss[:, 2 * t + w:2 * t + w + 1], None, ALU.mult)
                        last.then_inc(lat_ready, 1)
                    elif st == "forget":
                        dve.wait_ge(in_read, NI * l + 3)
                        own(nc.vector.tensor_tensor(fz[:, 0, :].rearrange("p (t h) -> p t h", t=TT), tail[:, :, 0:HEADS],
                                                    fb[:, l, :].unsqueeze(1).to_broadcast([P, TT, HEADS]), ALU.add))
                        nc.vector.scalar_tensor_tensor(fz[:, 1, :], fz[:, 0, :], -1.0, fz[:, 0, :], ALU.mult, ALU.max).then_inc(fz_ready, 1)
                        nc.vector.tensor_scalar(fz[:, 2, :], fz[:, 0, :], 0.0, None, ALU.min).then_inc(fz_ready, 1)
                        dve.wait_ge(fe_ready, 2 * l + 2)
                        nc.vector.tensor_tensor(fz[:, 3, :], fz[:, 2, :], fz[:, 1, :], ALU.subtract).then_inc(lf_ready, 1)
                        dve.wait_ge(gate_exp, l + 1)
                        own(nc.vector.tensor_scalar(gate_c, gate_c, 0.5, 0.5, ALU.mult, ALU.add))
                    elif st == "index":
                        dve.wait_ge(idx_relu, HEADS * l + i + 1)
                        if i:
                            dve.wait_ge(idx_acc, 2 * (HEADS * l + i))
                        for t, b in ((0, slice(0, 1)), (1, slice(1, 3))):
                            w = tail[:, t, T_WIDX + i:T_WIDX + i + 1]
                            if i == 0:
                                nc.vector.tensor_scalar(score[:, b, :], relu[0][:, b, :], w, None,
                                                        ALU.mult).then_inc(idx_acc, 1)
                            else:
                                nc.vector.scalar_tensor_tensor(score[:, b, :], relu[i % 2][:, b, :], w,
                                                               score[:, b, :], ALU.mult, ALU.add).then_inc(idx_acc, 1)
                    elif st == "choose":
                        if i == 0:
                            dve.wait_ge(score_masked, l + 1)
                        for b in (slice(0, 1), slice(1, 3)):
                            part = score[:, b, :].rearrange("p b k -> p (b k)")
                            own(nc.vector.max(top8[:, :], part))
                            own(nc.vector.match_replace(part, top8[:, :], part, TAKEN))
                        if i == TOPK // 8 - 1:
                            nc.vector.tensor_scalar(score[:, :, :], score[:, :, :], TAKEN / 2, BIG, ALU.is_gt,
                                                    ALU.mult).then_inc(chosen, 1)
                    elif st == "softmax":
                        g, h, comp = MAPS[i]
                        dve.wait_ge(s_ready, SC * l + HEADS + i + 1)
                        if g < 2:
                            if l == 0 and i == 0:
                                dve.wait_ge(flip_read, 6)
                            b = bias[:, 4 * g + h, :]
                            biases = b[:, P:2 * P], b.rearrange("p (b k) -> p b k", b=2)
                        else:
                            dve.wait_ge(own_ready, 8 * l + 4 * (g - 2) + h + 1)
                            biases = own_bias[:, h, 0, :], own_bias[:, h, 1:3, :]
                        if i < 3:
                            dve.wait_ge(idx_acc, 2 * HEADS * (l + 1))
                        else:
                            dve.wait_ge(t_ready, NT * l + turn_no[("probs", i - 3)] + 1)
                        s = bank[2 + i % 2][:, 0:384].rearrange("p (b k) -> p b k", b=3)
                        nc.vector.tensor_tensor_reduce(soft[i % 3][:, 0, :], s[:, 0, :], biases[0], 1.0, 3e38, ALU.add,
                                                       ALU.min, low[:, i % 3, 0:1]).then_inc(low_ready, 1)
                        nc.vector.tensor_tensor_reduce(soft[i % 3][:, 1:3, :], s[:, 1:3, :], biases[1], 1.0, 3e38,
                                                       ALU.add, ALU.min, low[:, i % 3, 1:2]).then_inc(low_ready, 1)
                    elif st == "probs":
                        n = turn_no[("probs", i)]
                        if n % 2:
                            dve.wait_ge(t_ready, NT * l + n + 1)
                            if i >= 3:
                                dve.wait_ge(pv_ready, NM * l + i - 2)
                            nc.vector.tensor_copy(probT[i % 3], bank[5][:, 0:384].rearrange("p (b q) -> p b q", b=3)).then_inc(
                                pt_dve, 1)
                    elif st == "heads":
                        own(nc.vector.reciprocal(rinv[:, :, :], rsum[:, i % 2, :, :]))
                        dve.wait_ge(pv_ready, NM * l + 4 * i + 4)
                        o = bank[6][:, :].rearrange("p (t s d) -> p t s d", t=TT, s=4)
                        r = rinv[:, :, :].unsqueeze(3).to_broadcast([P, TT, 4, HEAD])
                        g = max(i - 1, 0)
                        dst = pair[:, :, :, :] if i < 2 else heads_out[:, g, :, :].rearrange("p t (s d) -> p t s d", s=4)
                        ins = nc.vector.tensor_tensor(dst, o, r, ALU.mult)
                        ins.then_inc(o_read, 1)
                        if i < 2:
                            dve.wait_ge(o_read, 5 * l + i + 1)
                            for t in range(TT):
                                last = nc.vector.scalar_tensor_tensor(
                                    heads_out[:, 0, t, i * P:(i + 1) * P].rearrange("p (h d) -> p h d", h=2),
                                    pair[:, t, 1::2, :], nlam[:, l:l + 1], pair[:, t, 0::2, :], ALU.mult, ALU.add)
                                own(last)
                        elif g == 2:
                            dve.wait_ge(o_read, 5 * l + i + 1)
                            nc.vector.tensor_tensor(heads_out[:, 2, :, :], heads_out[:, 2, :, :], gate_c,
                                                    ALU.mult).then_inc(group_ready, 1)
                    elif st == "subln":
                        a_heads = heads_out[:, 0, :, :].rearrange("p t (h d) -> p (t h) d", h=HEADS)
                        sq = pair[:, :, :, :].rearrange("p t s d -> p (t s) d")
                        own(nc.vector.tensor_tensor(sq, a_heads, a_heads, ALU.mult))
                        own(nc.vector.tensor_reduce(nrm[:, :], sq, AX.X, ALU.add))
                        own(nc.vector.tensor_scalar(nrm[:, :], nrm[:, :], 1.0 / HEAD, EPS, ALU.mult, ALU.add))
                        nc.vector.reciprocal(nrm[:, :], nrm[:, :]).then_inc(sub_ss, 1)
                    elif st == "subln_end":
                        dve.wait_ge(sub_root, l + 1)
                        a_heads = heads_out[:, 0, :, :].rearrange("p t (h d) -> p (t h) d", h=HEADS)
                        own(nc.vector.tensor_tensor(a_heads, a_heads, nrm[:, :].unsqueeze(2).to_broadcast(
                            [P, TT * HEADS, HEAD]), ALU.mult))
                        nc.vector.tensor_tensor(a_heads, a_heads, gain64[:, l, :].unsqueeze(1).to_broadcast(
                            [P, TT * HEADS, HEAD]), ALU.mult).then_inc(group_ready, 1)
                    elif st == "turn":
                        n = turn_no[("turn", i)]
                        dve.wait_ge(turn_hi, 4 * l + i + 1)
                        nc.vector.tensor_tensor(act_lo[:, 2 * i:2 * i + 2, :],
                                                bank[4 + n % 2][:, :].rearrange("p (w t) -> p w t", w=2),
                                                act_hi[:, 2 * i:2 * i + 2, :].bitcast(F32),
                                                ALU.subtract).then_inc(turn_lo, 1)
                    elif st == "resid":
                        if i == 0:
                            wait_mod(NA * (l + 1))
                            amplitudes(l, 1)
                        dve.wait_ge(unit_used, unit_no(l, NI + i) + 1)
                        residual(l, 2, i, unit_bank(NI + i))
                first = unit_no(l, NI + NO)
                inverse(2 * l + 1)
                modulated(2 * l + 1, l, 1)

                def taps(j, which):
                    dve.wait_ge(tap_ready, 4 * (STEPS * l + j) + 2 * which + 2)
                    for tap, lag in ((V_W1, 1), (V_W0, 2)):
                        for f in range(2):
                            ch = which * FT + 2 * j + f
                            dst = conv[:, which, f, lag:SEQ]
                            ins = nc.vector.scalar_tensor_tensor(
                                dst, bank[which][:, f * SEQ:(f + 1) * SEQ - lag], vec[:, l, tap + ch:tap + ch + 1], dst,
                                ALU.mult, ALU.add)
                            if lag == 1:
                                ins.then_inc(dve_own, 1)
                                count[0] += 1
                        if lag == 1:
                            dve.wait_ge(dve_own, count[0])
                    ins.then_inc(conv_read, 1)

                for j in range(STEPS):
                    if j < STEPS - 1:
                        split_lo(first + 3 * j + 2)
                    taps(j, 0)
                    if j < STEPS - 1:
                        split_lo(first + 3 * j + 3)
                    taps(j, 1)
                    dve.wait_ge(silu_ready, STEPS * l + j + 1)
                    dve.wait_ge(conv_read, 2 * (STEPS * l + j) + 2)
                    nc.vector.tensor_tensor(prod, silu, conv[:, 1, :, :], ALU.mult).then_inc(prod_done, 1)
                    split_lo(first + (3 * j + 4 if j < STEPS - 1 else 3 * STEPS - 1))
                    dve.wait_ge(mlp_hi_ready, STEPS * l + j + 1)
                    nc.vector.tensor_tensor(mlp_lo[:, :, :], prod, mlp_hi[:, :, :].bitcast(F32),
                                            ALU.subtract).then_inc(mlp_lo_ready, 1)
                    for e in mlp_ada(l, j - 1)[:1] if j else []:
                        take_columns(e[1], e[2], 2)
                if l + 1 < DEPTH:
                    split_lo(unit_no(l + 1, 0), unit_width(0))
                for p in range(KT // 2):
                    if p < 3:
                        dve.wait_ge(down_ready, 3 * l + p + 1)
                    else:
                        dve.wait_ge(unit_used, unit_no(l + 1, 0))
                    residual(l, 5, p, bank[3 + p])
                    if l + 1 == DEPTH:
                        dve.wait_ge(x_new, 4 * 2 * DEPTH + p + 1)
                        for k in (2 * p, 2 * p + 1):
                            nc.vector.tensor_scalar(final[:, k, :], xT[:, k, :], vec[:, 0, V_FIN + k:V_FIN + k + 1], None,
                                                    ALU.mult).then_inc(fin_ready, 1)
                if l + 1 < DEPTH:
                    split_lo(unit_no(l + 1, 1), unit_width(1))
            mean_plus(2 * DEPTH)
            dve.wait_ge(rooted, 2 * DEPTH + 1)
            for q in range(2):
                dve.wait_ge(finT_ready, 2 * q + 1)
                nc.vector.tensor_scalar(x_tok[:, 0, 512 * q:512 * q + 512], bank[2 * q][:, :], root[:, 0:1], None,
                                        ALU.mult).then_inc(out_part[0], 1)


def kernel(**inputs):
    import concourse.bacc as bacc
    from concourse.bass_utils import run_bass_kernel_spmd

    names = ["x", "c", "w_ada", "b_ada", "norm1_gain", "w_in", "f_bias", "diff_lambda", "diff_subln_gain",
             "w_dq_up", "w_didx_q", "w_dkv_up", "w_out", "t5_table", "norm2_gain", "w_ffn_up", "ffn_conv_w",
             "ffn_conv_b", "w_ffn_down", "final_gain"]
    nc = bacc.Bacc("TRN2", target_bir_lowering=False, num_devices=1)
    arrays = {f"in_{n}": np.ascontiguousarray(inputs[n]) for n in names}
    arrays["in_buckets"] = bucket_rows()
    args = [nc.dram_tensor(n, a.shape, mybir.dt.from_np(a.dtype), kind="ExternalInput").ap() for n, a in arrays.items()]
    args.append(nc.dram_tensor("out_0", (1, SEQ, D_MODEL), F32, kind="ExternalOutput").ap())
    trunk(nc, *args)
    r = run_bass_kernel_spmd(nc, [arrays], core_ids=[0])
    return r.results[0]["out_0"]
```
